# Optimizing a Trainium2 kernel written in Bass

```python
import jax, jax.numpy as jnp
from jax import lax
import numpy as np

D_MODEL = 2048
BATCH = 1
SEQ = 256
DEPTH = 2

EPS = 1e-6
NEG_INF = -1e30

HEAD_DIM_A = 64
N_Q_HEADS_A = (D_MODEL // 2) // HEAD_DIM_A
N_KV_HEADS_A = N_Q_HEADS_A // 8
Q_PER_KV_A = N_Q_HEADS_A // N_KV_HEADS_A
WIDTH_A = N_Q_HEADS_A * HEAD_DIM_A
KV_WIDTH_A = N_KV_HEADS_A * HEAD_DIM_A
WINDOW = 128

CHUNK_B = 128
WIDTH_B = D_MODEL // 2
N_GROUPS_B = 8
GROUP_B = WIDTH_B // N_GROUPS_B

HEAD_K_C = 128
HEAD_V_C = 128
WIDTH_C = D_MODEL // 2
N_HEADS_C = WIDTH_C // HEAD_V_C
KEY_WIDTH_C = N_HEADS_C * HEAD_K_C

WIDTH_D = D_MODEL // 2
N_HEADS_D = 4
KEY_WIDTH_D = WIDTH_D // 2
HEAD_K_D = KEY_WIDTH_D // N_HEADS_D
HEAD_V_D = WIDTH_D // N_HEADS_D
GATE_RANK_D = 16
GATE_LOGIT_NORM_D = 16.0

LA_CHUNK = 64
PLE_DIM = 256

N_EVEN = (DEPTH + 1) // 2
N_ODD = DEPTH // 2

EVEN_SPLITS = (WIDTH_A, KV_WIDTH_A, KV_WIDTH_A, WIDTH_A, WIDTH_B, WIDTH_B, WIDTH_B)
ODD_SPLITS = (KEY_WIDTH_C, KEY_WIDTH_C, WIDTH_C, WIDTH_C,
              KEY_WIDTH_D, KEY_WIDTH_D, WIDTH_D, GATE_RANK_D, WIDTH_D)
IN_EVEN = sum(EVEN_SPLITS)
IN_ODD = sum(ODD_SPLITS)
MIX_EVEN = WIDTH_A + WIDTH_B
MIX_ODD = WIDTH_C + WIDTH_D

kernel_name = 'hybrid_swa_gmlp_hgrn2_gla_block'

def rmsnorm(x, g):
    xf = x.astype(jnp.float32)
    y = xf * lax.rsqrt(jnp.mean(xf * xf, axis=-1, keepdims=True) + EPS)
    return (y * g.astype(jnp.float32)).astype(x.dtype)

def head_rmsnorm(o, g, n_heads):
    b, s, w = o.shape
    of = o.astype(jnp.float32).reshape(b, s, n_heads, w // n_heads)
    of = of * lax.rsqrt(jnp.mean(of * of, axis=-1, keepdims=True) + EPS)
    return (of.reshape(b, s, w) * g.astype(jnp.float32)).astype(o.dtype)

def split_cols(z, sizes):
    offs = []
    acc = 0
    for sz in sizes[:-1]:
        acc += sz
        offs.append(acc)
    return jnp.split(z, offs, axis=-1)

def sliding_window_sink_attention(q, k, v, sinks):
    b, s, _, _ = q.shape
    n = s // WINDOW
    qb = q.reshape(b, n, WINDOW, N_KV_HEADS_A, Q_PER_KV_A, HEAD_DIM_A)
    kb = k.reshape(b, n, WINDOW, N_KV_HEADS_A, HEAD_DIM_A)
    vb = v.reshape(b, n, WINDOW, N_KV_HEADS_A, HEAD_DIM_A)
    prev = lambda t: jnp.concatenate([jnp.zeros_like(t[:, :1]), t[:, :-1]], axis=1)
    kk = jnp.concatenate([prev(kb), kb], axis=2)
    vv = jnp.concatenate([prev(vb), vb], axis=2)
    scores = jnp.einsum('bnqhgd,bnkhd->bnhgqk', qb, kk).astype(jnp.float32) * (HEAD_DIM_A ** -0.5)
    qi = jnp.arange(WINDOW)[:, None]
    kj = jnp.arange(2 * WINDOW)[None, :]
    band = (kj > qi) & (kj <= qi + WINDOW)
    valid = (jnp.arange(n)[:, None, None] > 0) | (kj >= WINDOW)[None]
    mask = band[None] & valid
    scores = jnp.where(mask[None, :, None, None], scores, NEG_INF)
    sink = jnp.broadcast_to(
        sinks.astype(jnp.float32).reshape(1, 1, N_KV_HEADS_A, Q_PER_KV_A, 1, 1),
        scores.shape[:-1] + (1,))
    probs = jax.nn.softmax(jnp.concatenate([scores, sink], axis=-1), axis=-1)[..., :-1]
    out = jnp.einsum('bnhgqk,bnkhd->bnqhgd', probs.astype(v.dtype), vv)
    return out.reshape(b, s, WIDTH_A)

def chunked_spatial_gating(u, v, w_s, b_s):
    b, s, _ = u.shape
    n = s // CHUNK_B
    vb = v.reshape(b, n, CHUNK_B, N_GROUPS_B, GROUP_B)
    causal = jnp.tril(jnp.ones((CHUNK_B, CHUNK_B), dtype=bool))
    w = jnp.where(causal[None], w_s, jnp.zeros_like(w_s))
    mixed = jnp.einsum('gts,bnsgc->bntgc', w, vb) + b_s.T[None, None, :, :, None]
    return u * mixed.reshape(b, s, WIDTH_B)

def chunked_gated_linear_attention(q, k, v, log_g, scale):
    b, s, h, dk = q.shape
    dv = v.shape[-1]
    n = s // LA_CHUNK
    to_chunks = lambda t: jnp.moveaxis(t.reshape(b, n, LA_CHUNK, h, t.shape[-1]), 1, 0)
    qc, kc, vc, gc = to_chunks(q * scale), to_chunks(k), to_chunks(v), to_chunks(log_g)
    causal = jnp.tril(jnp.ones((LA_CHUNK, LA_CHUNK), dtype=bool))[None, :, :, None, None]

    def step(state, inp):
        qi, ki, vi, gi = inp
        qf, kf, vf = qi.astype(jnp.float32), ki.astype(jnp.float32), vi.astype(jnp.float32)
        gcum = jnp.cumsum(gi.astype(jnp.float32), axis=1)
        o_inter = jnp.einsum('bthk,bhkv->bthv', qf * jnp.exp(gcum), state)
        diff = gcum[:, :, None] - gcum[:, None, :]
        decay = jnp.where(causal, jnp.exp(jnp.where(causal, diff, 0.0)), 0.0)
        attn = jnp.einsum('bthk,btshk->bhts', qf, decay * kf[:, None])
        o_intra = jnp.einsum('bhts,bshv->bthv', attn, vf)
        g_last = gcum[:, -1]
        k_dec = kf * jnp.exp(g_last[:, None] - gcum)
        new_state = state * jnp.exp(g_last)[..., None] + jnp.einsum('bshk,bshv->bhkv', k_dec, vf)
        return new_state, (o_inter + o_intra).astype(v.dtype)

    state0 = jnp.zeros((b, h, dk, dv), jnp.float32)
    _, out = lax.scan(step, state0, (qc, kc, vc, gc))
    return jnp.moveaxis(out, 0, 1).reshape(b, s, h * dv)

def even_mixer(hn, w_in, sinks, vnorm, w_sp, b_sp, w_out):
    b, s, _ = hn.shape
    z = hn @ w_in
    q, k, v, gate_a, u_b, v_b, gate_b = split_cols(z, EVEN_SPLITS)
    attn = sliding_window_sink_attention(
        q.reshape(b, s, N_Q_HEADS_A, HEAD_DIM_A),
        k.reshape(b, s, N_KV_HEADS_A, HEAD_DIM_A),
        v.reshape(b, s, N_KV_HEADS_A, HEAD_DIM_A), sinks)
    u_b = jax.nn.gelu(u_b, approximate=False)
    v_b = rmsnorm(jax.nn.gelu(v_b, approximate=False), vnorm)
    sgu = chunked_spatial_gating(u_b, v_b, w_sp, b_sp)
    y = jnp.concatenate([attn * jax.nn.silu(gate_a), sgu * jax.nn.silu(gate_b)], axis=-1)
    return y @ w_out

def odd_mixer(hn, layer, w_in, lower_bounds, onorm_c, w_gate_up_d, b_gate_d, onorm_d, w_out):
    b, s, _ = hn.shape
    z = hn @ w_in
    q_c, f_c, i_c, gate_c, q_d, k_d, v_d, glr_d, gate_d = split_cols(z, ODD_SPLITS)
    sm = jax.nn.softmax(lower_bounds.astype(jnp.float32), axis=0)
    lb = (jnp.cumsum(sm, axis=0) - sm[0])[layer].reshape(N_HEADS_C, HEAD_K_C)
    f = lb + (1.0 - lb) * jax.nn.sigmoid(f_c.astype(jnp.float32).reshape(b, s, N_HEADS_C, HEAD_K_C))
    o_c = chunked_gated_linear_attention(
        q_c.reshape(b, s, N_HEADS_C, HEAD_K_C), (1.0 - f).astype(hn.dtype),
        i_c.reshape(b, s, N_HEADS_C, HEAD_V_C), jnp.log(f), HEAD_K_C ** -0.5)
    o_c = head_rmsnorm(o_c, onorm_c, N_HEADS_C) * jax.nn.silu(gate_c)
    log_alpha = jax.nn.log_sigmoid((glr_d @ w_gate_up_d + b_gate_d).astype(jnp.float32)) / GATE_LOGIT_NORM_D
    o_d = chunked_gated_linear_attention(
        q_d.reshape(b, s, N_HEADS_D, HEAD_K_D), k_d.reshape(b, s, N_HEADS_D, HEAD_K_D),
        v_d.reshape(b, s, N_HEADS_D, HEAD_V_D), log_alpha.reshape(b, s, N_HEADS_D, HEAD_K_D),
        HEAD_K_D ** -0.5)
    o_d = head_rmsnorm(o_d, onorm_d, N_HEADS_D) * jax.nn.silu(gate_d)
    return jnp.concatenate([o_c, o_d], axis=-1) @ w_out

def setup_inputs(seed: int = 0) -> dict:
    key = jax.random.key(seed)
    ks = jax.random.split(key, 24)
    f32 = jnp.float32
    nrm = lambda k, shape, scale: jax.random.normal(k, shape, f32) * scale
    gain = lambda k, shape: 1.0 + 0.02 * jax.random.normal(k, shape, f32)
    return {
        'x': nrm(ks[0], (BATCH, SEQ, D_MODEL), 1.0),
        'p': nrm(ks[1], (DEPTH, BATCH, SEQ, PLE_DIM), 1.0),
        'norm_mix': gain(ks[2], (DEPTH, D_MODEL)),
        'w_in_even': nrm(ks[3], (N_EVEN, D_MODEL, IN_EVEN), D_MODEL ** -0.5),
        'sinks_a': nrm(ks[4], (N_EVEN, N_Q_HEADS_A), 0.5),
        'vnorm_b': gain(ks[5], (N_EVEN, WIDTH_B)),
        'w_spatial_b': nrm(ks[6], (N_EVEN, N_GROUPS_B, CHUNK_B, CHUNK_B), CHUNK_B ** -0.5),
        'b_spatial_b': 1.0 + nrm(ks[7], (N_EVEN, N_GROUPS_B, CHUNK_B), 0.02),
        'w_out_even': nrm(ks[8], (N_EVEN, MIX_EVEN, D_MODEL), MIX_EVEN ** -0.5),
        'w_in_odd': nrm(ks[9], (N_ODD, D_MODEL, IN_ODD), D_MODEL ** -0.5),
        'lower_bounds_c': nrm(ks[10], (DEPTH, KEY_WIDTH_C), 0.5),
        'onorm_c': gain(ks[11], (N_ODD, WIDTH_C)),
        'w_gate_up_d': nrm(ks[12], (N_ODD, GATE_RANK_D, KEY_WIDTH_D), GATE_RANK_D ** -0.5),
        'b_gate_d': nrm(ks[13], (N_ODD, KEY_WIDTH_D), 0.1),
        'onorm_d': gain(ks[14], (N_ODD, WIDTH_D)),
        'w_out_odd': nrm(ks[15], (N_ODD, MIX_ODD, D_MODEL), MIX_ODD ** -0.5),
        'w_ple_proj': nrm(ks[16], (DEPTH, PLE_DIM, D_MODEL), PLE_DIM ** -0.5),
        'ple_norm': gain(ks[17], (DEPTH, D_MODEL)),
        'ple_gate_norm': gain(ks[18], (DEPTH, D_MODEL)),
        'w_ple_gate': nrm(ks[19], (DEPTH, D_MODEL, D_MODEL), D_MODEL ** -0.5),
        'final_norm': gain(ks[20], (D_MODEL,)),
    }

def reference(x, p, norm_mix, w_in_even, sinks_a, vnorm_b, w_spatial_b, b_spatial_b, w_out_even,
              w_in_odd, lower_bounds_c, onorm_c, w_gate_up_d, b_gate_d, onorm_d, w_out_odd,
              w_ple_proj, ple_norm, ple_gate_norm, w_ple_gate, final_norm):
    h = x
    for i in range(DEPTH):
        hn = rmsnorm(h, norm_mix[i])
        j = i // 2
        if i % 2 == 0:
            h = h + even_mixer(hn, w_in_even[j], sinks_a[j], vnorm_b[j], w_spatial_b[j],
                               b_spatial_b[j], w_out_even[j])
        else:
            h = h + odd_mixer(hn, i, w_in_odd[j], lower_bounds_c, onorm_c[j], w_gate_up_d[j],
                              b_gate_d[j], onorm_d[j], w_out_odd[j])
        e = rmsnorm(p[i] @ w_ple_proj[i], ple_norm[i])
        gate = jax.nn.sigmoid(rmsnorm(h, ple_gate_norm[i]) @ w_ple_gate[i])
        h = h + e * gate
    return rmsnorm(h, final_norm)


_drawn_inputs = setup_inputs


def setup_inputs(seed=0):
    import zlib

    import numpy as np

    out = dict(_drawn_inputs(seed))
    spreads = {}
    factors = {'norm_mix': 2.688,
     'sinks_a': 35.23,
     'vnorm_b': 28.745,
     'b_spatial_b': 8.0,
     'onorm_c': 200.0,
     'b_gate_d': 4.55,
     'onorm_d': 200.0,
     'ple_norm': 93.127,
     'ple_gate_norm': 64.0,
     'final_norm': 23.783}
    for name, (base, spread) in spreads.items():
        noise = np.random.default_rng([zlib.crc32(name.encode()), seed]).standard_normal(out[name].shape)
        drawn = base * np.exp(spread * noise) if base else spread * noise
        out[name] = __import__('jax').numpy.asarray(drawn.astype(out[name].dtype))
    for name, factor in factors.items():
        out[name] = (out[name] * factor).astype(out[name].dtype)
    return out
```

```python
from contextlib import ExitStack

import concourse.bass as bass
from concourse import mybir

P = 128
F32 = mybir.dt.float32
F32R = mybir.dt.float32r
I32 = mybir.dt.int32
ALU = mybir.AluOpType
ACT = mybir.ActivationFunctionType
AX = mybir.AxisListType
EPS = 1e-6
NEG_INF = -1e30

D_MODEL = 2048
SEQ = 256
TILES = SEQ // P
KT = D_MODEL // P
COLS = 512
K_PER_SLOT = 2
SLOTS = KT // K_PER_SLOT
RING = 4
CHUNKS = D_MODEL // COLS
PLE = 256
HEADS_A, KV_A, HD_A = 16, 2, 64
GROUPS_B = 8
WIDTH_B = D_MODEL // 2
LEVELS = (128, 64, 32, 16, 8, 4, 2, 1)
SCALE_LA = float(P) ** -0.5
LN_LEAST = 2.0 ** -63

EVEN_IN = [(1024, 256), (0, 512), (512, 512)] + [(1280 + 512 * i, 512) for i in range(8)]
E_KV, E_Q, E_GA, E_U, E_VB, E_GB = 0, 1, 3, 5, 7, 9
ODD_IN = [(c, 512) for c in (0, 1024, 512, 1536, 4096, 4608, 2048, 2560, 5120, 5632, 3072, 3584, 6160, 6672)]
GLR_COL, GLR = 6144, 16
O_V, O_GATE = 6, 10
GROUPS_LA = 3

C_MIX, C_GATE, C_ONORM = 0, 2 * KT, 4 * KT
C_BSP = C_ONORM + KT
C_LB = C_BSP + GROUPS_B
C_BG = C_LB + 16
N_ROWS = C_BG + 4

PLAN = ([("in0", i) for i in range(len(EVEN_IN))] + [("e0", i) for i in range(CHUNKS)]
        + [("out0", i) for i in range(CHUNKS)] + [("gate0", i) for i in range(CHUNKS)]
        + [("in1", 0), ("in1", 1), ("glr", 0)] + [("in1", i) for i in range(2, len(ODD_IN))]
        + [("e1", i) for i in range(CHUNKS)] + [("out1", i) for i in range(CHUNKS)]
        + [("gate1", i) for i in range(CHUNKS)])
NUMBER = {c: n for n, c in enumerate(PLAN)}


def slots_of(c):
    return 1 if c[0] in ("e0", "e1", "glr") else SLOTS


FIRST_SLOT = {c: sum(slots_of(d) for d in PLAN[:n]) for n, c in enumerate(PLAN)}

UNITS = ([(0, list(range(4 * u, 4 * u + 4))) for u in range(HEADS_A // 4)]
         + [(1, list(range(2 * u, 2 * u + 2))) for u in range(HEADS_A // 2)])

T_USES = (["cols", "wsp"] + [f"x{c}" for c in range(CHUNKS)] + ["p0", "k", "q0", "q1"]
          + [f"P{u}" for u in range(len(UNITS))] + ["ya0", "ya1", "yb0", "yb1"]
          + [f"out0{c}" for c in range(CHUNKS)] + [f"gate0{c}" for c in range(CHUNKS)]
          + ["p1", "f0", "glr", "g0", "f1", "g1", "f2", "g2"] + [f"yo{c}" for c in range(CHUNKS)]
          + [f"out1{c}" for c in range(CHUNKS)])
M0_USES = ([f"S{u}" for u in range(len(UNITS))]
           + [f"A{n}{a}" for n in range(GROUPS_LA) for a in [*range(len(LEVELS)), "d0", "d1"]])
M1_USES = ([f"O{u}" for u in range(len(UNITS))] + [f"mix{i}" for i in range(4)]
           + ["up0", "up1"] + [f"AV{i}" for i in range(8)])
T_NO, M0_NO, M1_NO = ({u: i for i, u in enumerate(x)} for x in (T_USES, M0_USES, M1_USES))

SPLITS = {**{f"x{c}": (0, 4 * c, C_MIX + 4 * c) for c in range(CHUNKS)}, "p0": ("p", 0, None),
          "ya0": (1, 0, None), "ya1": (1, 4, None), "yb0": (1, 8, None), "yb1": (1, 12, None),
          **{f"out0{c}": (0, 4 * c, C_GATE + 4 * c) for c in range(CHUNKS)},
          **{f"gate0{c}": (1, 4 * c, C_MIX + KT + 4 * c) for c in range(CHUNKS)},
          "p1": ("p", 0, None), **{f"yo{c}": (0, 4 * c, C_ONORM + 4 * c) for c in range(CHUNKS)},
          **{f"out1{c}": (1, 4 * c, C_GATE + KT + 4 * c) for c in range(CHUNKS)}}
SPLIT_NO = {u: i for i, u in enumerate(u for u in T_USES if u in SPLITS)}

STATS = [("X", 2, D_MODEL), ("V", 2, WIDTH_B), ("E0", 8, D_MODEL), ("H0", 8, D_MODEL), ("H1", 8, D_MODEL),
         ("E1", 8, D_MODEL), ("H2", 8, D_MODEL), ("H3", 8, D_MODEL)]
STAT_NO = {s[0]: i for i, s in enumerate(STATS)}

AT_K, AT_Q, AT_SCORES, AT_TURN, AT_VALUES = 10, 18, 30, 33, 35
AT_YA, AT_MIX, AT_YB = 62, 78, 85
AT_GLR, AT_P1 = 19, 5
G_F, G_Q, G_LEVEL, G_DIAG = 1, 4, 8, 16
AT_AV, AT_YO = 59, 91


def group_start(n):
    return SLOTS * (2 * n + 2) + 1


def av_place(i):
    return AT_AV + SLOTS * (i // 2) + 2 * (i % 2)


def trunk(nc, x, p, norm_mix, w_in_even, sinks_a, vnorm_b, w_spatial_b, b_spatial_b, w_out_even,
          w_in_odd, lower_bounds_c, onorm_c, w_gate_up_d, b_gate_d, onorm_d, w_out_odd,
          w_ple_proj, ple_norm, ple_gate_norm, w_ple_gate, final_norm, out):
    with ExitStack() as ctx:
        def sb(name, shape, dt=F32):
            return ctx.enter_context(nc.sbuf_tensor(name, shape, dt))

        def sem(name):
            return ctx.enter_context(nc.semaphore(name))

        raw = sb("raw", [P, RING, K_PER_SLOT * COLS])
        whi = sb("whi", [P, RING, K_PER_SLOT * COLS], F32R)
        wlo = sb("wlo", [P, RING, K_PER_SLOT * COLS], F32R)
        h = sb("h", [P, TILES, D_MODEL])
        bhi = [sb(f"bhi{i}", [P, KT, SEQ], F32R) for i in range(2)]
        blo = [sb(f"blo{i}", [P, KT, SEQ], F32R) for i in range(2)]
        phi = sb("phi", [P, PLE // P, SEQ], F32R)
        plo = sb("plo", [P, PLE // P, SEQ], F32R)
        e = sb("e", [P, TILES, D_MODEL])
        ident = sb("ident", [P, P])
        ones = sb("ones", [P, P])
        cols = sb("cols", [P, N_ROWS])
        band = sb("band", [P, 2, P])
        lmask = sb("lmask", [P, len(LEVELS) - 1, P // 2])
        nsink = sb("nsink", [P, HEADS_A])
        small = sb("small", [P, 512])
        glrT = sb("glrT", [GLR, SEQ])
        glr = sb("glr_z", [P, TILES, GLR])
        junk = sb("junk", [P, 1024])
        WORK = 15872
        work = sb("work", [P, WORK])

        def flat(a):
            return a.rearrange("p a b -> p (a b)")

        def part(first, a, b):
            return work[:, first:first + a * b].rearrange("p (a b) -> p a b", b=b)

        qo = part(0, TILES, 1024)
        qT = part(2048, 8, SEQ)
        kv = part(4096, TILES, 256)
        kT = work[:, 4608:5632].rearrange("p (g z n) -> p g z n", g=KV_A, z=2)
        Pm = part(5632, 2, COLS)
        PT = part(6656, 2, COLS)
        ga = part(7680, TILES, 1024)
        u_b = part(9728, TILES, 1024)
        v_b = part(11776, TILES, 1024)
        vgain = work[:, 13824:14848]
        wT = part(14848, GROUPS_B, P)
        kpad = work[:, 6656:7680].rearrange("p (t g z d) -> p t g z d", t=TILES, g=KV_A, z=2)
        rows = work[0:N_ROWS, 7680:7680 + P]
        wsp = part(11776, GROUPS_B, P)
        pin0 = part(5632, TILES, PLE)
        sg0 = part(2048, TILES, COLS)
        zq = part(0, TILES, COLS)
        zf = part(1024, TILES, COLS)
        gq = part(2048, 4, SEQ)
        gk = part(3072, 4, SEQ)
        gg = part(4096, 4, SEQ)
        lv = part(5120, 2, 1024)
        ATd = part(7168, 24, P)
        ATx = part(10240, 12, P)
        O = part(11776, TILES, D_MODEL)
        pin1 = part(0, TILES, PLE)
        upw = work[0:GLR, 11776:11776 + 512]
        sgate = [part(5120 + 1024 * i, TILES, COLS) for i in range(2)]
        gbc = work[:, 13824:15872]

        ms = small[:, 0:64].rearrange("p (r t c) -> p r t c", r=8, t=2)
        mean = small[:, 64:80].rearrange("p (r t) -> p r t", r=8)
        var = small[:, 80:96].rearrange("p (r t) -> p r t", r=8)
        rstd = small[:, 96:112].rearrange("p (r t) -> p r t", r=8)

        def heads_of(first, n):
            return small[:, first:first + 2 * n].rearrange("p (t h) -> p t h", t=2)

        mhalf = small[:, 112:136]
        nmax, dsink, esink, psumr, rinv = (heads_of(136 + 32 * i, HEADS_A) for i in range(5))
        oms, ovar, orstd = (heads_of(296 + 24 * i, 12) for i in range(3))
        lb_max, lb_a, lb_b, lb_sum, lb, omlb = (small[:, 368 + 8 * i:376 + 8 * i] for i in range(6))

        acc = [[ctx.enter_context(nc.psum_tensor(f"acc{a}{t}", [P, COLS], F32)) for t in range(2)] for a in range(2)]
        T = [ctx.enter_context(nc.psum_tensor(f"T{i}", [P, COLS], F32)) for i in range(2)]
        M0 = ctx.enter_context(nc.psum_tensor("M0", [P, COLS], F32))
        M1 = ctx.enter_context(nc.psum_tensor("M1", [P, COLS], F32))

        landed = [sem(f"landed{i}") for i in range(RING)]
        hi_made, lo_made, slot_used = sem("hi_made"), sem("lo_made"), sem("slot_used")
        acc_read = [sem("acc_read0"), sem("acc_read1")]
        t_full, t_read, t_hi = sem("t_full"), sem("t_read"), sem("t_hi")
        m0_full, m0_read, m1_full, m1_read = sem("m0_full"), sem("m0_read"), sem("m1_full"), sem("m1_read")
        x_in, rows_in, wsp_in, p_in, sink_in, vgain_in, up_in, gain_in, stored = (
            sem(n) for n in ("x_in", "rows_in", "wsp_in", "p_in", "sink_in", "vgain_in", "up_in", "gain_in", "stored"))
        small_zero, ident_made, masks_made, kpad_zero, scores_zero = (
            sem(n) for n in ("small_zero", "ident_made", "masks_made", "kpad_zero", "scores_zero"))
        cols_made, spatial_turned, spatial_masked, lb_shifted, lb_exps = (
            sem(n) for n in ("cols_made", "spatial_turned", "spatial_masked", "lb_shifted", "lb_exps"))
        squares, mean_made, rstd_made = sem("squares"), sem("mean_made"), sem("rstd_made")
        kpad_made, scores_shifted, probs_made, ga_made, y_gated, v_normed = (
            sem(n) for n in ("kpad_made", "scores_shifted", "probs_made", "ga_made", "y_gated", "v_normed"))
        sig_made, f_made, ln_made, abs_made, lv_sub, lv_exp, lv_mul, o_squares, o_rstd = (
            sem(n) for n in ("sig_made", "f_made", "ln_made", "abs_made", "lv_sub", "lv_exp", "lv_mul",
                             "o_squares", "o_rstd"))
        e_scaled, h_gated, normed = sem("e_scaled"), sem("h_gated"), sem("normed")
        dve_step, act_step, pool_step = sem("dve_step"), sem("act_step"), sem("pool_step")

        def source(c, s):
            phase, i = c
            if phase == "glr":
                return w_in_odd[0, :, GLR_COL:GLR_COL + GLR].rearrange("(k p) n -> p k n", p=P)
            layer = int(phase[-1])
            if phase[:-1] == "in":
                w = (w_in_even, w_in_odd)[layer][0]
                c0, n = (EVEN_IN, ODD_IN)[layer][i]
            else:
                w = {"e0": w_ple_proj[0], "e1": w_ple_proj[1], "out0": w_out_even[0], "out1": w_out_odd[0],
                     "gate0": w_ple_gate[0], "gate1": w_ple_gate[1]}[phase]
                c0, n = i * COLS, COLS
            r0 = s * K_PER_SLOT * P
            return w[r0:r0 + K_PER_SLOT * P, c0:c0 + n].rearrange("(k p) n -> p k n", p=P)

        def slot_view(ring, c, s):
            k, n = (KT, GLR) if c[0] == "glr" else (K_PER_SLOT, EVEN_IN[c[1]][1] if c[0] == "in0" else COLS)
            r = (FIRST_SLOT[c] + s) % RING
            return ring[:, r, 0:k * n].rearrange("p (k n) -> p k n", n=n)

        def wait_chunk(eng, c):
            eng.wait_ge(slot_used, FIRST_SLOT[c] + slots_of(c))

        def wait_read(eng, c):
            eng.wait_ge(acc_read[NUMBER[c] % 2], NUMBER[c] // 2 + 1)

        def wait_use(eng, s, table, name):
            eng.wait_ge(s, table[name] + 1)

        def wait_rstd(eng, name):
            eng.wait_ge(rstd_made, STAT_NO[name] + 1)

        def level_views(a, m):
            return a.rearrange("p (b z m) -> p b z m", z=2, m=m)

        block = ctx.enter_context(nc.Block())

        @block.sync
        def _(sp):
            for t in range(TILES):
                sp.dma_start(h[:, t, :], x[0, t * P:(t + 1) * P, :]).then_inc(x_in, 16)
            row = 0
            for v in (norm_mix.rearrange("a b -> (a b)"), ple_gate_norm.rearrange("a b -> (a b)"), onorm_c[0], onorm_d[0],
                      b_spatial_b[0].rearrange("a b -> (a b)"), lower_bounds_c.rearrange("a b -> (a b)"), b_gate_d[0]):
                n = v.shape[0] // P
                sp.dma_start(rows[row:row + n, :], v.rearrange("(r c) -> r c", c=P)).then_inc(rows_in, 16)
                row += n

            def weights(c):
                for s in range(slots_of(c)):
                    n = FIRST_SLOT[c] + s
                    if n >= RING:
                        sp.wait_ge(lo_made, n - RING + 1)
                    sp.dma_start(slot_view(raw, c, s), source(c, s)).then_inc(landed[n % RING], 16)

            weights(PLAN[0])
            sp.dma_start(wsp, w_spatial_b[0].rearrange("g t s -> t g s")).then_inc(wsp_in, 16)
            sp.dma_start(pin0, p[0, 0].rearrange("(t p) d -> p t d", p=P)).then_inc(p_in, 16)
            sp.dma_start(nsink[:], sinks_a[0].partition_broadcast(P)).then_inc(sink_in, 16)
            sp.dma_start(vgain, vnorm_b[0].partition_broadcast(P)).then_inc(vgain_in, 16)
            for c in PLAN[1:]:
                weights(c)
                if c == ("out0", 0):
                    wait_use(sp, m1_read, M1_NO, "mix3")
                    sp.dma_start(gbc, ple_norm[0].partition_broadcast(P)).then_inc(gain_in, 16)
                    sp.dma_start(upw, w_gate_up_d[0]).then_inc(up_in, 16)
                    wait_use(sp, t_full, T_NO, "ya1")
                    sp.dma_start(pin1, p[1, 0].rearrange("(t p) d -> p t d", p=P)).then_inc(p_in, 16)
                if c == ("out1", 0):
                    wait_use(sp, t_full, T_NO, "yo3")
                    sp.dma_start(gbc, ple_norm[1].partition_broadcast(P)).then_inc(gain_in, 16)
                if c == ("gate1", 0):
                    sp.wait_ge(e_scaled, 2 * CHUNKS)
                    sp.dma_start(gbc, final_norm.partition_broadcast(P)).then_inc(gain_in, 16)
            for t in range(TILES):
                sp.wait_ge(normed, t + 1)
                sp.dma_start(out[0, t * P:(t + 1) * P, :], e[:, t, :]).then_inc(stored, 16)
            sp.wait_ge(stored, 16 * TILES)

        @block.tensor
        def _(pe):
            def take_T(name):
                if T_NO[name]:
                    pe.wait_ge(t_read, T_NO[name])

            def turn(name, src):
                take_T(name)
                for k in range(4):
                    for t in range(TILES):
                        last = nc.tensor.transpose(T[k // 2][:, (k % 2) * SEQ + t * P:(k % 2) * SEQ + (t + 1) * P],
                                                   src[:, t, k * P:(k + 1) * P], ident[:])
                last.then_inc(t_full, 1)

            def turn_p(name, src, loads):
                pe.wait_ge(p_in, 16 * loads)
                take_T(name)
                for k in range(PLE // P):
                    for t in range(TILES):
                        last = nc.tensor.transpose(T[0][:, k * SEQ + t * P:k * SEQ + (t + 1) * P],
                                                   src[:, t, k * P:(k + 1) * P], ident[:])
                last.then_inc(t_full, 1)

            def slot(c, s, hi, lo):
                n = FIRST_SLOT[c] + s
                wh, wl = slot_view(whi, c, s), slot_view(wlo, c, s)
                k_n, w = wh.shape[1:]
                pe.wait_ge(lo_made, n + 1)
                for k in range(k_n):
                    first, final = s == 0 and k == 0, s == slots_of(c) - 1 and k == k_n - 1
                    for t in range(TILES):
                        o = acc[NUMBER[c] % 2][t][:, 0:w]
                        xh, xl = (b[:, K_PER_SLOT * s + k, t * P:(t + 1) * P] for b in (hi, lo))
                        nc.tensor.matmul(o, xh, wl[:, k, :], start=first, stop=False)
                        nc.tensor.matmul(o, xl, wh[:, k, :], start=False, stop=False)
                        last = nc.tensor.matmul(o, xh, wh[:, k, :], start=False, stop=final)
                last.then_inc(slot_used, 1)

            def chunk(c, buf, late=None, between=lambda s: None):
                if NUMBER[c] >= 2:
                    wait_read(pe, PLAN[NUMBER[c] - 2])
                for s in range(SLOTS):
                    if s == SLOTS - 2 and late:
                        wait_use(pe, t_read, T_NO, late)
                    slot(c, s, bhi[buf], blo[buf])
                    between(s)

            def embed(layer):
                wait_use(pe, t_read, T_NO, f"p{layer}")
                for i in range(CHUNKS):
                    wait_read(pe, PLAN[NUMBER[(f"e{layer}", i)] - 2])
                    slot((f"e{layer}", i), 0, phi, plo)

            def scores(u):
                b, heads = UNITS[u]
                if u == 0:
                    wait_use(pe, t_read, T_NO, "q1")
                else:
                    wait_use(pe, m0_read, M0_NO, f"S{u - 1}")
                nk = P * (b + 1)
                for i, hd in enumerate(heads):
                    last = nc.tensor.matmul(M0[:, i * nk:(i + 1) * nk], qT[:, hd // 2, b * P:(b + 1) * P],
                                            kT[:, hd // 8, hd % 2, 0:nk], start=True, stop=True)
                last.then_inc(m0_full, 1)

            def turn_probs(u):
                pe.wait_ge(probs_made, u + 1)
                take_T(f"P{u}")
                for i in range(4):
                    last = nc.tensor.transpose(T[0][:, i * P:(i + 1) * P], Pm[:, u % 2, i * P:(i + 1) * P], ident[:])
                last.then_inc(t_full, 1)

            def values(u):
                b, heads = UNITS[u]
                wait_use(pe, t_read, T_NO, f"P{u}")
                if u:
                    wait_use(pe, m1_read, M1_NO, f"O{u - 1}")
                for i, hd in enumerate(heads):
                    v0 = P + (hd // 8) * HD_A
                    for j in range(b + 1):
                        q = (i * (b + 1) + j) * P
                        last = nc.tensor.matmul(M1[:, i * HD_A:(i + 1) * HD_A], PT[:, u % 2, q:q + P],
                                                kv[:, j, v0:v0 + HD_A], start=(j == 0), stop=(j == b))
                last.then_inc(m1_full, 1)

            def mix(i):
                t, half = i // 2, i % 2
                pe.wait_ge(m1_read, M1_NO[f"mix{i}"])
                for g in range(4 * half, 4 * half + 4):
                    last = nc.tensor.matmul(M1[:, (g % 4) * P:(g % 4 + 1) * P], wT[:, g, :],
                                            v_b[:, t, g * P:(g + 1) * P], start=True, stop=True)
                last.then_inc(m1_full, 1)

            def even(i, s):
                at = SLOTS * i + s
                if at == AT_K:
                    pe.wait_ge(kpad_made, 1)
                    take_T("k")
                    for g in range(KV_A):
                        for z in range(2):
                            for t in range(TILES):
                                last = nc.tensor.transpose(T[g][:, z * SEQ + t * P:z * SEQ + (t + 1) * P],
                                                           kpad[:, t, g, z, :], ident[:])
                    last.then_inc(t_full, 1)
                for c in range(2):
                    if at == AT_Q + SLOTS * c:
                        wait_read(pe, ("in0", E_Q + c))
                        turn(f"q{c}", qo[:, :, c * COLS:(c + 1) * COLS])
                for u in range(len(UNITS)):
                    if at == AT_SCORES + 2 * u:
                        scores(u)
                    if at == AT_TURN + 2 * u:
                        turn_probs(u)
                    if at == AT_VALUES + 2 * u:
                        values(u)
                for c in range(2):
                    if at == AT_YA + 3 * c:
                        pe.wait_ge(y_gated, c + 1)
                        turn(f"ya{c}", qo[:, :, c * COLS:(c + 1) * COLS])
                for m in range(4):
                    if at == AT_MIX + m:
                        if m == 0:
                            pe.wait_ge(v_normed, TILES)
                            pe.wait_ge(spatial_masked, 1)
                        mix(m)
                if at == AT_YB:
                    pe.wait_ge(y_gated, 3)
                    turn("yb0", u_b[:, :, 0:COLS])

            def level(n, i):
                m, X = LEVELS[i], lv[:, i % 2, :]
                pe.wait_ge(lv_mul, n * len(LEVELS) + i + 1)
                pe.wait_ge(m0_read, M0_NO[f"A{n}{i}"])
                if m == P:
                    for hd in range(4):
                        last = nc.tensor.matmul(M0[:, hd * P:(hd + 1) * P], X[:, hd * SEQ:hd * SEQ + P],
                                                X[:, hd * SEQ + P:(hd + 1) * SEQ], start=True, stop=True)
                else:
                    for j in range(8):
                        Xj = X[:, j * P:(j + 1) * P]
                        last = nc.tensor.matmul(M0[:, j * 64:(j + 1) * 64].rearrange("p (b m) -> p b m", m=m), Xj,
                                                level_views(Xj, m)[:, :, 1, :], start=True, stop=True)
                last.then_inc(m0_full, 1)

            def diagonal(n, half):
                pe.wait_ge(m0_read, M0_NO[f"A{n}d{half}"])
                for j in range(4):
                    o = (4 * half + j) * P
                    last = nc.tensor.matmul(M0[:, j * P:(j + 1) * P], flat(gk)[:, o:o + P], flat(gq)[:, o:o + P],
                                            start=True, stop=True)
                last.then_inc(m0_full, 1)

            def apply_scores(i):
                c, t = i // 2, i % 2
                wait_read(pe, ("in1", O_V + c))
                pe.wait_ge(m1_read, M1_NO[f"AV{i}"])
                n_heads, dv = (4, P) if c < 2 else (2, 2 * P)
                first = 4 * c if c < 2 else 8 + 2 * (c - 2)
                wait_use(pe, m0_read, M0_NO, f"A{first // 4}d1")
                v = (zq, zf)[c % 2]
                for j in range(n_heads):
                    o = M1[:, j * dv:(j + 1) * dv]
                    if t:
                        nc.tensor.matmul(o, ATx[:, first + j, :], v[:, 0, j * dv:(j + 1) * dv], start=True, stop=False)
                    last = nc.tensor.matmul(o, ATd[:, 2 * (first + j) + t, :], v[:, t, j * dv:(j + 1) * dv],
                                            start=(t == 0), stop=True)
                last.then_inc(m1_full, 1)

            def odd(i, s):
                at = SLOTS * i + s
                if at == 2:
                    pe.wait_ge(h_gated, CHUNKS)
                    turn("gate03", h[:, :, 3 * COLS:4 * COLS])
                if at == AT_P1:
                    turn_p("p1", pin1, 2)
                for n in range(GROUPS_LA):
                    b = group_start(n)
                    if at == b + G_F:
                        wait_read(pe, ("in1", 2 * n + 1))
                        turn(f"f{n}", zf)
                        if n == 2:
                            pe.wait_ge(up_in, 16)
                            for half in range(2):
                                pe.wait_ge(m1_read, M1_NO[f"up{half}"])
                                for j in range(2):
                                    hd = 2 * half + j
                                    last = nc.tensor.matmul(M1[:, j * SEQ:(j + 1) * SEQ], upw[:, hd * P:(hd + 1) * P],
                                                            glrT[:], start=True, stop=True)
                                last.then_inc(m1_full, 1)
                    if at == b + G_Q:
                        turn(f"g{n}", zq)
                    for j in range(len(LEVELS)):
                        if at == b + G_LEVEL + j:
                            level(n, j)
                    for half in range(2):
                        if at == b + G_DIAG + half:
                            diagonal(n, half)
                if at == AT_GLR:
                    wait_read(pe, ("glr", 0))
                    take_T("glr")
                    for t in range(TILES):
                        last = nc.tensor.transpose(T[0][0:GLR, t * P:(t + 1) * P], glr[:, t, :], ident[:])
                    last.then_inc(t_full, 1)
                for j in range(8):
                    if at == av_place(j):
                        apply_scores(j)
                for c in range(3):
                    if at == AT_YO + SLOTS * c:
                        pe.wait_ge(y_gated, 5 + c)
                        turn(f"yo{c}", O[:, :, c * COLS:(c + 1) * COLS])

            def turn_out(layer, c):
                wait_read(pe, (f"out{layer}", c))
                turn(f"out{layer}{c}", h[:, :, c * COLS:(c + 1) * COLS])

            def turn_gate(c):
                pe.wait_ge(h_gated, c + 1)
                turn(f"gate0{c}", h[:, :, c * COLS:(c + 1) * COLS])

            pe.wait_ge(ident_made, 1)
            pe.wait_ge(rows_in, 16 * 7)
            nc.tensor.transpose(T[0][:, 0:N_ROWS], rows, ident[0:N_ROWS, 0:N_ROWS]).then_inc(t_full, 1)
            pe.wait_ge(wsp_in, 16)
            take_T("wsp")
            for g in range(GROUPS_B):
                last = nc.tensor.transpose(T[g // 4][:, (g % 4) * P:(g % 4 + 1) * P], wsp[:, g, :], ident[:])
            last.then_inc(t_full, 1)
            pe.wait_ge(x_in, 16 * TILES)
            for c in range(CHUNKS):
                turn(f"x{c}", h[:, :, c * COLS:(c + 1) * COLS])
            turn_p("p0", pin0, 1)
            wait_use(pe, t_read, T_NO, "x3")
            for i in range(len(EVEN_IN)):
                chunk(("in0", i), 0, between=lambda s: even(i, s))
            embed(0)
            pe.wait_ge(y_gated, 4)
            turn("yb1", u_b[:, :, COLS:2 * COLS])
            for c in range(CHUNKS):
                chunk(("out0", c), 1, late=None if c else "yb1",
                      between=lambda s: turn_out(0, c - 1) if c and s == 2 else None)
            for c in range(CHUNKS):
                chunk(("gate0", c), 0, late=None if c else "out03",
                      between=lambda s: None if s != 2 else turn_gate(c - 1) if c else turn_out(0, 3))
            for i in range(len(ODD_IN)):
                chunk(("in1", i), 1, late=None if i else "gate03", between=lambda s: odd(i, s))
                if i == 1:
                    wait_read(pe, PLAN[NUMBER[("glr", 0)] - 2])
                    slot(("glr", 0), 0, bhi[1], blo[1])
            embed(1)
            pe.wait_ge(y_gated, 8)
            turn("yo3", O[:, :, 3 * COLS:4 * COLS])
            for c in range(CHUNKS):
                chunk(("out1", c), 0, late=None if c else "yo3",
                      between=lambda s: turn_out(1, c - 1) if c and s == 2 else None)
            for c in range(CHUNKS):
                chunk(("gate1", c), 1, late=None if c else "out13",
                      between=lambda s: turn_out(1, 3) if c == 0 and s == 2 else None)

        @block.scalar
        def _(act):
            steps = [0]
            sq_n, o_sq_n = [0], [0]

            def link(ins):
                steps[0] += 1
                ins.then_inc(act_step, 1)
                act.wait_ge(act_step, steps[0])

            def split_w(c, s):
                n = FIRST_SLOT[c] + s
                act.wait_ge(landed[n % RING], 16 * (n // RING + 1))
                if n >= RING:
                    act.wait_ge(slot_used, n - RING + 1)
                nc.scalar.activation(slot_view(whi, c, s), slot_view(raw, c, s), ACT.Copy).then_inc(hi_made, 1)

            def split_T(name):
                buf, k0, gain = SPLITS[name]
                wait_use(act, t_full, T_NO, name)
                if gain is None:
                    hi = phi if buf == "p" else bhi[buf]
                    for i in range(1 if buf == "p" else 2):
                        last = nc.scalar.activation(hi[:, k0 + 2 * i:k0 + 2 * i + 2, :].rearrange("p a b -> p (a b)"),
                                                    T[i][:], ACT.Copy)
                else:
                    if gain == C_MIX:
                        act.wait_ge(cols_made, 1)
                    for k in range(4):
                        last = nc.scalar.activation(bhi[buf][:, k0 + k, :], T[k // 2][:, (k % 2) * SEQ:(k % 2 + 1) * SEQ],
                                                    ACT.Copy, scale=cols[:, gain + k:gain + k + 1])
                last.then_inc(t_hi, 1)

            def square(src, dst):
                if sq_n[0]:
                    act.wait_ge(squares, sq_n[0])
                sq_n[0] += 1
                nc.scalar.activation(junk[:, 0:src.shape[-1]], src, ACT.Square, accum_out=dst).then_inc(squares, 1)

            def square_chunk(src, stat, c):
                for t in range(TILES):
                    square(src[:, t, c * COLS:(c + 1) * COLS], ms[:, STAT_NO[stat], t, c:c + 1])

            def read_out(c, dst, func, stat):
                wait_chunk(act, c)
                wait_rstd(act, stat)
                for t in range(TILES):
                    last = nc.scalar.activation(dst(t), acc[NUMBER[c] % 2][t][:, 0:dst(t).shape[-1]], func,
                                                scale=rstd[:, STAT_NO[stat], t:t + 1])
                last.then_inc(acc_read[NUMBER[c] % 2], 1)

            def softmax(u):
                b, heads = UNITS[u]
                act.wait_ge(scores_shifted, u + 1)
                nk = P * (b + 1)
                for i, hd in enumerate(heads):
                    s = Pm[:, u % 2, i * nk:(i + 1) * nk]
                    nc.scalar.activation(s, s, ACT.Exp, bias=nmax[:, b, hd:hd + 1], accum_out=psumr[:, b, hd:hd + 1])
                hs = slice(heads[0], heads[-1] + 1)
                nc.scalar.activation(esink[:, b, hs], dsink[:, b, hs], ACT.Exp).then_inc(probs_made, 1)

            def even(i, s):
                at = SLOTS * i + s
                if s == 1 and i:
                    c = i - 1
                    if c == E_KV:
                        read_out(("in0", c), lambda t: kv[:, t, :], ACT.Copy, "X")
                    for first, dst, func in ((E_Q, qo, ACT.Copy), (E_GA, ga, ACT.Copy), (E_U, u_b, ACT.Gelu),
                                             (E_VB, v_b, ACT.Gelu)):
                        if first <= c < first + 2:
                            o = (c - first) * COLS
                            read_out(("in0", c), lambda t: dst[:, t, o:o + COLS], func, "X")
                    if c == E_GB:
                        read_out(("in0", c), lambda t: sg0[:, t, :], ACT.Silu, "X")
                if at == AT_K + 2:
                    wait_use(act, t_full, T_NO, "k")
                    for g in range(KV_A):
                        last = nc.scalar.activation(kT[:, g].rearrange("p z n -> p (z n)"), T[g][:], ACT.Copy)
                    last.then_inc(t_read, 1)
                for c in range(2):
                    if at == AT_Q + SLOTS * c + 2:
                        wait_use(act, t_full, T_NO, f"q{c}")
                        for j in range(2):
                            last = nc.scalar.activation(flat(qT[:, 4 * c + 2 * j:4 * c + 2 * j + 2, :]), T[j][:], ACT.Copy,
                                                        scale=HD_A ** -0.5)
                        last.then_inc(t_read, 1)
                for u in range(len(UNITS)):
                    if at == AT_SCORES + 2 * u + 2:
                        softmax(u)
                    if at == AT_TURN + 2 * u + 2:
                        wait_use(act, t_full, T_NO, f"P{u}")
                        if u >= 2:
                            wait_use(act, m1_full, M1_NO, f"O{u - 2}")
                        nc.scalar.activation(PT[:, u % 2, :], T[0][:], ACT.Copy).then_inc(t_read, 1)
                for c in range(2):
                    if at == AT_YA - 2 + c:
                        g = ga[:, :, c * COLS:(c + 1) * COLS]
                        wait_read(act, ("in0", E_GA + c))
                        nc.scalar.activation(g, g, ACT.Silu).then_inc(ga_made, 1)
                    if at == AT_YA + 3 * c + 2:
                        split_T(f"ya{c}")
                if at == SLOTS * (E_VB + 2) + 2:
                    wait_read(act, ("in0", E_VB + 1))
                    for t in range(TILES):
                        square(v_b[:, t, :], ms[:, STAT_NO["V"], t, 0:1])
                if at == AT_YB + 2:
                    split_T("yb0")

            def read_embed(layer, i):
                wait_read(act, (f"e{layer}", i))
                square_chunk(e, f"E{layer}", i)

            def read_outproj(layer, c):
                wait_read(act, (f"out{layer}", c))
                square_chunk(h, f"H{2 * layer}", c)

            def read_gate(layer, c):
                n = CHUNKS * layer + c
                if n >= 2:
                    act.wait_ge(h_gated, n - 1)
                read_out((f"gate{layer}", c), lambda t: sgate[n % 2][:, t, :], ACT.Sigmoid, f"H{2 * layer}")

            def square_gate(layer, c):
                act.wait_ge(h_gated, CHUNKS * layer + c + 1)
                square_chunk(h, f"H{2 * layer + 1}", c)

            def odd(i, s):
                at = SLOTS * i + s
                if at == 1:
                    read_gate(0, 3)
                if at == 3:
                    square_gate(0, 3)
                if at == 4:
                    split_T("gate03")
                if at == AT_P1 + 2:
                    split_T("p1")
                if s == 1 and i:
                    c = i - 1
                    if c < O_GATE:
                        dst = (zq, zf)[c % 2]
                        if c in (0, 1):
                            wait_use(act, t_full, T_NO, "p1")
                        elif c < O_V + 2:
                            wait_use(act, t_full, T_NO, f"{'gf'[c % 2]}{(c - 2) // 2}")
                        else:
                            wait_use(act, m1_full, M1_NO, f"AV{2 * (c - O_V - 2) + 1}")
                        read_out(("in1", c), lambda t: dst[:, t, :], ACT.Copy, "H1")
                    else:
                        gates(c - O_GATE)
                    if c == 1:
                        read_out(("glr", 0), lambda t: glr[:, t, :], ACT.Copy, "H1")
                if at == AT_GLR + 2:
                    wait_use(act, t_full, T_NO, "glr")
                    nc.scalar.activation(glrT[:], T[0][0:GLR, 0:SEQ], ACT.Copy).then_inc(t_read, 1)
                for n in range(GROUPS_LA):
                    b = group_start(n)
                    if at == b + G_F + 2 and n < 2:
                        wait_use(act, t_full, T_NO, f"f{n}")
                        if n:
                            wait_use(act, m0_full, M0_NO, f"A{n - 1}6")
                        for j in range(2):
                            last = nc.scalar.activation(lv[:, 0, j * COLS:(j + 1) * COLS], T[j][:], ACT.Sigmoid)
                        last.then_inc(t_read, 1)
                    if at == b + G_F + 3 and n < 2:
                        act.wait_ge(f_made, n + 1)
                        nc.scalar.activation(lv[:, 0, :], lv[:, 1, :], ACT.Ln).then_inc(ln_made, 1)
                    if at == b + G_F + 2 and n == 2:
                        wait_use(act, t_full, T_NO, "f2")
                        wait_use(act, m0_full, M0_NO, "A1d1")
                        for j in range(2):
                            last = nc.scalar.activation(flat(gk)[:, j * COLS:(j + 1) * COLS], T[j][:], ACT.Copy)
                        last.then_inc(t_read, 1)
                        for half in range(2):
                            wait_use(act, m1_full, M1_NO, f"up{half}")
                            for j in range(2):
                                hd = 2 * half + j
                                last = nc.scalar.activation(lv[:, 0, hd * SEQ:(hd + 1) * SEQ], M1[:, j * SEQ:(j + 1) * SEQ],
                                                            ACT.Abs, bias=cols[:, C_BG + hd:C_BG + hd + 1])
                            last.then_inc(abs_made, 1)
                        act.wait_ge(abs_made, 2)
                        link(nc.scalar.activation(lv[:, 0, :], lv[:, 0, :], ACT.Exp, scale=-1.0))
                        nc.scalar.activation(lv[:, 0, :], lv[:, 0, :], ACT.Ln, bias=1.0).then_inc(ln_made, 1)
                    if at == b + G_Q + 2:
                        wait_use(act, t_full, T_NO, f"g{n}")
                        if n:
                            wait_use(act, m0_full, M0_NO, f"A{n - 1}d1")
                        for j in range(2):
                            last = nc.scalar.activation(flat(gq)[:, j * COLS:(j + 1) * COLS], T[j][:], ACT.Copy,
                                                        scale=SCALE_LA)
                        last.then_inc(t_read, 1)
                    for j in range(len(LEVELS)):
                        if at == b + G_LEVEL + j - 1:
                            act.wait_ge(lv_sub, n * len(LEVELS) + j + 1)
                            nc.scalar.activation(lv[:, j % 2, :], lv[:, j % 2, :], ACT.Exp).then_inc(lv_exp, 1)
                for j in range(8):
                    if at == av_place(j) + 3:
                        c, t = j // 2, j % 2
                        wait_use(act, m1_read, M1_NO, f"AV{j}")
                        n_heads, dv = (4, P) if c < 2 else (2, 2 * P)
                        first = 4 * c if c < 2 else 8 + 2 * (c - 2)
                        for k in range(n_heads):
                            if o_sq_n[0]:
                                act.wait_ge(o_squares, o_sq_n[0])
                            o_sq_n[0] += 1
                            nc.scalar.activation(junk[:, 0:dv], O[:, t, c * COLS + k * dv:c * COLS + (k + 1) * dv],
                                                 ACT.Square, accum_out=oms[:, t, first + k:first + k + 1]).then_inc(o_squares, 1)
                for c in range(3):
                    if at == AT_YO + SLOTS * c + 2:
                        split_T(f"yo{c}")

            def gates(c):
                if c >= 2:
                    act.wait_ge(y_gated, 4 + c - 1)
                read_out(("in1", O_GATE + c), lambda t: lv[:, c % 2, t * COLS:(t + 1) * COLS], ACT.Silu, "H1")

            def embed_and_out(layer, last_of_in, turned):
                for i in range(CHUNKS):
                    split_w((f"e{layer}", i), 0)
                    if i == 1:
                        last_of_in()
                read_embed(layer, 0)
                read_embed(layer, 1)
                for c in range(CHUNKS):
                    for s in range(SLOTS):
                        split_w((f"out{layer}", c), s)
                        if c == 0:
                            if s == 1:
                                read_embed(layer, 2)
                                read_embed(layer, 3)
                            if s == 2:
                                split_T(turned)
                        else:
                            if s == 1:
                                read_outproj(layer, c - 1)
                            if s == 4:
                                split_T(f"out{layer}{c - 1}")

            def gate_phase(layer):
                for c in range(CHUNKS):
                    for s in range(SLOTS):
                        split_w((f"gate{layer}", c), s)
                        if s == 1 and c == 0:
                            read_outproj(layer, 3)
                        if s == 4 and c == 0:
                            split_T(f"out{layer}3")
                        if s == 1 and c:
                            read_gate(layer, c - 1)
                        if s == 3 and c:
                            square_gate(layer, c - 1)
                        if s == 4 and c and layer == 0:
                            split_T(f"gate0{c - 1}")

            act.wait_ge(x_in, 16 * TILES)
            act.wait_ge(small_zero, 1)
            for t in range(TILES):
                nc.scalar.activation(e[:, t, :], h[:, t, :], ACT.Square,
                                     accum_out=ms[:, STAT_NO["X"], t, 0:1]).then_inc(squares, 1)
                sq_n[0] += 1
            for s in range(RING):
                split_w(PLAN[0], s)
            for c in range(CHUNKS):
                split_T(f"x{c}")
            split_T("p0")
            act.wait_ge(lb_shifted, 1)
            nc.scalar.activation(small[:, 376:392], small[:, 376:392], ACT.Exp).then_inc(lb_exps, 1)
            for i in range(len(EVEN_IN)):
                for s in range(SLOTS):
                    if i or s >= RING:
                        split_w(("in0", i), s)
                    even(i, s)

            def last_gate_b():
                act.wait_ge(y_gated, 3)
                read_out(("in0", E_GB + 1), lambda t: sg0[:, t, :], ACT.Silu, "X")

            embed_and_out(0, last_gate_b, "yb1")
            gate_phase(0)
            for i in range(len(ODD_IN)):
                for s in range(SLOTS):
                    split_w(("in1", i), s)
                    odd(i, s)
                if i == 1:
                    split_w(("glr", 0), 0)
            embed_and_out(1, lambda: gates(3), "yo3")
            gate_phase(1)
            read_gate(1, 3)
            square_gate(1, 3)

        @block.vector
        def _(dve):
            steps = [0]

            def link(ins):
                steps[0] += 1
                ins.then_inc(dve_step, 1)
                dve.wait_ge(dve_step, steps[0])

            def split_w(c, s):
                n = FIRST_SLOT[c] + s
                dve.wait_ge(hi_made, n + 1)
                if n >= RING:
                    dve.wait_ge(slot_used, n - RING + 1)
                nc.vector.tensor_tensor(slot_view(wlo, c, s), slot_view(raw, c, s), slot_view(whi, c, s).bitcast(F32),
                                        ALU.subtract).then_inc(lo_made, 1)

            def split_T(name):
                buf, k0, gain = SPLITS[name]
                dve.wait_ge(t_hi, SPLIT_NO[name] + 1)
                hi, lo = (phi, plo) if buf == "p" else (bhi[buf], blo[buf])
                if gain is None:
                    for i in range(1 if buf == "p" else 2):
                        ks = slice(k0 + 2 * i, k0 + 2 * i + 2)
                        last = nc.vector.tensor_tensor(flat(lo[:, ks, :]), T[i][:], flat(hi[:, ks, :]).bitcast(F32),
                                                       ALU.subtract)
                else:
                    for k in range(4):
                        last = nc.vector.scalar_tensor_tensor(
                            out=lo[:, k0 + k, :], in0=T[k // 2][:, (k % 2) * SEQ:(k % 2 + 1) * SEQ],
                            scalar=cols[:, gain + k:gain + k + 1], in1=hi[:, k0 + k, :].bitcast(F32),
                            op0=ALU.mult, op1=ALU.subtract)
                last.then_inc(t_read, 1)

            def row_mean(name):
                i = STAT_NO[name]
                dve.wait_ge(squares, sum(n for _, n, _ in STATS[:i + 1]))
                nc.vector.tensor_reduce(mean[:, i, :], ms[:, i], AX.X, ALU.add).then_inc(mean_made, 1)

            def shift_scores(u):
                b, heads = UNITS[u]
                n, nk = len(heads), P * (b + 1)
                hs = slice(heads[0], heads[-1] + 1)
                wait_use(dve, m0_full, M0_NO, f"S{u}")
                if u >= 2:
                    wait_use(dve, t_full, T_NO, f"P{u - 2}")
                mask = band[:] if b else band[:, 1:2, :]
                mask = flat(mask).unsqueeze(1).to_broadcast([P, n, nk])
                S = Pm[:, u % 2, :].rearrange("p (n k) -> p n k", k=nk)
                nc.vector.tensor_tensor(S, M0[:].rearrange("p (n k) -> p n k", k=nk), mask, ALU.add).then_inc(m0_read, 1)
                wait_use(dve, m0_read, M0_NO, f"S{u}")
                link(nc.vector.tensor_reduce(nmax[:, b, hs], S, AX.X, ALU.max, negate=True))
                link(nc.vector.tensor_tensor(nmax[:, b, hs], nmax[:, b, hs], nsink[:, hs], ALU.min))
                nc.vector.tensor_tensor(dsink[:, b, hs], nmax[:, b, hs], nsink[:, hs], ALU.subtract).then_inc(scores_shifted, 1)

            def attention_out(u):
                b, heads = UNITS[u]
                n = len(heads)
                hs = slice(heads[0], heads[-1] + 1)
                dve.wait_ge(probs_made, u + 1)
                link(nc.vector.tensor_tensor(rinv[:, b, hs], psumr[:, b, hs], esink[:, b, hs], ALU.add))
                link(nc.vector.reciprocal(rinv[:, b, hs], rinv[:, b, hs]))
                wait_use(dve, m1_full, M1_NO, f"O{u}")
                o = qo[:, b, heads[0] * HD_A:(heads[-1] + 1) * HD_A].rearrange("p (n d) -> p n d", d=HD_A)
                nc.vector.tensor_tensor(o, M1[:, 0:n * HD_A].rearrange("p (n d) -> p n d", d=HD_A),
                                        rinv[:, b, hs].unsqueeze(2).to_broadcast([P, n, HD_A]), ALU.mult).then_inc(m1_read, 1)

            def gate_b(c):
                wait_read(dve, ("in0", E_GB + c))
                wait_use(dve, m1_read, M1_NO, "mix3")
                ub = u_b[:, :, c * COLS:(c + 1) * COLS]
                nc.vector.tensor_tensor(ub, ub, sg0, ALU.mult).then_inc(y_gated, 1)

            def even(i, s):
                at = SLOTS * i + s
                if at == AT_K - 1:
                    wait_read(dve, ("in0", E_KV))
                    dve.wait_ge(kpad_zero, 1)
                    for g in range(KV_A):
                        for z in range(2):
                            last = nc.vector.tensor_copy(kpad[:, :, g, z, z * HD_A:(z + 1) * HD_A],
                                                         kv[:, :, g * HD_A:(g + 1) * HD_A])
                    last.then_inc(kpad_made, 1)
                for u in range(len(UNITS)):
                    if at == AT_SCORES + 2 * u + 2:
                        shift_scores(u)
                    if at == AT_VALUES + 2 * u + 2:
                        attention_out(u)
                for c in range(2):
                    if at == AT_YA - 1 + c:
                        dve.wait_ge(ga_made, c + 1)
                        wait_use(dve, m1_read, M1_NO, f"O{len(UNITS) - 1}")
                        q = qo[:, :, c * COLS:(c + 1) * COLS]
                        nc.vector.tensor_tensor(q, q, ga[:, :, c * COLS:(c + 1) * COLS], ALU.mult).then_inc(y_gated, 1)
                    if at == AT_YA + 3 * c + 2:
                        split_T(f"ya{c}")
                if at == AT_MIX - 3:
                    row_mean("V")
                if at == AT_MIX - 1:
                    wait_rstd(dve, "V")
                    dve.wait_ge(vgain_in, 16)
                    for t in range(TILES):
                        nc.vector.scalar_tensor_tensor(out=v_b[:, t, :], in0=v_b[:, t, :], scalar=rstd[:, STAT_NO["V"], t:t + 1],
                                                       in1=vgain, op0=ALU.mult, op1=ALU.mult).then_inc(v_normed, 1)
                for m in range(4):
                    if at == AT_MIX + m + 2:
                        wait_use(dve, m1_full, M1_NO, f"mix{m}")
                        t, half = m // 2, m % 2
                        for g in range(4 * half, 4 * half + 4):
                            ub = u_b[:, t, g * P:(g + 1) * P]
                            last = nc.vector.scalar_tensor_tensor(
                                out=ub, in0=M1[:, (g % 4) * P:(g % 4 + 1) * P], scalar=cols[:, C_BSP + g:C_BSP + g + 1],
                                in1=ub, op0=ALU.add, op1=ALU.mult)
                        last.then_inc(m1_read, 1)
                if at == AT_YB - 1:
                    gate_b(0)
                if at == AT_YB + 2:
                    split_T("yb0")

            def read_embed(layer, i):
                c = (f"e{layer}", i)
                wait_chunk(dve, c)
                for t in range(TILES):
                    last = nc.vector.tensor_copy(e[:, t, i * COLS:(i + 1) * COLS], acc[NUMBER[c] % 2][t][:])
                last.then_inc(acc_read[NUMBER[c] % 2], 1)

            def read_outproj(layer, i):
                c = (f"out{layer}", i)
                wait_chunk(dve, c)
                for t in range(TILES):
                    ht = h[:, t, i * COLS:(i + 1) * COLS]
                    last = nc.vector.tensor_tensor(ht, acc[NUMBER[c] % 2][t][:], ht, ALU.add)
                last.then_inc(acc_read[NUMBER[c] % 2], 1)

            def scale_embed(layer, i):
                if i == 0:
                    row_mean(f"E{layer}")
                    wait_rstd(dve, f"E{layer}")
                    dve.wait_ge(gain_in, 16 * (layer + 1))
                for t in range(TILES):
                    et = e[:, t, i * COLS:(i + 1) * COLS]
                    last = nc.vector.scalar_tensor_tensor(out=et, in0=et, scalar=rstd[:, STAT_NO[f"E{layer}"], t:t + 1],
                                                          in1=gbc[:, i * COLS:(i + 1) * COLS], op0=ALU.mult, op1=ALU.mult)
                last.then_inc(e_scaled, 1)

            def apply_gate(layer, i):
                c = (f"gate{layer}", i)
                n = CHUNKS * layer + i
                wait_read(dve, c)
                dve.wait_ge(e_scaled, n + 1)
                g, cs = sgate[n % 2], slice(i * COLS, (i + 1) * COLS)
                link(nc.vector.tensor_tensor(g, g, e[:, :, cs], ALU.mult))
                nc.vector.tensor_tensor(h[:, :, cs], h[:, :, cs], g, ALU.add).then_inc(h_gated, 1)

            def select(n, i):
                m = LEVELS[i]
                wait_use(dve, m0_full, M0_NO, f"A{n}{i}")
                if m == P:
                    nc.vector.tensor_copy(flat(ATx[:, 4 * n:4 * n + 4, :]), M0[:]).then_inc(m0_read, 1)
                    return
                if n == 0:
                    dve.wait_ge(scores_zero, 1)
                    dve.wait_ge(masks_made, 1)
                nb = P // (2 * m)
                dst = ATd[:, 8 * n:8 * n + 8, :].rearrange("p j (b z m) -> p j b z m", z=2, m=m)[:, :, :, 1, :]
                mask = lmask[:, i - 1, :].bitcast(I32).rearrange("p (b m) -> p b m", m=m).unsqueeze(1).to_broadcast([P, 8, nb, m])
                nc.vector.copy_predicated(dst, mask, M0[:].rearrange("p (j b m) -> p j b m", j=8, m=m)).then_inc(m0_read, 1)

            def select_diagonal(n, half):
                wait_use(dve, m0_full, M0_NO, f"A{n}d{half}")
                mask = ident[:].bitcast(I32).unsqueeze(1).to_broadcast([P, 4, P])
                nc.vector.copy_predicated(ATd[:, 8 * n + 4 * half:8 * n + 4 * half + 4, :], mask,
                                          M0[:].rearrange("p (j b) -> p j b", j=4)).then_inc(m0_read, 1)

            def sum_decays():
                for j in range(8):
                    last = nc.vector.tensor_tensor_scan(flat(gg)[:, j * P:(j + 1) * P], ones[:], lv[:, 0, j * P:(j + 1) * P],
                                                        0.0, ALU.mult, ALU.add)
                link(last)

            def exponents(n, i):
                m = LEVELS[i]
                if i >= 2:
                    wait_use(dve, m0_full, M0_NO, f"A{n}{i - 2}")
                g, X = level_views(flat(gg), m), level_views(lv[:, i % 2, :], m)
                nb = g.shape[1]
                ref = g[:, :, 0, m - 1:m].to_broadcast([P, nb, m])
                nc.vector.tensor_tensor(X[:, :, 0, :], ref, g[:, :, 0, :], ALU.subtract)
                if m == P:
                    last = nc.vector.tensor_copy(X[:, :, 1, :], g[:, :, 1, :])
                else:
                    last = nc.vector.tensor_tensor(X[:, :, 1, :], g[:, :, 1, :], ref, ALU.subtract)
                last.then_inc(lv_sub, 1)

            def gate_o(c):
                wait_read(dve, ("in1", O_GATE + c))
                dve.wait_ge(o_rstd, 1)
                n_heads, dv = (4, P) if c < 2 else (2, 2 * P)
                first = 4 * c if c < 2 else 8 + 2 * (c - 2)
                for t in range(TILES):
                    for j in range(n_heads):
                        o = O[:, t, c * COLS + j * dv:c * COLS + (j + 1) * dv]
                        last = nc.vector.scalar_tensor_tensor(
                            out=o, in0=o, scalar=orstd[:, t, first + j:first + j + 1],
                            in1=lv[:, c % 2, t * COLS + j * dv:t * COLS + (j + 1) * dv], op0=ALU.mult, op1=ALU.mult)
                last.then_inc(y_gated, 1)

            def odd(i, s):
                at = SLOTS * i + s
                if at == 2:
                    apply_gate(0, 3)
                if at == 4:
                    split_T("gate03")
                    row_mean("H1")
                if at == AT_P1 + 2:
                    split_T("p1")
                for n in range(GROUPS_LA):
                    b = group_start(n)
                    if at == b + G_F + 2 and n < 2:
                        wait_use(dve, t_read, T_NO, f"f{n}")
                        if n:
                            wait_use(dve, m0_full, M0_NO, f"A{n - 1}d1")
                        f = lv[:, 1, :]
                        for hd in range(4):
                            hc = 4 * n + hd
                            last = nc.vector.tensor_scalar(f[:, hd * SEQ:(hd + 1) * SEQ], lv[:, 0, hd * SEQ:(hd + 1) * SEQ],
                                                           omlb[:, hc:hc + 1], lb[:, hc:hc + 1], ALU.mult, ALU.add)
                        link(last)
                        link(nc.vector.tensor_scalar(flat(gk), f, -1.0, 1.0, ALU.mult, ALU.add))
                        nc.vector.tensor_scalar(f, f, LN_LEAST, None, ALU.max).then_inc(f_made, 1)
                    if at == b + G_F + 2 and n == 2:
                        f = lv[:, 1, :]
                        wait_use(dve, m0_full, M0_NO, "A1d1")
                        for half in range(2):
                            dve.wait_ge(abs_made, half + 1)
                            for j in range(2):
                                hd = 2 * half + j
                                last = nc.vector.tensor_scalar(f[:, hd * SEQ:(hd + 1) * SEQ], M1[:, j * SEQ:(j + 1) * SEQ],
                                                               cols[:, C_BG + hd:C_BG + hd + 1], 0.0, ALU.add, ALU.min)
                            last.then_inc(m1_read, 1)
                    if at == b + G_F + 4:
                        if n == 2:
                            f = lv[:, 1, :]
                            wait_use(dve, m1_read, M1_NO, "up1")
                            dve.wait_ge(ln_made, 3)
                            link(nc.vector.tensor_tensor(lv[:, 0, :], f, lv[:, 0, :], ALU.subtract))
                            link(nc.vector.tensor_scalar(lv[:, 0, :], lv[:, 0, :], 1.0 / 16.0, None, ALU.mult))
                        else:
                            dve.wait_ge(ln_made, n + 1)
                        sum_decays()
                    for j in range(len(LEVELS)):
                        if at == b + G_LEVEL + j - 1:
                            exponents(n, j)
                        if at == b + G_LEVEL + j + 2:
                            select(n, j)
                    for half in range(2):
                        if at == b + G_DIAG + half + 2:
                            select_diagonal(n, half)
                for j in range(8):
                    if at == av_place(j) + 2:
                        c, t = j // 2, j % 2
                        wait_use(dve, m1_full, M1_NO, f"AV{j}")
                        nc.vector.tensor_copy(O[:, t, c * COLS:(c + 1) * COLS], M1[:]).then_inc(m1_read, 1)
                for c in range(3):
                    if at == AT_YO + SLOTS * c - 1:
                        gate_o(c)
                    if at == AT_YO + SLOTS * c + 2:
                        split_T(f"yo{c}")

            def embed_and_out(layer, last_of_in, turned):
                for i in range(CHUNKS):
                    split_w((f"e{layer}", i), 0)
                    if i == 1:
                        last_of_in()
                read_embed(layer, 0)
                read_embed(layer, 1)
                for c in range(CHUNKS):
                    for s in range(SLOTS):
                        split_w((f"out{layer}", c), s)
                        if c == 0:
                            if s == 1:
                                read_embed(layer, 2)
                                read_embed(layer, 3)
                            if s == 2:
                                split_T(turned)
                        else:
                            if s == 1:
                                read_outproj(layer, c - 1)
                            if s == 4:
                                split_T(f"out{layer}{c - 1}")
                        if s == 6:
                            scale_embed(layer, c)

            def gate_phase(layer):
                for c in range(CHUNKS):
                    for s in range(SLOTS):
                        split_w((f"gate{layer}", c), s)
                        if s == 1 and c == 0:
                            read_outproj(layer, 3)
                        if s == 4 and c == 0:
                            split_T(f"out{layer}3")
                            row_mean(f"H{2 * layer}")
                        if s == 2 and c:
                            apply_gate(layer, c - 1)
                        if s == 4 and c and layer == 0:
                            split_T(f"gate0{c - 1}")

            nc.vector.memset(small[:], 0.0).then_inc(small_zero, 1)
            dve.wait_ge(small_zero, 1)
            link(nc.vector.memset(mhalf, -0.5))
            wait_use(dve, t_full, T_NO, "cols")
            nc.vector.tensor_copy(cols[:], T[0][:, 0:N_ROWS]).then_inc(t_read, 1)
            wait_use(dve, t_read, T_NO, "cols")
            row_mean("X")
            dve.wait_ge(dve_step, steps[0])
            link(nc.vector.tensor_tensor(lb_max, cols[:, C_LB:C_LB + 8], cols[:, C_LB + 8:C_LB + 16], ALU.max))
            nc.vector.tensor_tensor(lb_a, cols[:, C_LB:C_LB + 8], lb_max, ALU.subtract).then_inc(cols_made, 1)
            nc.vector.tensor_tensor(lb_b, cols[:, C_LB + 8:C_LB + 16], lb_max, ALU.subtract).then_inc(lb_shifted, 1)
            for s in range(RING):
                split_w(PLAN[0], s)
            wait_use(dve, t_full, T_NO, "wsp")
            for i in range(2):
                last = nc.vector.tensor_copy(flat(wT[:, 4 * i:4 * i + 4, :]), T[i][:])
            last.then_inc(t_read, 1)
            for c in range(CHUNKS):
                split_T(f"x{c}")
            split_T("p0")
            dve.wait_ge(lb_exps, 1)
            link(nc.vector.tensor_tensor(lb_sum, lb_a, lb_b, ALU.add))
            link(nc.vector.reciprocal(lb_sum, lb_sum))
            link(nc.vector.tensor_tensor(lb, lb_b, lb_sum, ALU.mult))
            link(nc.vector.tensor_scalar(omlb, lb, -1.0, 1.0, ALU.mult, ALU.add))
            dve.wait_ge(sink_in, 16)
            link(nc.vector.tensor_scalar(nsink[:], nsink[:], -1.0, None, ALU.mult))
            dve.wait_ge(masks_made, 1)
            for i in range(len(EVEN_IN)):
                for s in range(SLOTS):
                    if i or s >= RING:
                        split_w(("in0", i), s)
                    even(i, s)
            embed_and_out(0, lambda: gate_b(1), "yb1")
            gate_phase(0)
            for i in range(len(ODD_IN)):
                for s in range(SLOTS):
                    split_w(("in1", i), s)
                    odd(i, s)
                if i == 1:
                    split_w(("glr", 0), 0)
            embed_and_out(1, lambda: gate_o(3), "yo3")
            gate_phase(1)
            apply_gate(1, 3)
            row_mean("H3")
            wait_rstd(dve, "H3")
            dve.wait_ge(gain_in, 48)
            dve.wait_ge(h_gated, 2 * CHUNKS)
            for t in range(TILES):
                nc.vector.scalar_tensor_tensor(out=e[:, t, :], in0=h[:, t, :], scalar=rstd[:, STAT_NO["H3"], t:t + 1],
                                               in1=gbc, op0=ALU.mult, op1=ALU.mult).then_inc(normed, 1)

        @block.gpsimd
        def _(pool):
            steps = [0]

            def link(ins):
                steps[0] += 1
                ins.then_inc(pool_step, 1)
                pool.wait_ge(pool_step, steps[0])

            def keep(a, pattern, base, per_partition, fill, op=ALU.is_ge):
                return nc.gpsimd.affine_select(out=a, in_=a, pattern=pattern, compare_op=op, fill=fill, base=base,
                                               channel_multiplier=per_partition)

            def root(name):
                i = STAT_NO[name]
                pool.wait_ge(mean_made, i + 1)
                link(nc.gpsimd.tensor_scalar(var[:, i, :], mean[:, i, :], 1.0 / STATS[i][2], EPS, ALU.mult, ALU.add))
                nc.gpsimd.tensor_tensor(rstd[:, i, :], var[:, i, :], mhalf[:, 0:TILES], ALU.pow).then_inc(rstd_made, 1)

            link(nc.gpsimd.memset(ident[:], 0.0))
            keep(ident[:], [[-1, P]], 0, 1, 1.0, ALU.not_equal).then_inc(ident_made, 1)
            nc.gpsimd.memset(kpad, 0.0).then_inc(kpad_zero, 1)
            link(nc.gpsimd.memset(band[:], 0.0))
            link(keep(band[:, 0, :], [[1, P]], -1, -1, NEG_INF))
            link(keep(band[:, 1, :], [[-1, P]], 0, 1, NEG_INF))
            link(nc.gpsimd.memset(lmask[:], 1.0))
            for i, m in enumerate(LEVELS[1:]):
                v, nb = lmask[:, i, :], P // (2 * m)
                link(keep(v, [[-2 * m, nb], [0, m]], 0, 1, 0.0))
                link(keep(v, [[2 * m, nb], [0, m]], m - 1, -1, 0.0))
            nc.gpsimd.memset(ones[:], 1.0).then_inc(masks_made, 1)
            root("X")
            wait_use(pool, t_read, T_NO, "wsp")
            nc.gpsimd.affine_select(out=wT, in_=wT, pattern=[[0, GROUPS_B], [1, P]], compare_op=ALU.is_ge, fill=0.0, base=0,
                                    channel_multiplier=-1).then_inc(spatial_masked, 1)
            for name in ("V", "E0", "H0"):
                root(name)
            wait_use(pool, t_full, T_NO, "yb1")
            nc.gpsimd.memset(ATd, 0.0).then_inc(scores_zero, 1)
            root("H1")
            for n in range(GROUPS_LA):
                for i, m in enumerate(LEVELS):
                    pool.wait_ge(lv_exp, n * len(LEVELS) + i + 1)
                    X, k, q = (level_views(a, m) for a in (lv[:, i % 2, :], flat(gk), flat(gq)))
                    nc.gpsimd.tensor_tensor(X[:, :, 0, :], X[:, :, 0, :], k[:, :, 0, :], ALU.mult)
                    nc.gpsimd.tensor_tensor(X[:, :, 1, :], X[:, :, 1, :], q[:, :, 1, :], ALU.mult).then_inc(lv_mul, 1)
            pool.wait_ge(o_squares, 2 * (8 + 4))
            link(nc.gpsimd.tensor_scalar(ovar[:, :, 0:8], oms[:, :, 0:8], 1.0 / P, EPS, ALU.mult, ALU.add))
            link(nc.gpsimd.tensor_scalar(ovar[:, :, 8:12], oms[:, :, 8:12], 1.0 / (2 * P), EPS, ALU.mult, ALU.add))
            nc.gpsimd.tensor_tensor(orstd, ovar, mhalf.rearrange("p (t h) -> p t h", t=2), ALU.pow).then_inc(o_rstd, 1)
            for name in ("E1", "H2", "H3"):
                root(name)


_INS = ["x", "p", "norm_mix", "w_in_even", "sinks_a", "vnorm_b", "w_spatial_b", "b_spatial_b", "w_out_even",
        "w_in_odd", "lower_bounds_c", "onorm_c", "w_gate_up_d", "b_gate_d", "onorm_d", "w_out_odd",
        "w_ple_proj", "ple_norm", "ple_gate_norm", "w_ple_gate", "final_norm"]


def kernel(**inputs):
    import numpy as np
    import concourse.bacc as bacc
    from concourse.bass_utils import run_bass_kernel_spmd

    nc = bacc.Bacc("TRN2", target_bir_lowering=False, num_devices=1, dynamic_dma_scratch_size=1024)
    arrays, args = {}, []
    for name in _INS:
        a = np.ascontiguousarray(inputs[name])
        arrays[f"in_{name}"] = a
        args.append(nc.dram_tensor(f"in_{name}", a.shape, mybir.dt.from_np(a.dtype), kind="ExternalInput").ap())
    out = nc.dram_tensor("out", (1, SEQ, D_MODEL), F32, kind="ExternalOutput").ap()
    trunk(nc, *args, out)
    return run_bass_kernel_spmd(nc, [arrays], core_ids=[0]).results[0]["out"]
```

```python
from contextlib import ExitStack

import concourse.bass as bass
from concourse import mybir

P = 128
F32 = mybir.dt.float32
F32R = mybir.dt.float32r
I32 = mybir.dt.int32
ALU = mybir.AluOpType
ACT = mybir.ActivationFunctionType
AX = mybir.AxisListType
EPS = 1e-6
NEG_INF = -1e30

D_MODEL = 2048
SEQ = 256
TILES = SEQ // P
KT = D_MODEL // P
COLS = 512
K_PER_SLOT = 2
SLOTS = KT // K_PER_SLOT
RING = 4
CHUNKS = D_MODEL // COLS
PLE = 256
HEADS_A, KV_A, HD_A = 16, 2, 64
GROUPS_B = 8
WIDTH_B = D_MODEL // 2
LEVELS = (128, 64, 32, 16, 8, 4, 2, 1)
SCALE_LA = float(P) ** -0.5
LN_LEAST = 2.0 ** -63

EVEN_IN = [(1024, 256), (0, 512), (512, 512)] + [(1280 + 512 * i, 512) for i in range(8)]
E_KV, E_Q, E_GA, E_U, E_VB, E_GB = 0, 1, 3, 5, 7, 9
ODD_IN = [(0, 512), (1024, 512), (3072, 512), (512, 512), (1536, 512), (3584, 512), (6144, 272), (4096, 512), (4608, 512),
          (6416, 512), (6928, 256), (2048, 512), (2560, 512), (5120, 512), (5632, 512)]
GLR = 16
O_Q, O_F, O_GATES, O_GLR, O_V = (0, 3, 7), (1, 4, 8), {2: 0, 5: 512, 6: 1024, 9: 1280, 10: 1792}, 6, 11
GROUPS_LA = 3

C_MIX, C_GATE, C_ONORM = 0, 2 * KT, 4 * KT
C_BSP = C_ONORM + KT
C_LB = C_BSP + GROUPS_B
C_BG = C_LB + 16
N_ROWS = C_BG + 4

PLAN = ([("in0", i) for i in range(len(EVEN_IN))] + [("e0", i) for i in range(CHUNKS)]
        + [("out0", i) for i in range(CHUNKS)] + [("gate0", i) for i in range(CHUNKS)]
        + [("in1", i) for i in range(len(ODD_IN))]
        + [("e1", i) for i in range(CHUNKS)] + [("out1", i) for i in range(CHUNKS)]
        + [("gate1", i) for i in range(CHUNKS)])
NUMBER = {c: n for n, c in enumerate(PLAN)}


def slots_of(c):
    return 1 if c[0] in ("e0", "e1") else SLOTS


FIRST_SLOT = {c: sum(slots_of(d) for d in PLAN[:n]) for n, c in enumerate(PLAN)}

UNITS = ([(0, list(range(4 * u, 4 * u + 4))) for u in range(HEADS_A // 4)]
         + [(1, list(range(2 * u, 2 * u + 2))) for u in range(HEADS_A // 2)])

T_USES = (["x0", "x3", "p0", "wsp", "k", "q0", "q1"] + [f"P{u}" for u in range(len(UNITS))]
          + ["ya0", "ya1", "yb0", "yb1"] + [f"out0{c}" for c in range(CHUNKS)] + [f"gate0{c}" for c in range(CHUNKS)]
          + ["p1", "f0", "g0", "f1", "g1", "glr", "f2", "g2"] + [f"yo{c}" for c in range(CHUNKS)]
          + [f"out1{c}" for c in range(CHUNKS)])
M0_USES = ([f"S{u}" for u in range(len(UNITS))]
           + [f"A{n}{a}" for n in range(GROUPS_LA) for a in ["d0", "d1", *range(len(LEVELS))]] + [f"AV{i}" for i in (1, 3, 5, 7)])
M1_USES = [f"O{u}" for u in range(len(UNITS))] + [f"mix{i}" for i in range(4)] + ["up0", "up1"] + [f"AV{i}" for i in (0, 2, 4, 6)]
T_NO, M0_NO, M1_NO = ({u: i for i, u in enumerate(x)} for x in (T_USES, M0_USES, M1_USES))

SPLITS = {**{f"x{c}": (0, 4 * c, C_MIX + 4 * c) for c in range(CHUNKS)}, "p0": ("p", 0, None),
          "ya0": (1, 0, None), "ya1": (1, 4, None), "yb0": (1, 8, None), "yb1": (1, 12, None),
          **{f"out0{c}": (0, 4 * c, C_GATE + 4 * c) for c in range(CHUNKS)},
          **{f"gate0{c}": (1, 4 * c, C_MIX + KT + 4 * c) for c in range(CHUNKS)},
          "p1": ("p", 0, None), **{f"yo{c}": (0, 4 * c, C_ONORM + 4 * c) for c in range(CHUNKS)},
          **{f"out1{c}": (1, 4 * c, C_GATE + KT + 4 * c) for c in range(CHUNKS)}}
SPLIT_NO = {u: i for i, u in enumerate(["x0", "x1", "x2"] + [u for u in T_USES[1:] if u in SPLITS])}

STATS = [("X", 2, D_MODEL), ("V", 4, WIDTH_B), ("E0", 8, D_MODEL), ("H0", 8, D_MODEL), ("H1", 8, D_MODEL),
         ("E1", 8, D_MODEL), ("H2", 8, D_MODEL), ("H3", 8, D_MODEL)]
STAT_NO = {s[0]: i for i, s in enumerate(STATS)}

AT_K, AT_Q, AT_SCORES, AT_TURN, AT_VALUES = 10, 18, 30, 33, 35
AT_YA, AT_MIX, AT_YB = 62, 78, 85
AT_P0, AT_SPATIAL = 2, 4
AT_P1, AT_GLR, AT_AV, AT_YO = 5, 59, 99, 104
G_F, G_Q, G_DIAG, G_LEVEL = 1, 4, 7, 10


def group_start(n):
    return SLOTS * (O_F[n] + 1) + 1


def av_place(i):
    return AT_AV + SLOTS * (i // 2) + 2 * (i % 2)


def av_heads(i):
    c = i // 2
    return (4, P, 4 * c) if c < 2 else (2, 2 * P, 8 + 2 * (c - 2))


def trunk(nc, x, p, norm_mix, w_in_even, sinks_a, vnorm_b, w_spatial_b, b_spatial_b, w_out_even,
          w_in_odd, lower_bounds_c, onorm_c, w_gate_up_d, b_gate_d, onorm_d, w_out_odd,
          w_ple_proj, ple_norm, ple_gate_norm, w_ple_gate, final_norm, out):
    with ExitStack() as ctx:
        def sb(name, shape, dt=F32):
            return ctx.enter_context(nc.sbuf_tensor(name, shape, dt))

        def sem(name):
            return ctx.enter_context(nc.semaphore(name))

        raw = sb("raw", [P, RING, K_PER_SLOT * COLS])
        whi = sb("whi", [P, RING, K_PER_SLOT * COLS], F32R)
        wlo = sb("wlo", [P, RING, K_PER_SLOT * COLS], F32R)
        h = sb("h", [P, TILES, D_MODEL])
        bhi = [sb(f"bhi{i}", [P, KT, SEQ], F32R) for i in range(2)]
        blo = [sb(f"blo{i}", [P, KT, SEQ], F32R) for i in range(2)]
        phi = sb("phi", [P, PLE // P, SEQ], F32R)
        plo = sb("plo", [P, PLE // P, SEQ], F32R)
        e = sb("e", [P, TILES, D_MODEL])
        ident = sb("ident", [P, P])
        ones = sb("ones", [P, P])
        cols = sb("cols", [P, N_ROWS])
        band = sb("band", [P, 2, P])
        lmask = sb("lmask", [P, len(LEVELS) - 1, P // 2])
        nsink = sb("nsink", [P, HEADS_A])
        small = sb("small", [P, 512])
        glrT = sb("glrT", [GLR, SEQ])
        glr = sb("glr_z", [P, TILES, GLR])
        junk = sb("junk", [P, COLS])
        upw = sb("upw", [GLR, 4 * P])
        WORK = 15872
        work = sb("work", [P, WORK])

        def flat(a):
            return a.rearrange("p a b -> p (a b)")

        def part(first, a, b):
            return work[:, first:first + a * b].rearrange("p (a b) -> p a b", b=b)

        qo = part(0, TILES, 1024)
        qT = part(2048, 8, SEQ)
        kv = part(4096, TILES, 256)
        kT = work[:, 4608:5632].rearrange("p (g z n) -> p g z n", g=KV_A, z=2)
        Pm = part(5632, 2, COLS)
        PT = part(6656, 2, COLS)
        ga = part(7680, TILES, 1024)
        u_b = part(9728, TILES, 1024)
        v_b = part(11776, TILES, 1024)
        vgain = work[:, 13824:14848]
        wT = part(14848, GROUPS_B, P)
        kpad = work[:, 6656:7680].rearrange("p (t g z d) -> p t g z d", t=TILES, g=KV_A, z=2)
        rows = work[0:N_ROWS, 7680:7680 + P]
        level_buf = [flat(e)[:, 1024 * i:1024 * (i + 1)] for i in range(4)]
        wsp = part(11776, GROUPS_B, P)
        pin0 = part(5632, TILES, PLE)
        sg0 = part(2048, TILES, COLS)
        zq = part(0, TILES, COLS)
        zf = part(1024, TILES, COLS)
        gq = part(2048, 4, SEQ)
        gk = part(3072, 4, SEQ)
        gg = part(4096, 4, SEQ)
        lv = part(5120, 2, 1024)
        ATd = part(7168, 24, P)
        ATx = part(10240, 12, P)
        O = part(11776, TILES, D_MODEL)
        pin1 = part(0, TILES, PLE)
        sgate = [part(5120 + 1024 * i, TILES, COLS) for i in range(2)]
        gbc = work[:, 13824:15872]

        ms = small[:, 0:64].rearrange("p (r t c) -> p r t c", r=8, t=2)
        mean = small[:, 64:80].rearrange("p (r t) -> p r t", r=8)
        var = small[:, 80:96].rearrange("p (r t) -> p r t", r=8)
        rstd = small[:, 96:112].rearrange("p (r t) -> p r t", r=8)

        def heads_of(first, n):
            return small[:, first:first + 2 * n].rearrange("p (t h) -> p t h", t=2)

        mhalf = small[:, 112:136]
        nmax, dsink, esink, psumr, rinv = (heads_of(136 + 32 * i, HEADS_A) for i in range(5))
        oms, ovar, orstd = (heads_of(296 + 24 * i, 12) for i in range(3))
        lb_max, lb_a, lb_b, lb_sum, lb, omlb = (small[:, 368 + 8 * i:376 + 8 * i] for i in range(6))

        acc = [[ctx.enter_context(nc.psum_tensor(f"acc{a}{t}", [P, COLS], F32)) for t in range(2)] for a in range(2)]
        T = [ctx.enter_context(nc.psum_tensor(f"T{i}", [P, COLS], F32)) for i in range(2)]
        M0 = ctx.enter_context(nc.psum_tensor("M0", [P, COLS], F32))
        M1 = ctx.enter_context(nc.psum_tensor("M1", [P, COLS], F32))

        landed = [sem(f"landed{i}") for i in range(RING)]
        hi_made, lo_made, slot_used = sem("hi_made"), sem("lo_made"), sem("slot_used")
        acc_read = [sem("acc_read0"), sem("acc_read1")]
        t_full, t_read, t_hi, x_turned = sem("t_full"), sem("t_read"), sem("t_hi"), sem("x_turned")
        m0_full, m0_read, m1_full, m1_read = sem("m0_full"), sem("m0_read"), sem("m1_full"), sem("m1_read")
        x_in = [sem(f"x_in{i}") for i in range(CHUNKS)]
        rows_in, wsp_in, p_in, sink_in, vgain_in, up_in, gain_in, stored = (
            sem(n) for n in ("rows_in", "wsp_in", "p_in", "sink_in", "vgain_in", "up_in", "gain_in", "stored"))
        small_zero, ident_made, masks_made, kpad_zero, scores_zero = (
            sem(n) for n in ("small_zero", "ident_made", "masks_made", "kpad_zero", "scores_zero"))
        cols_full, cols_made, spatial_masked, lb_shifted, lb_exps = (
            sem(n) for n in ("cols_full", "cols_made", "spatial_masked", "lb_shifted", "lb_exps"))
        squares, mean_made, rstd_made = sem("squares"), sem("mean_made"), sem("rstd_made")
        kpad_made, scores_shifted, probs_made, ga_made, y_gated, v_normed = (
            sem(n) for n in ("kpad_made", "scores_shifted", "probs_made", "ga_made", "y_gated", "v_normed"))
        sig_made, f_made, ln_made, abs_made, lv_sub, lv_exp, lv_mul, o_squares, o_rstd = (
            sem(n) for n in ("sig_made", "f_made", "ln_made", "abs_made", "lv_sub", "lv_exp", "lv_mul",
                             "o_squares", "o_rstd"))
        e_scaled, h_gated, h_gained = sem("e_scaled"), sem("h_gated"), sem("h_gained")
        normed = [sem("normed0"), sem("normed1")]
        dve_step, act_step, pool_step = sem("dve_step"), sem("act_step"), sem("pool_step")

        def source(c, s):
            phase, i = c
            layer = int(phase[-1])
            if phase[:-1] == "in":
                w = (w_in_even, w_in_odd)[layer][0]
                c0, n = (EVEN_IN, ODD_IN)[layer][i]
            else:
                w = {"e0": w_ple_proj[0], "e1": w_ple_proj[1], "out0": w_out_even[0], "out1": w_out_odd[0],
                     "gate0": w_ple_gate[0], "gate1": w_ple_gate[1]}[phase]
                c0, n = i * COLS, COLS
            r0 = s * K_PER_SLOT * P
            return w[r0:r0 + K_PER_SLOT * P, c0:c0 + n].rearrange("(k p) n -> p k n", p=P)

        def slot_view(ring, c, s):
            n = EVEN_IN[c[1]][1] if c[0] == "in0" else ODD_IN[c[1]][1] if c[0] == "in1" else COLS
            r = (FIRST_SLOT[c] + s) % RING
            return ring[:, r, 0:K_PER_SLOT * n].rearrange("p (k n) -> p k n", n=n)

        def wait_chunk(eng, c):
            eng.wait_ge(slot_used, FIRST_SLOT[c] + slots_of(c))

        def wait_read(eng, c):
            eng.wait_ge(acc_read[NUMBER[c] % 2], NUMBER[c] // 2 + 1)

        def wait_use(eng, s, table, name):
            eng.wait_ge(s, table[name] + 1)

        def wait_rstd(eng, name):
            eng.wait_ge(rstd_made, STAT_NO[name] + 1)

        banks = {"x1": (M0, M1), "x2": acc[1]}

        def av_bank(i):
            return (M1, m1_full, m1_read, M1_NO) if i % 2 == 0 else (M0, m0_full, m0_read, M0_NO)

        def level_views(a, m):
            return a.rearrange("p (b z m) -> p b z m", z=2, m=m)

        block = ctx.enter_context(nc.Block())

        @block.sync
        def _(sp):
            row = 0
            for v in (norm_mix.rearrange("a b -> (a b)"), ple_gate_norm.rearrange("a b -> (a b)"), onorm_c[0], onorm_d[0],
                      b_spatial_b[0].rearrange("a b -> (a b)"), lower_bounds_c.rearrange("a b -> (a b)"), b_gate_d[0]):
                n = v.shape[0] // P
                sp.dma_start(rows[row:row + n, :], v.rearrange("(r c) -> r c", c=P)).then_inc(rows_in, 16)
                row += n
            for c in range(CHUNKS):
                sp.dma_start(h[:, :, c * COLS:(c + 1) * COLS],
                             x[0, :, c * COLS:(c + 1) * COLS].rearrange("(t p) d -> p t d", p=P)).then_inc(x_in[c], 16)

            def weights(c, first=0, end=SLOTS):
                for s in range(first, min(end, slots_of(c))):
                    n = FIRST_SLOT[c] + s
                    if n >= RING:
                        sp.wait_ge(lo_made, n - RING + 1)
                    sp.dma_start(slot_view(raw, c, s), source(c, s)).then_inc(landed[n % RING], 16)

            weights(PLAN[0], 0, RING)
            sp.dma_start(pin0, p[0, 0].rearrange("(t p) d -> p t d", p=P)).then_inc(p_in, 16)
            sp.dma_start(wsp, w_spatial_b[0].rearrange("g t s -> t g s")).then_inc(wsp_in, 16)
            sp.dma_start(nsink[:], sinks_a[0].partition_broadcast(P)).then_inc(sink_in, 16)
            sp.dma_start(vgain, vnorm_b[0].partition_broadcast(P)).then_inc(vgain_in, 16)
            weights(PLAN[0], RING)
            for c in PLAN[1:]:
                weights(c)
                if c == ("out0", 0):
                    wait_use(sp, m1_read, M1_NO, "mix3")
                    sp.dma_start(gbc, ple_norm[0].partition_broadcast(P)).then_inc(gain_in, 16)
                    sp.dma_start(upw[:], w_gate_up_d[0]).then_inc(up_in, 16)
                    wait_use(sp, t_full, T_NO, "ya1")
                    sp.dma_start(pin1, p[1, 0].rearrange("(t p) d -> p t d", p=P)).then_inc(p_in, 16)
                if c == ("out1", 0):
                    wait_use(sp, t_full, T_NO, "yo3")
                    sp.dma_start(gbc, ple_norm[1].partition_broadcast(P)).then_inc(gain_in, 16)
                if c == ("gate1", 0):
                    sp.wait_ge(e_scaled, 2 * CHUNKS)
                    sp.dma_start(gbc, final_norm.partition_broadcast(P)).then_inc(gain_in, 16)
            for half in range(2):
                for t in range(TILES):
                    sp.wait_ge(normed[t], half + 1)
                    cs = slice(half * 1024, (half + 1) * 1024)
                    sp.dma_start(out[0, t * P:(t + 1) * P, cs], e[:, t, cs]).then_inc(stored, 16)
            sp.wait_ge(stored, 16 * 2 * TILES)

        @block.tensor
        def _(pe):
            def take_T(name):
                if T_NO[name]:
                    pe.wait_ge(t_read, T_NO[name])

            def turn(name, src):
                B = banks.get(name, T)
                if B is T:
                    take_T(name)
                for k in range(4):
                    for t in range(TILES):
                        last = nc.tensor.transpose(B[k // 2][:, (k % 2) * SEQ + t * P:(k % 2) * SEQ + (t + 1) * P],
                                                   src[:, t, k * P:(k + 1) * P], ident[:])
                last.then_inc(t_full if B is T else x_turned, 1)

            def turn_p(name, src, loads):
                pe.wait_ge(p_in, 16 * loads)
                take_T(name)
                for k in range(PLE // P):
                    for t in range(TILES):
                        last = nc.tensor.transpose(T[0][:, k * SEQ + t * P:k * SEQ + (t + 1) * P],
                                                   src[:, t, k * P:(k + 1) * P], ident[:])
                last.then_inc(t_full, 1)

            def slot(c, s, hi, lo):
                n = FIRST_SLOT[c] + s
                wh, wl = slot_view(whi, c, s), slot_view(wlo, c, s)
                k_n, w = wh.shape[1:]
                pe.wait_ge(lo_made, n + 1)
                for k in range(k_n):
                    first, final = s == 0 and k == 0, s == slots_of(c) - 1 and k == k_n - 1
                    for t in range(TILES):
                        o = acc[NUMBER[c] % 2][t][:, 0:w]
                        xh, xl = (b[:, K_PER_SLOT * s + k, t * P:(t + 1) * P] for b in (hi, lo))
                        nc.tensor.matmul(o, xh, wl[:, k, :], start=first, stop=False)
                        nc.tensor.matmul(o, xl, wh[:, k, :], start=False, stop=False)
                        last = nc.tensor.matmul(o, xh, wh[:, k, :], start=False, stop=final)
                last.then_inc(slot_used, 1)

            def chunk(c, buf, late=None, between=lambda s: None):
                if NUMBER[c] >= 2:
                    wait_read(pe, PLAN[NUMBER[c] - 2])
                for s in range(SLOTS):
                    if s == SLOTS - 2 and late:
                        wait_use(pe, t_read, T_NO, late)
                    slot(c, s, bhi[buf], blo[buf])
                    between(s)

            def embed(layer):
                wait_use(pe, t_read, T_NO, f"p{layer}")
                for i in range(CHUNKS):
                    wait_read(pe, PLAN[NUMBER[(f"e{layer}", i)] - 2])
                    slot((f"e{layer}", i), 0, phi, plo)

            def scores(u):
                b, heads = UNITS[u]
                if u == 0:
                    wait_use(pe, t_read, T_NO, "q1")
                else:
                    wait_use(pe, m0_read, M0_NO, f"S{u - 1}")
                nk = P * (b + 1)
                for i, hd in enumerate(heads):
                    last = nc.tensor.matmul(M0[:, i * nk:(i + 1) * nk], qT[:, hd // 2, b * P:(b + 1) * P],
                                            kT[:, hd // 8, hd % 2, 0:nk], start=True, stop=True)
                last.then_inc(m0_full, 1)

            def turn_probs(u):
                pe.wait_ge(probs_made, u + 1)
                take_T(f"P{u}")
                for i in range(4):
                    last = nc.tensor.transpose(T[0][:, i * P:(i + 1) * P], Pm[:, u % 2, i * P:(i + 1) * P], ident[:])
                last.then_inc(t_full, 1)

            def values(u):
                b, heads = UNITS[u]
                wait_use(pe, t_read, T_NO, f"P{u}")
                if u:
                    wait_use(pe, m1_read, M1_NO, f"O{u - 1}")
                for i, hd in enumerate(heads):
                    v0 = P + (hd // 8) * HD_A
                    for j in range(b + 1):
                        q = (i * (b + 1) + j) * P
                        last = nc.tensor.matmul(M1[:, i * HD_A:(i + 1) * HD_A], PT[:, u % 2, q:q + P],
                                                kv[:, j, v0:v0 + HD_A], start=(j == 0), stop=(j == b))
                last.then_inc(m1_full, 1)

            def mix(i):
                t, half = i // 2, i % 2
                pe.wait_ge(m1_read, M1_NO[f"mix{i}"])
                for g in range(4 * half, 4 * half + 4):
                    last = nc.tensor.matmul(M1[:, (g % 4) * P:(g % 4 + 1) * P], wT[:, g, :],
                                            v_b[:, t, g * P:(g + 1) * P], start=True, stop=True)
                last.then_inc(m1_full, 1)

            def even(i, s):
                at = SLOTS * i + s
                if at == AT_P0:
                    turn_p("p0", pin0, 1)
                if at == AT_SPATIAL:
                    pe.wait_ge(wsp_in, 16)
                    take_T("wsp")
                    for g in range(GROUPS_B):
                        last = nc.tensor.transpose(T[g // 4][:, (g % 4) * P:(g % 4 + 1) * P], wsp[:, g, :], ident[:])
                    last.then_inc(t_full, 1)
                if at == AT_K:
                    pe.wait_ge(kpad_made, 1)
                    take_T("k")
                    for g in range(KV_A):
                        for z in range(2):
                            for t in range(TILES):
                                last = nc.tensor.transpose(T[g][:, z * SEQ + t * P:z * SEQ + (t + 1) * P],
                                                           kpad[:, t, g, z, :], ident[:])
                    last.then_inc(t_full, 1)
                for c in range(2):
                    if at == AT_Q + SLOTS * c:
                        wait_read(pe, ("in0", E_Q + c))
                        turn(f"q{c}", qo[:, :, c * COLS:(c + 1) * COLS])
                for u in range(len(UNITS)):
                    if at == AT_SCORES + 2 * u:
                        scores(u)
                    if at == AT_TURN + 2 * u:
                        turn_probs(u)
                    if at == AT_VALUES + 2 * u:
                        values(u)
                for c in range(2):
                    if at == AT_YA + 3 * c:
                        pe.wait_ge(y_gated, c + 1)
                        turn(f"ya{c}", qo[:, :, c * COLS:(c + 1) * COLS])
                for m in range(4):
                    if at == AT_MIX + m:
                        if m == 0:
                            pe.wait_ge(v_normed, TILES)
                            pe.wait_ge(spatial_masked, 1)
                        mix(m)
                if at == AT_YB:
                    pe.wait_ge(y_gated, 3)
                    turn("yb0", u_b[:, :, 0:COLS])

            def level(n, i):
                m, X = LEVELS[i], level_buf[i % 4]
                pe.wait_ge(lv_mul, n * len(LEVELS) + i + 1)
                pe.wait_ge(m0_read, M0_NO[f"A{n}{i}"])
                if m == P:
                    for hd in range(4):
                        last = nc.tensor.matmul(M0[:, hd * P:(hd + 1) * P], X[:, hd * SEQ:hd * SEQ + P],
                                                X[:, hd * SEQ + P:(hd + 1) * SEQ], start=True, stop=True)
                else:
                    for j in range(8):
                        Xj = X[:, j * P:(j + 1) * P]
                        last = nc.tensor.matmul(M0[:, j * 64:(j + 1) * 64].rearrange("p (b m) -> p b m", m=m), Xj,
                                                level_views(Xj, m)[:, :, 1, :], start=True, stop=True)
                last.then_inc(m0_full, 1)

            def diagonal(n, half):
                pe.wait_ge(m0_read, M0_NO[f"A{n}d{half}"])
                for j in range(4):
                    o = (4 * half + j) * P
                    last = nc.tensor.matmul(M0[:, j * P:(j + 1) * P], flat(gk)[:, o:o + P], flat(gq)[:, o:o + P],
                                            start=True, stop=True)
                last.then_inc(m0_full, 1)

            def apply_scores(i):
                c, t = i // 2, i % 2
                bank, full, read, number = av_bank(i)
                n_heads, dv, first = av_heads(i)
                wait_read(pe, ("in1", O_V + c))
                wait_use(pe, m0_read, M0_NO, f"A{first // 4}7")
                pe.wait_ge(read, number[f"AV{i}"])
                v = (zq, zf)[c % 2]
                for j in range(n_heads):
                    o = bank[:, j * dv:(j + 1) * dv]
                    if t:
                        nc.tensor.matmul(o, ATx[:, first + j, :], v[:, 0, j * dv:(j + 1) * dv], start=True, stop=False)
                    last = nc.tensor.matmul(o, ATd[:, 2 * (first + j) + t, :], v[:, t, j * dv:(j + 1) * dv],
                                            start=(t == 0), stop=True)
                last.then_inc(full, 1)

            def turn_o(c):
                wait_use(pe, m0_read, M0_NO, f"AV{2 * c + 1}")
                turn(f"yo{c}", O[:, :, c * COLS:(c + 1) * COLS])

            def odd(i, s):
                at = SLOTS * i + s
                if at == 2:
                    pe.wait_ge(h_gated, CHUNKS)
                    turn("gate03", h[:, :, 3 * COLS:4 * COLS])
                if at == AT_P1:
                    turn_p("p1", pin1, 2)
                for n in range(GROUPS_LA):
                    b = group_start(n)
                    if at == b + G_F:
                        wait_read(pe, ("in1", O_F[n]))
                        turn(f"f{n}", zf)
                        if n == 2:
                            pe.wait_ge(up_in, 16)
                            for half in range(2):
                                pe.wait_ge(m1_read, M1_NO[f"up{half}"])
                                for j in range(2):
                                    hd = 2 * half + j
                                    last = nc.tensor.matmul(M1[:, j * SEQ:(j + 1) * SEQ], upw[:, hd * P:(hd + 1) * P],
                                                            glrT[:], start=True, stop=True)
                                last.then_inc(m1_full, 1)
                    if at == b + G_Q:
                        turn(f"g{n}", zq)
                    for j in range(len(LEVELS)):
                        if at == b + G_LEVEL + 2 * j:
                            level(n, j)
                    for half in range(2):
                        if at == b + G_DIAG + half:
                            diagonal(n, half)
                if at == AT_GLR:
                    wait_read(pe, ("in1", O_GLR))
                    take_T("glr")
                    for t in range(TILES):
                        last = nc.tensor.transpose(T[0][0:GLR, t * P:(t + 1) * P], glr[:, t, :], ident[:])
                    last.then_inc(t_full, 1)
                for j in range(6):
                    if at == av_place(j):
                        apply_scores(j)
                for c in range(2):
                    if at == AT_YO + SLOTS * c:
                        turn_o(c)

            def turn_out(layer, c):
                wait_read(pe, (f"out{layer}", c))
                turn(f"out{layer}{c}", h[:, :, c * COLS:(c + 1) * COLS])

            def turn_gate(c):
                pe.wait_ge(h_gated, c + 1)
                turn(f"gate0{c}", h[:, :, c * COLS:(c + 1) * COLS])

            pe.wait_ge(ident_made, 1)
            pe.wait_ge(rows_in, 16 * 7)
            nc.tensor.transpose(acc[0][0][:, 0:N_ROWS], rows, ident[0:N_ROWS, 0:N_ROWS]).then_inc(cols_full, 1)
            for c in range(CHUNKS):
                pe.wait_ge(x_in[c], 16)
                turn(f"x{c}", h[:, :, c * COLS:(c + 1) * COLS])
            wait_use(pe, t_read, T_NO, "x3")
            for i in range(len(EVEN_IN)):
                chunk(("in0", i), 0, between=lambda s: even(i, s))
            embed(0)
            pe.wait_ge(y_gated, 4)
            turn("yb1", u_b[:, :, COLS:2 * COLS])
            for c in range(CHUNKS):
                chunk(("out0", c), 1, late=None if c else "yb1",
                      between=lambda s: turn_out(0, c - 1) if c and s == 2 else None)
            for c in range(CHUNKS):
                chunk(("gate0", c), 0, late=None if c else "out03",
                      between=lambda s: None if s != 2 else turn_gate(c - 1) if c else turn_out(0, 3))
            for i in range(len(ODD_IN)):
                chunk(("in1", i), 1, late=None if i else "gate03", between=lambda s: odd(i, s))
            embed(1)
            turn_o(2)
            apply_scores(6)
            apply_scores(7)
            for c in range(CHUNKS):
                chunk(("out1", c), 0, late=None if c else "yo3",
                      between=lambda s: turn_out(1, c - 1) if c and s == 2 else turn_o(3) if c == 0 and s == 3 else None)
            for c in range(CHUNKS):
                chunk(("gate1", c), 1, late=None if c else "out13",
                      between=lambda s: turn_out(1, 3) if c == 0 and s == 2 else None)

        @block.scalar
        def _(act):
            steps = [0]
            sq_n, o_sq_n = [0], [0]

            def link(ins):
                steps[0] += 1
                ins.then_inc(act_step, 1)
                act.wait_ge(act_step, steps[0])

            def split_w(c, s):
                n = FIRST_SLOT[c] + s
                act.wait_ge(landed[n % RING], 16 * (n // RING + 1))
                if n >= RING:
                    act.wait_ge(slot_used, n - RING + 1)
                nc.scalar.activation(slot_view(whi, c, s), slot_view(raw, c, s), ACT.Copy).then_inc(hi_made, 1)

            def split_T(name):
                buf, k0, gain = SPLITS[name]
                B = banks.get(name, T)
                if B is T:
                    wait_use(act, t_full, T_NO, name)
                else:
                    act.wait_ge(x_turned, ["x1", "x2"].index(name) + 1)
                if gain is None:
                    hi = phi if buf == "p" else bhi[buf]
                    for i in range(1 if buf == "p" else 2):
                        last = nc.scalar.activation(hi[:, k0 + 2 * i:k0 + 2 * i + 2, :].rearrange("p a b -> p (a b)"),
                                                    T[i][:], ACT.Copy)
                else:
                    if gain == C_MIX:
                        act.wait_ge(cols_made, 1)
                    for k in range(4):
                        last = nc.scalar.activation(bhi[buf][:, k0 + k, :], B[k // 2][:, (k % 2) * SEQ:(k % 2 + 1) * SEQ],
                                                    ACT.Copy, scale=cols[:, gain + k:gain + k + 1])
                last.then_inc(t_hi, 1)

            def square(src, dst):
                if sq_n[0]:
                    act.wait_ge(squares, sq_n[0])
                if o_sq_n[0]:
                    act.wait_ge(o_squares, o_sq_n[0])
                sq_n[0] += 1
                nc.scalar.activation(junk[:, 0:src.shape[-1]], src, ACT.Square, accum_out=dst).then_inc(squares, 1)

            def square_chunk(src, stat, c):
                for t in range(TILES):
                    square(src[:, t, c * COLS:(c + 1) * COLS], ms[:, STAT_NO[stat], t, c:c + 1])

            def read_out(c, dst, func, stat):
                wait_chunk(act, c)
                wait_rstd(act, stat)
                for t in range(TILES):
                    last = nc.scalar.activation(dst(t), acc[NUMBER[c] % 2][t][:, 0:dst(t).shape[-1]], func,
                                                scale=rstd[:, STAT_NO[stat], t:t + 1])
                last.then_inc(acc_read[NUMBER[c] % 2], 1)

            def softmax(u):
                b, heads = UNITS[u]
                act.wait_ge(scores_shifted, u + 1)
                nk = P * (b + 1)
                for i, hd in enumerate(heads):
                    s = Pm[:, u % 2, i * nk:(i + 1) * nk]
                    nc.scalar.activation(s, s, ACT.Exp, bias=nmax[:, b, hd:hd + 1], accum_out=psumr[:, b, hd:hd + 1])
                hs = slice(heads[0], heads[-1] + 1)
                nc.scalar.activation(esink[:, b, hs], dsink[:, b, hs], ACT.Exp).then_inc(probs_made, 1)

            def even(i, s):
                at = SLOTS * i + s
                if at == AT_P0 + 2:
                    split_T("p0")
                if at == AT_SPATIAL + 2:
                    act.wait_ge(lb_shifted, 1)
                    nc.scalar.activation(small[:, 376:392], small[:, 376:392], ACT.Exp).then_inc(lb_exps, 1)
                if s == 1 and i:
                    c = i - 1
                    if c == E_KV:
                        read_out(("in0", c), lambda t: kv[:, t, :], ACT.Copy, "X")
                    for first, dst, func in ((E_Q, qo, ACT.Copy), (E_GA, ga, ACT.Copy), (E_U, u_b, ACT.Gelu),
                                             (E_VB, v_b, ACT.Gelu)):
                        if first <= c < first + 2:
                            o = (c - first) * COLS
                            read_out(("in0", c), lambda t: dst[:, t, o:o + COLS], func, "X")
                    if c == E_GB:
                        read_out(("in0", c), lambda t: sg0[:, t, :], ACT.Silu, "X")
                if at == AT_K + 2:
                    wait_use(act, t_full, T_NO, "k")
                    for g in range(KV_A):
                        last = nc.scalar.activation(kT[:, g].rearrange("p z n -> p (z n)"), T[g][:], ACT.Copy)
                    last.then_inc(t_read, 1)
                for c in range(2):
                    if at == AT_Q + SLOTS * c + 2:
                        wait_use(act, t_full, T_NO, f"q{c}")
                        for j in range(2):
                            last = nc.scalar.activation(flat(qT[:, 4 * c + 2 * j:4 * c + 2 * j + 2, :]), T[j][:], ACT.Copy,
                                                        scale=HD_A ** -0.5)
                        last.then_inc(t_read, 1)
                for u in range(len(UNITS)):
                    if at == AT_SCORES + 2 * u + 2:
                        softmax(u)
                    if at == AT_TURN + 2 * u + 2:
                        wait_use(act, t_full, T_NO, f"P{u}")
                        if u >= 2:
                            wait_use(act, m1_full, M1_NO, f"O{u - 2}")
                        nc.scalar.activation(PT[:, u % 2, :], T[0][:], ACT.Copy).then_inc(t_read, 1)
                for c in range(2):
                    if at == AT_YA - 2 + c:
                        g = ga[:, :, c * COLS:(c + 1) * COLS]
                        wait_read(act, ("in0", E_GA + c))
                        nc.scalar.activation(g, g, ACT.Silu).then_inc(ga_made, 1)
                    if at == AT_YA + 3 * c + 2:
                        split_T(f"ya{c}")
                if at == SLOTS * (E_VB + 2) + 2:
                    wait_read(act, ("in0", E_VB + 1))
                    for c in range(2):
                        square_chunk(v_b, "V", c)
                if at == AT_YB + 2:
                    split_T("yb0")

            def read_embed(layer, i):
                wait_read(act, (f"e{layer}", i))
                square_chunk(e, f"E{layer}", i)

            def read_outproj(layer, c):
                wait_read(act, (f"out{layer}", c))
                square_chunk(h, f"H{2 * layer}", c)

            def read_gate(layer, c):
                n = CHUNKS * layer + c
                if n >= 2:
                    act.wait_ge(h_gated, n - 1)
                read_out((f"gate{layer}", c), lambda t: sgate[n % 2][:, t, :], ACT.Sigmoid, f"H{2 * layer}")

            def square_gate(layer, c):
                act.wait_ge(h_gated, CHUNKS * layer + c + 1)
                square_chunk(h, f"H{2 * layer + 1}", c)

            def odd(i, s):
                at = SLOTS * i + s
                if at == 1:
                    read_gate(0, 3)
                if at == 3:
                    square_gate(0, 3)
                if at == 4:
                    split_T("gate03")
                if at == AT_P1 + 2:
                    split_T("p1")
                if s == 1 and i:
                    read_odd(i - 1)
                if at == AT_GLR + 2:
                    wait_use(act, t_full, T_NO, "glr")
                    nc.scalar.activation(glrT[:], T[0][0:GLR, 0:SEQ], ACT.Copy).then_inc(t_read, 1)
                for n in range(GROUPS_LA):
                    b = group_start(n)
                    if at == b + G_F + 2 and n < 2:
                        wait_use(act, t_full, T_NO, f"f{n}")
                        for j in range(2):
                            last = nc.scalar.activation(lv[:, 0, j * COLS:(j + 1) * COLS], T[j][:], ACT.Sigmoid)
                        last.then_inc(t_read, 1)
                    if at == b + G_F + 3 and n < 2:
                        act.wait_ge(f_made, n + 1)
                        nc.scalar.activation(lv[:, 0, :], lv[:, 1, :], ACT.Ln).then_inc(ln_made, 1)
                    if at == b + G_F + 2 and n == 2:
                        wait_use(act, t_full, T_NO, "f2")
                        wait_use(act, m0_full, M0_NO, "A17")
                        for j in range(2):
                            last = nc.scalar.activation(flat(gk)[:, j * COLS:(j + 1) * COLS], T[j][:], ACT.Copy)
                        last.then_inc(t_read, 1)
                        for half in range(2):
                            wait_use(act, m1_full, M1_NO, f"up{half}")
                            for j in range(2):
                                hd = 2 * half + j
                                last = nc.scalar.activation(lv[:, 0, hd * SEQ:(hd + 1) * SEQ], M1[:, j * SEQ:(j + 1) * SEQ],
                                                            ACT.Abs, bias=cols[:, C_BG + hd:C_BG + hd + 1])
                            last.then_inc(abs_made, 1)
                        act.wait_ge(abs_made, 2)
                        link(nc.scalar.activation(lv[:, 0, :], lv[:, 0, :], ACT.Exp, scale=-1.0))
                        nc.scalar.activation(lv[:, 0, :], lv[:, 0, :], ACT.Ln, bias=1.0).then_inc(ln_made, 1)
                    if at == b + G_Q + 2:
                        wait_use(act, t_full, T_NO, f"g{n}")
                        if n:
                            wait_use(act, m0_full, M0_NO, f"A{n - 1}7")
                        for j in range(2):
                            last = nc.scalar.activation(flat(gq)[:, j * COLS:(j + 1) * COLS], T[j][:], ACT.Copy,
                                                        scale=SCALE_LA)
                        last.then_inc(t_read, 1)
                    for j in range(len(LEVELS)):
                        if at == b + G_LEVEL + 2 * j - 3:
                            act.wait_ge(lv_sub, n * len(LEVELS) + j + 1)
                            X = level_buf[j % 4]
                            if j == 0:
                                for hd in range(4):
                                    nc.scalar.activation(X[:, hd * SEQ:hd * SEQ + P], gg[:, hd, 0:P], ACT.Exp,
                                                         bias=gg[:, hd, P - 1:P], scale=-1.0)
                                nc.scalar.activation(level_views(X, P)[:, :, 1, :], gg[:, :, P:SEQ], ACT.Exp).then_inc(lv_exp, 1)
                            else:
                                nc.scalar.activation(X, X, ACT.Exp).then_inc(lv_exp, 1)
                    if at == b + G_LEVEL + 2:
                        wait_use(act, m0_full, M0_NO, f"A{n}0")
                        nc.scalar.activation(flat(ATx[:, 4 * n:4 * n + 4, :]), M0[:], ACT.Copy).then_inc(m0_read, 1)
                for j in range(6):
                    if at == av_place(j) + 2:
                        square_o(j)
                for c in range(2):
                    if at == AT_YO + SLOTS * c + 2:
                        split_T(f"yo{c}")

            def square_o(j):
                bank, full, _, number = av_bank(j)
                n_heads, dv, first = av_heads(j)
                wait_use(act, full, number, f"AV{j}")
                act.wait_ge(squares, sq_n[0])
                for k in range(n_heads):
                    if o_sq_n[0]:
                        act.wait_ge(o_squares, o_sq_n[0])
                    o_sq_n[0] += 1
                    nc.scalar.activation(junk[:, 0:dv], bank[:, k * dv:(k + 1) * dv], ACT.Square,
                                         accum_out=oms[:, j % 2, first + k:first + k + 1]).then_inc(o_squares, 1)

            def read_odd(c):
                cc = ("in1", c)
                if c in O_GATES:
                    col, skip = O_GATES[c], GLR if c == O_GLR else 0
                    n = ODD_IN[c][1] - skip
                    wait_chunk(act, cc)
                    wait_rstd(act, "H1")
                    if c == O_GLR:
                        for t in range(TILES):
                            nc.scalar.activation(glr[:, t, :], acc[NUMBER[cc] % 2][t][:, 0:GLR], ACT.Copy,
                                                 scale=rstd[:, STAT_NO["H1"], t:t + 1])
                    for t in range(TILES):
                        last = nc.scalar.activation(O[:, t, col:col + n], acc[NUMBER[cc] % 2][t][:, skip:skip + n], ACT.Silu,
                                                    scale=rstd[:, STAT_NO["H1"], t:t + 1])
                    last.then_inc(acc_read[NUMBER[cc] % 2], 1)
                    return
                if c in (O_Q[0], O_F[0]):
                    wait_use(act, t_full, T_NO, "p1")
                elif c in O_Q or c in O_F:
                    wait_use(act, t_full, T_NO, f"g{O_Q.index(c) - 1}" if c in O_Q else f"f{O_F.index(c) - 1}")
                elif c < O_V + 2:
                    wait_use(act, t_full, T_NO, ("g2", "f2")[c - O_V])
                else:
                    wait_use(act, m0_full, M0_NO, f"AV{2 * (c - O_V) - 3}")
                dst = zq if c in O_Q or c in (O_V, O_V + 2) else zf
                read_out(cc, lambda t: dst[:, t, :], ACT.Copy, "H1")

            def embed_and_out(layer, last_of_in):
                for i in range(CHUNKS):
                    split_w((f"e{layer}", i), 0)
                    if i == 1:
                        last_of_in()
                for c in range(CHUNKS):
                    for s in range(SLOTS):
                        split_w((f"out{layer}", c), s)
                        if c:
                            if s == 1:
                                read_outproj(layer, c - 1)
                            if s == 4:
                                split_T(f"out{layer}{c - 1}")
                        elif layer:
                            if s == 0:
                                split_T("yo2")
                            if s in (1, 2):
                                square_o(5 + s)
                            if s == 5:
                                split_T("yo3")
                            if s in (3, 4, 6, 7):
                                read_embed(layer, (3, 4, 6, 7).index(s))
                        else:
                            if s == 2:
                                split_T("yb1")
                            if s >= 4:
                                read_embed(layer, s - 4)

            def gate_phase(layer):
                for c in range(CHUNKS):
                    for s in range(SLOTS):
                        split_w((f"gate{layer}", c), s)
                        if s == 1 and c == 0:
                            read_outproj(layer, 3)
                        if s == 4 and c == 0:
                            split_T(f"out{layer}3")
                        if s == 1 and c:
                            read_gate(layer, c - 1)
                        if s == 3 and c:
                            square_gate(layer, c - 1)
                        if s == 4 and c and layer == 0:
                            split_T(f"gate0{c - 1}")

            for s in range(RING):
                split_w(PLAN[0], s)
            for c in range(CHUNKS):
                split_T(f"x{c}")
            act.wait_ge(small_zero, 1)
            for t in range(TILES):
                nc.scalar.activation(e[:, t, :], h[:, t, :], ACT.Square,
                                     accum_out=ms[:, STAT_NO["X"], t, 0:1]).then_inc(squares, 1)
                sq_n[0] += 1
            for i in range(len(EVEN_IN)):
                for s in range(SLOTS):
                    if i or s >= RING:
                        split_w(("in0", i), s)
                    even(i, s)

            def last_gate_b():
                act.wait_ge(y_gated, 3)
                read_out(("in0", E_GB + 1), lambda t: sg0[:, t, :], ACT.Silu, "X")

            embed_and_out(0, last_gate_b)
            gate_phase(0)
            for i in range(len(ODD_IN)):
                for s in range(SLOTS):
                    split_w(("in1", i), s)
                    odd(i, s)
            embed_and_out(1, lambda: read_odd(len(ODD_IN) - 1))
            gate_phase(1)
            read_gate(1, 3)
            square_gate(1, 3)
            wait_rstd(act, "H3")
            act.wait_ge(h_gained, TILES * CHUNKS)
            for half in range(2):
                o = e[:, 1, half * 1024:(half + 1) * 1024]
                nc.scalar.activation(o, o, ACT.Copy, scale=rstd[:, STAT_NO["H3"], 1:2]).then_inc(normed[1], 1)

        @block.vector
        def _(dve):
            steps = [0]

            def link(ins):
                steps[0] += 1
                ins.then_inc(dve_step, 1)
                dve.wait_ge(dve_step, steps[0])

            def split_w(c, s):
                n = FIRST_SLOT[c] + s
                dve.wait_ge(hi_made, n + 1)
                if n >= RING:
                    dve.wait_ge(slot_used, n - RING + 1)
                nc.vector.tensor_tensor(slot_view(wlo, c, s), slot_view(raw, c, s), slot_view(whi, c, s).bitcast(F32),
                                        ALU.subtract).then_inc(lo_made, 1)

            def split_T(name):
                buf, k0, gain = SPLITS[name]
                dve.wait_ge(t_hi, SPLIT_NO[name] + 1)
                B = banks.get(name, T)
                hi, lo = (phi, plo) if buf == "p" else (bhi[buf], blo[buf])
                if gain is None:
                    for i in range(1 if buf == "p" else 2):
                        ks = slice(k0 + 2 * i, k0 + 2 * i + 2)
                        last = nc.vector.tensor_tensor(flat(lo[:, ks, :]), T[i][:], flat(hi[:, ks, :]).bitcast(F32),
                                                       ALU.subtract)
                else:
                    for k in range(4):
                        last = nc.vector.scalar_tensor_tensor(
                            out=lo[:, k0 + k, :], in0=B[k // 2][:, (k % 2) * SEQ:(k % 2 + 1) * SEQ],
                            scalar=cols[:, gain + k:gain + k + 1], in1=hi[:, k0 + k, :].bitcast(F32),
                            op0=ALU.mult, op1=ALU.subtract)
                if B is T:
                    last.then_inc(t_read, 1)

            def row_mean(name):
                i = STAT_NO[name]
                dve.wait_ge(squares, sum(n for _, n, _ in STATS[:i + 1]))
                nc.vector.tensor_reduce(mean[:, i, :], ms[:, i], AX.X, ALU.add).then_inc(mean_made, 1)

            def shift_scores(u):
                b, heads = UNITS[u]
                n, nk = len(heads), P * (b + 1)
                hs = slice(heads[0], heads[-1] + 1)
                wait_use(dve, m0_full, M0_NO, f"S{u}")
                if u >= 2:
                    wait_use(dve, t_full, T_NO, f"P{u - 2}")
                mask = band[:] if b else band[:, 1:2, :]
                mask = flat(mask).unsqueeze(1).to_broadcast([P, n, nk])
                S = Pm[:, u % 2, :].rearrange("p (n k) -> p n k", k=nk)
                nc.vector.tensor_tensor(S, M0[:].rearrange("p (n k) -> p n k", k=nk), mask, ALU.add).then_inc(m0_read, 1)
                wait_use(dve, m0_read, M0_NO, f"S{u}")
                link(nc.vector.tensor_reduce(nmax[:, b, hs], S, AX.X, ALU.max, negate=True))
                link(nc.vector.tensor_tensor(nmax[:, b, hs], nmax[:, b, hs], nsink[:, hs], ALU.min))
                nc.vector.tensor_tensor(dsink[:, b, hs], nmax[:, b, hs], nsink[:, hs], ALU.subtract).then_inc(scores_shifted, 1)

            def attention_out(u):
                b, heads = UNITS[u]
                n = len(heads)
                hs = slice(heads[0], heads[-1] + 1)
                dve.wait_ge(probs_made, u + 1)
                link(nc.vector.tensor_tensor(rinv[:, b, hs], psumr[:, b, hs], esink[:, b, hs], ALU.add))
                link(nc.vector.reciprocal(rinv[:, b, hs], rinv[:, b, hs]))
                wait_use(dve, m1_full, M1_NO, f"O{u}")
                o = qo[:, b, heads[0] * HD_A:(heads[-1] + 1) * HD_A].rearrange("p (n d) -> p n d", d=HD_A)
                nc.vector.tensor_tensor(o, M1[:, 0:n * HD_A].rearrange("p (n d) -> p n d", d=HD_A),
                                        rinv[:, b, hs].unsqueeze(2).to_broadcast([P, n, HD_A]), ALU.mult).then_inc(m1_read, 1)

            def gate_b(c):
                wait_read(dve, ("in0", E_GB + c))
                wait_use(dve, m1_read, M1_NO, "mix3")
                ub = u_b[:, :, c * COLS:(c + 1) * COLS]
                nc.vector.tensor_tensor(ub, ub, sg0, ALU.mult).then_inc(y_gated, 1)

            def even(i, s):
                at = SLOTS * i + s
                if at == AT_P0 + 2:
                    split_T("p0")
                if at == AT_SPATIAL + 2:
                    wait_use(dve, t_full, T_NO, "wsp")
                    for j in range(2):
                        last = nc.vector.tensor_copy(flat(wT[:, 4 * j:4 * j + 4, :]), T[j][:])
                    last.then_inc(t_read, 1)
                    dve.wait_ge(lb_exps, 1)
                    link(nc.vector.tensor_tensor(lb_sum, lb_a, lb_b, ALU.add))
                    link(nc.vector.reciprocal(lb_sum, lb_sum))
                    link(nc.vector.tensor_tensor(lb, lb_b, lb_sum, ALU.mult))
                    link(nc.vector.tensor_scalar(omlb, lb, -1.0, 1.0, ALU.mult, ALU.add))
                    dve.wait_ge(sink_in, 16)
                    link(nc.vector.tensor_scalar(nsink[:], nsink[:], -1.0, None, ALU.mult))
                    dve.wait_ge(masks_made, 1)
                if at == AT_K - 1:
                    wait_read(dve, ("in0", E_KV))
                    dve.wait_ge(kpad_zero, 1)
                    for g in range(KV_A):
                        for z in range(2):
                            last = nc.vector.tensor_copy(kpad[:, :, g, z, z * HD_A:(z + 1) * HD_A],
                                                         kv[:, :, g * HD_A:(g + 1) * HD_A])
                    last.then_inc(kpad_made, 1)
                for u in range(len(UNITS)):
                    if at == AT_SCORES + 2 * u + 2:
                        shift_scores(u)
                    if at == AT_VALUES + 2 * u + 2:
                        attention_out(u)
                for c in range(2):
                    if at == AT_YA - 1 + c:
                        dve.wait_ge(ga_made, c + 1)
                        wait_use(dve, m1_read, M1_NO, f"O{len(UNITS) - 1}")
                        q = qo[:, :, c * COLS:(c + 1) * COLS]
                        nc.vector.tensor_tensor(q, q, ga[:, :, c * COLS:(c + 1) * COLS], ALU.mult).then_inc(y_gated, 1)
                    if at == AT_YA + 3 * c + 2:
                        split_T(f"ya{c}")
                if at == AT_MIX - 3:
                    row_mean("V")
                if at == AT_MIX - 1:
                    wait_rstd(dve, "V")
                    dve.wait_ge(vgain_in, 16)
                    for t in range(TILES):
                        nc.vector.scalar_tensor_tensor(out=v_b[:, t, :], in0=v_b[:, t, :], scalar=rstd[:, STAT_NO["V"], t:t + 1],
                                                       in1=vgain, op0=ALU.mult, op1=ALU.mult).then_inc(v_normed, 1)
                for m in range(4):
                    if at == AT_MIX + m + 2:
                        wait_use(dve, m1_full, M1_NO, f"mix{m}")
                        t, half = m // 2, m % 2
                        for g in range(4 * half, 4 * half + 4):
                            ub = u_b[:, t, g * P:(g + 1) * P]
                            last = nc.vector.scalar_tensor_tensor(
                                out=ub, in0=M1[:, (g % 4) * P:(g % 4 + 1) * P], scalar=cols[:, C_BSP + g:C_BSP + g + 1],
                                in1=ub, op0=ALU.add, op1=ALU.mult)
                        last.then_inc(m1_read, 1)
                if at == AT_YB - 1:
                    gate_b(0)
                if at == AT_YB + 2:
                    split_T("yb0")

            def read_embed(layer, i):
                c = (f"e{layer}", i)
                wait_chunk(dve, c)
                for t in range(TILES):
                    last = nc.vector.tensor_copy(e[:, t, i * COLS:(i + 1) * COLS], acc[NUMBER[c] % 2][t][:])
                last.then_inc(acc_read[NUMBER[c] % 2], 1)

            def read_outproj(layer, i):
                c = (f"out{layer}", i)
                wait_chunk(dve, c)
                for t in range(TILES):
                    ht = h[:, t, i * COLS:(i + 1) * COLS]
                    last = nc.vector.tensor_tensor(ht, acc[NUMBER[c] % 2][t][:], ht, ALU.add)
                last.then_inc(acc_read[NUMBER[c] % 2], 1)

            def scale_embed(layer, i):
                if i == 0:
                    row_mean(f"E{layer}")
                    wait_rstd(dve, f"E{layer}")
                    dve.wait_ge(gain_in, 16 * (layer + 1))
                for t in range(TILES):
                    et = e[:, t, i * COLS:(i + 1) * COLS]
                    last = nc.vector.scalar_tensor_tensor(out=et, in0=et, scalar=rstd[:, STAT_NO[f"E{layer}"], t:t + 1],
                                                          in1=gbc[:, i * COLS:(i + 1) * COLS], op0=ALU.mult, op1=ALU.mult)
                last.then_inc(e_scaled, 1)

            def apply_gate(layer, i):
                c = (f"gate{layer}", i)
                n = CHUNKS * layer + i
                wait_read(dve, c)
                dve.wait_ge(e_scaled, n + 1)
                g, cs = sgate[n % 2], slice(i * COLS, (i + 1) * COLS)
                link(nc.vector.tensor_tensor(g, g, e[:, :, cs], ALU.mult))
                nc.vector.tensor_tensor(h[:, :, cs], h[:, :, cs], g, ALU.add).then_inc(h_gated, 1)
                if layer:
                    gain_h(i)

            def gain_h(i):
                if i == 0:
                    dve.wait_ge(gain_in, 48)
                dve.wait_ge(h_gated, CHUNKS + i + 1)
                for t in range(TILES):
                    cs = slice(i * COLS, (i + 1) * COLS)
                    nc.vector.tensor_tensor(e[:, t, cs], h[:, t, cs], gbc[:, cs], ALU.mult).then_inc(h_gained, 1)

            def select(n, i):
                m = LEVELS[i]
                wait_use(dve, m0_full, M0_NO, f"A{n}{i}")
                nb = P // (2 * m)
                dst = ATd[:, 8 * n:8 * n + 8, :].rearrange("p j (b z m) -> p j b z m", z=2, m=m)[:, :, :, 1, :]
                mask = lmask[:, i - 1, :].bitcast(I32).rearrange("p (b m) -> p b m", m=m).unsqueeze(1).to_broadcast([P, 8, nb, m])
                nc.vector.copy_predicated(dst, mask, M0[:].rearrange("p (j b m) -> p j b m", j=8, m=m)).then_inc(m0_read, 1)

            def select_diagonal(n, half):
                wait_use(dve, m0_full, M0_NO, f"A{n}d{half}")
                dve.wait_ge(scores_zero, 1)
                mask = ident[:].bitcast(I32).unsqueeze(1).to_broadcast([P, 4, P])
                nc.vector.copy_predicated(ATd[:, 8 * n + 4 * half:8 * n + 4 * half + 4, :], mask,
                                          M0[:].rearrange("p (j b) -> p j b", j=4)).then_inc(m0_read, 1)

            def sum_decays(n):
                for j in range(8):
                    last = nc.vector.tensor_tensor_scan(flat(gg)[:, j * P:(j + 1) * P], ones[:], lv[:, 0, j * P:(j + 1) * P],
                                                        0.0, ALU.mult, ALU.add)
                last.then_inc(lv_sub, 1)
                dve.wait_ge(lv_sub, n * len(LEVELS) + 1)

            def exponents(n, i):
                m = LEVELS[i]
                g, X = level_views(flat(gg), m), level_views(level_buf[i % 4], m)
                ref = g[:, :, 0, m - 1:m].to_broadcast([P, g.shape[1], m])
                nc.vector.tensor_tensor(X[:, :, 0, :], ref, g[:, :, 0, :], ALU.subtract)
                nc.vector.tensor_tensor(X[:, :, 1, :], g[:, :, 1, :], ref, ALU.subtract).then_inc(lv_sub, 1)

            def gate_o(i):
                t, col = i % 2, (i // 2) * COLS
                bank, full, read, number = av_bank(i)
                n_heads, dv, first = av_heads(i)
                wait_use(dve, full, number, f"AV{i}")
                dve.wait_ge(o_rstd, i + 1)
                for j in range(n_heads):
                    o = O[:, t, col + j * dv:col + (j + 1) * dv]
                    last = nc.vector.scalar_tensor_tensor(out=o, in0=bank[:, j * dv:(j + 1) * dv],
                                                          scalar=orstd[:, t, first + j:first + j + 1], in1=o,
                                                          op0=ALU.mult, op1=ALU.mult)
                last.then_inc(read, 1)

            def odd(i, s):
                at = SLOTS * i + s
                if at == 2:
                    apply_gate(0, 3)
                if at == 4:
                    split_T("gate03")
                    row_mean("H1")
                if at == AT_P1 + 2:
                    split_T("p1")
                for n in range(GROUPS_LA):
                    b = group_start(n)
                    if at == b + G_F + 2 and n < 2:
                        wait_use(dve, t_read, T_NO, f"f{n}")
                        f = lv[:, 1, :]
                        for hd in range(4):
                            hc = 4 * n + hd
                            last = nc.vector.tensor_scalar(f[:, hd * SEQ:(hd + 1) * SEQ], lv[:, 0, hd * SEQ:(hd + 1) * SEQ],
                                                           omlb[:, hc:hc + 1], lb[:, hc:hc + 1], ALU.mult, ALU.add)
                        link(last)
                        link(nc.vector.tensor_scalar(flat(gk), f, -1.0, 1.0, ALU.mult, ALU.add))
                        nc.vector.tensor_scalar(f, f, LN_LEAST, None, ALU.max).then_inc(f_made, 1)
                    if at == b + G_F + 2 and n == 2:
                        f = lv[:, 1, :]
                        for half in range(2):
                            dve.wait_ge(abs_made, half + 1)
                            for j in range(2):
                                hd = 2 * half + j
                                last = nc.vector.tensor_scalar(f[:, hd * SEQ:(hd + 1) * SEQ], M1[:, j * SEQ:(j + 1) * SEQ],
                                                               cols[:, C_BG + hd:C_BG + hd + 1], 0.0, ALU.add, ALU.min)
                            last.then_inc(m1_read, 1)
                    if at == b + G_F + 4:
                        if n == 2:
                            f = lv[:, 1, :]
                            wait_use(dve, m1_read, M1_NO, "up1")
                            dve.wait_ge(ln_made, 3)
                            link(nc.vector.tensor_tensor(lv[:, 0, :], f, lv[:, 0, :], ALU.subtract))
                            link(nc.vector.tensor_scalar(lv[:, 0, :], lv[:, 0, :], 1.0 / 16.0, None, ALU.mult))
                        else:
                            dve.wait_ge(ln_made, n + 1)
                        sum_decays(n)
                    for half in range(2):
                        if at == b + G_DIAG + half + 2:
                            select_diagonal(n, half)
                    for j in range(1, len(LEVELS)):
                        if at == b + G_LEVEL + 2 * j - 3:
                            exponents(n, j)
                        if at == b + G_LEVEL + 2 * j + 2:
                            select(n, j)
                for j in range(5):
                    if at == av_place(j) + 3:
                        gate_o(j)
                for c in range(2):
                    if at == AT_YO + SLOTS * c + 2:
                        split_T(f"yo{c}")

            def embed_and_out(layer, last_of_in):
                for i in range(CHUNKS):
                    split_w((f"e{layer}", i), 0)
                    if i == 1:
                        last_of_in()
                read_embed(layer, 0)
                read_embed(layer, 1)
                for c in range(CHUNKS):
                    for s in range(SLOTS):
                        split_w((f"out{layer}", c), s)
                        if c:
                            if s == 1:
                                read_outproj(layer, c - 1)
                            if s == 4:
                                split_T(f"out{layer}{c - 1}")
                            if s == 6:
                                scale_embed(layer, c - 1)
                        else:
                            if s == 0:
                                read_embed(layer, 2)
                                read_embed(layer, 3)
                            if layer and s == 0:
                                split_T("yo2")
                            if layer and s in (1, 2):
                                gate_o(5 + s)
                            if s == (5 if layer else 2):
                                split_T("yo3" if layer else "yb1")
                scale_embed(layer, 3)

            def gate_phase(layer):
                for c in range(CHUNKS):
                    for s in range(SLOTS):
                        split_w((f"gate{layer}", c), s)
                        if s == 1 and c == 0:
                            read_outproj(layer, 3)
                        if s == 4 and c == 0:
                            split_T(f"out{layer}3")
                            row_mean(f"H{2 * layer}")
                        if s == 2 and c:
                            apply_gate(layer, c - 1)
                        if s == 4 and c and layer == 0:
                            split_T(f"gate0{c - 1}")

            nc.vector.memset(small[:], 0.0).then_inc(small_zero, 1)
            dve.wait_ge(small_zero, 1)
            link(nc.vector.memset(mhalf, -0.5))
            dve.wait_ge(cols_full, 1)
            link(nc.vector.tensor_copy(cols[:], acc[0][0][:, 0:N_ROWS]))
            link(nc.vector.tensor_tensor(lb_max, cols[:, C_LB:C_LB + 8], cols[:, C_LB + 8:C_LB + 16], ALU.max))
            nc.vector.tensor_tensor(lb_a, cols[:, C_LB:C_LB + 8], lb_max, ALU.subtract).then_inc(cols_made, 1)
            nc.vector.tensor_tensor(lb_b, cols[:, C_LB + 8:C_LB + 16], lb_max, ALU.subtract).then_inc(lb_shifted, 1)
            for s in range(RING):
                split_w(PLAN[0], s)
            for c in range(CHUNKS):
                split_T(f"x{c}")
            row_mean("X")
            for i in range(len(EVEN_IN)):
                for s in range(SLOTS):
                    if i or s >= RING:
                        split_w(("in0", i), s)
                    even(i, s)
            embed_and_out(0, lambda: gate_b(1))
            gate_phase(0)
            for i in range(len(ODD_IN)):
                for s in range(SLOTS):
                    split_w(("in1", i), s)
                    odd(i, s)
            embed_and_out(1, lambda: gate_o(5))
            gate_phase(1)
            apply_gate(1, 3)
            row_mean("H3")
            wait_rstd(dve, "H3")
            dve.wait_ge(h_gained, TILES * CHUNKS)
            for half in range(2):
                o = e[:, 0, half * 1024:(half + 1) * 1024]
                nc.vector.tensor_scalar(o, o, rstd[:, STAT_NO["H3"], 0:1], None, ALU.mult).then_inc(normed[0], 1)

        @block.gpsimd
        def _(pool):
            steps = [0]

            def link(ins):
                steps[0] += 1
                ins.then_inc(pool_step, 1)
                pool.wait_ge(pool_step, steps[0])

            def keep(a, pattern, base, per_partition, fill, op=ALU.is_ge):
                return nc.gpsimd.affine_select(out=a, in_=a, pattern=pattern, compare_op=op, fill=fill, base=base,
                                               channel_multiplier=per_partition)

            def root(name):
                i = STAT_NO[name]
                pool.wait_ge(mean_made, i + 1)
                link(nc.gpsimd.tensor_scalar(var[:, i, :], mean[:, i, :], 1.0 / STATS[i][2], EPS, ALU.mult, ALU.add))
                nc.gpsimd.tensor_tensor(rstd[:, i, :], var[:, i, :], mhalf[:, 0:TILES], ALU.pow).then_inc(rstd_made, 1)

            link(nc.gpsimd.memset(ident[:], 0.0))
            keep(ident[:], [[-1, P]], 0, 1, 1.0, ALU.not_equal).then_inc(ident_made, 1)
            nc.gpsimd.memset(kpad, 0.0).then_inc(kpad_zero, 1)
            link(nc.gpsimd.memset(band[:], 0.0))
            link(keep(band[:, 0, :], [[1, P]], -1, -1, NEG_INF))
            link(keep(band[:, 1, :], [[-1, P]], 0, 1, NEG_INF))
            link(nc.gpsimd.memset(lmask[:], 1.0))
            for i, m in enumerate(LEVELS[1:]):
                v, nb = lmask[:, i, :], P // (2 * m)
                link(keep(v, [[-2 * m, nb], [0, m]], 0, 1, 0.0))
                link(keep(v, [[2 * m, nb], [0, m]], m - 1, -1, 0.0))
            nc.gpsimd.memset(ones[:], 1.0).then_inc(masks_made, 1)
            root("X")
            wait_use(pool, t_read, T_NO, "wsp")
            nc.gpsimd.affine_select(out=wT, in_=wT, pattern=[[0, GROUPS_B], [1, P]], compare_op=ALU.is_ge, fill=0.0, base=0,
                                    channel_multiplier=-1).then_inc(spatial_masked, 1)
            for name in ("V", "E0", "H0"):
                root(name)
            wait_use(pool, t_full, T_NO, "yb1")
            nc.gpsimd.memset(ATd, 0.0).then_inc(scores_zero, 1)
            root("H1")
            for n in range(GROUPS_LA):
                for i, m in enumerate(LEVELS):
                    pool.wait_ge(lv_exp, n * len(LEVELS) + i + 1)
                    X, k, q = (level_views(a, m) for a in (level_buf[i % 4], flat(gk), flat(gq)))
                    nc.gpsimd.tensor_tensor(X[:, :, 0, :], X[:, :, 0, :], k[:, :, 0, :], ALU.mult)
                    nc.gpsimd.tensor_tensor(X[:, :, 1, :], X[:, :, 1, :], q[:, :, 1, :], ALU.mult).then_inc(lv_mul, 1)
            for i in range(8):
                n_heads, dv, first = av_heads(i)
                pool.wait_ge(o_squares, sum(av_heads(j)[0] for j in range(i + 1)))
                hs = slice(first, first + n_heads)
                link(nc.gpsimd.tensor_scalar(ovar[:, i % 2, hs], oms[:, i % 2, hs], 1.0 / dv, EPS, ALU.mult, ALU.add))
                nc.gpsimd.tensor_tensor(orstd[:, i % 2, hs], ovar[:, i % 2, hs], mhalf[:, 0:n_heads], ALU.pow).then_inc(o_rstd, 1)
            for name in ("E1", "H2", "H3"):
                root(name)


_INS = ["x", "p", "norm_mix", "w_in_even", "sinks_a", "vnorm_b", "w_spatial_b", "b_spatial_b", "w_out_even",
        "w_in_odd", "lower_bounds_c", "onorm_c", "w_gate_up_d", "b_gate_d", "onorm_d", "w_out_odd",
        "w_ple_proj", "ple_norm", "ple_gate_norm", "w_ple_gate", "final_norm"]


def kernel(**inputs):
    import numpy as np
    import concourse.bacc as bacc
    from concourse.bass_utils import run_bass_kernel_spmd

    nc = bacc.Bacc("TRN2", target_bir_lowering=False, num_devices=1, dynamic_dma_scratch_size=1024)
    arrays, args = {}, []
    for name in _INS:
        a = np.ascontiguousarray(inputs[name])
        arrays[f"in_{name}"] = a
        args.append(nc.dram_tensor(f"in_{name}", a.shape, mybir.dt.from_np(a.dtype), kind="ExternalInput").ap())
    out = nc.dram_tensor("out", (1, SEQ, D_MODEL), F32, kind="ExternalOutput").ap()
    trunk(nc, *args, out)
    return run_bass_kernel_spmd(nc, [arrays], core_ids=[0]).results[0]["out"]
```

```python
from contextlib import ExitStack

import concourse.bass as bass
from concourse import mybir

P = 128
F32 = mybir.dt.float32
F32R = mybir.dt.float32r
I32 = mybir.dt.int32
ALU = mybir.AluOpType
ACT = mybir.ActivationFunctionType
AX = mybir.AxisListType
EPS = 1e-6
NEG_INF = -1e30

D_MODEL = 2048
SEQ = 256
TILES = SEQ // P
KT = D_MODEL // P
COLS = 512
K_PER_SLOT = 2
SLOTS = KT // K_PER_SLOT
RING = 4
CHUNKS = D_MODEL // COLS
PLE = 256
HEADS_A, KV_A, HD_A = 16, 2, 64
GROUPS_B = 8
WIDTH_B = D_MODEL // 2
LEVELS = (128, 64, 32, 16, 8, 4, 2, 1)
SCALE_LA = float(P) ** -0.5
LN_LEAST = 2.0 ** -63

EVEN_IN = [(1024, 256), (0, 512), (512, 512)] + [(1280 + 512 * i, 512) for i in range(8)]
E_KV, E_Q, E_GA, E_U, E_VB, E_GB = 0, 1, 3, 5, 7, 9
E_WIDE = E_GA
ODD_IN = [(0, 512), (1024, 512), (3072, 512), (512, 512), (1536, 512), (3584, 512), (6144, 352), (4096, 512), (4608, 512),
          (6496, 344), (6840, 344), (2048, 512), (2560, 512), (5120, 512), (5632, 512)]
GLR = 16
O_Q, O_F, O_GATES, O_GLR, O_V = (0, 3, 7), (1, 4, 8), {2: 0, 5: 512, 6: 1024, 9: 1360, 10: 1704}, 6, 11
GROUPS_LA = 3

C_MIX, C_GATE, C_ONORM = 0, 2 * KT, 4 * KT
C_BSP = C_ONORM + KT
C_LB = C_BSP + GROUPS_B
C_BG = C_LB + 16
N_ROWS = C_BG + 4

PLAN = ([("in0", i) for i in range(len(EVEN_IN))] + [("e0", i) for i in range(CHUNKS)]
        + [("out0", i) for i in range(CHUNKS)] + [("gate0", i) for i in range(CHUNKS)]
        + [("in1", i) for i in range(len(ODD_IN))]
        + [("e1", i) for i in range(CHUNKS)] + [("out1", i) for i in range(CHUNKS)]
        + [("gate1", i) for i in range(CHUNKS)])
NUMBER = {c: n for n, c in enumerate(PLAN)}


def slots_of(c):
    return 1 if c[0] in ("e0", "e1") else SLOTS


FIRST_SLOT = {c: sum(slots_of(d) for d in PLAN[:n]) for n, c in enumerate(PLAN)}

UNITS = ([(0, list(range(4 * u, 4 * u + 4))) for u in range(HEADS_A // 4)]
         + [(1, list(range(2 * u, 2 * u + 2))) for u in range(HEADS_A // 2)])

T_USES = (["x0", "x3", "cols", "k", "p0", "wsp", "q0", "q1"] + [f"P{u}" for u in range(len(UNITS))]
          + ["ya0", "ya1", "yb0", "yb1"] + [f"out0{c}" for c in range(CHUNKS)] + [f"gate0{c}" for c in range(CHUNKS)]
          + ["p1", "f0", "g0", "f1", "g1", "glr", "f2", "g2"] + [f"yo{c}" for c in range(CHUNKS)]
          + [f"out1{c}" for c in range(CHUNKS)])
SCORES = ["d0", "d1", *range(len(LEVELS))]
M0_USES = ([f"S{u}" for u in range(len(UNITS))] + [f"A{n}{a}" for n in range(GROUPS_LA) for a in SCORES[0::2]]
           + [f"AV{i}" for i in (1, 3, 5, 7)])
M1_USES = ([f"O{u}" for u in range(len(UNITS))] + [f"mix{i}" for i in range(4)]
           + [f"A{n}{a}" for n in range(GROUPS_LA - 1) for a in SCORES[1::2]] + ["up0", "up1"]
           + [f"A{GROUPS_LA - 1}{a}" for a in SCORES[1::2]] + [f"AV{i}" for i in (0, 2, 4, 6)])
T_NO, M0_NO, M1_NO = ({u: i for i, u in enumerate(x)} for x in (T_USES, M0_USES, M1_USES))

SPLITS = {**{f"x{c}": (0, 4 * c, C_MIX + 4 * c) for c in range(CHUNKS)}, "p0": ("p", 0, None),
          "ya0": (1, 0, None), "ya1": (1, 4, None), "yb0": (1, 8, None), "yb1": (1, 12, None),
          **{f"out0{c}": (0, 4 * c, C_GATE + 4 * c) for c in range(CHUNKS)},
          **{f"gate0{c}": (1, 4 * c, C_MIX + KT + 4 * c) for c in range(CHUNKS)},
          "p1": ("p", 0, None), **{f"yo{c}": (0, 4 * c, C_ONORM + 4 * c) for c in range(CHUNKS)},
          **{f"out1{c}": (1, 4 * c, C_GATE + KT + 4 * c) for c in range(CHUNKS)}}
SPLIT_NO = {u: i for i, u in enumerate(["x0", "x1", "x2"] + [u for u in T_USES[1:] if u in SPLITS])}

STATS = [("X", 2, D_MODEL), ("V", 4, WIDTH_B), ("E0", 8, D_MODEL), ("H0", 8, D_MODEL), ("H1", 8, D_MODEL),
         ("E1", 8, D_MODEL), ("H2", 8, D_MODEL), ("H3", 8, D_MODEL)]
STAT_NO = {s[0]: i for i, s in enumerate(STATS)}

AT_K, AT_Q, AT_SCORES, AT_TURN, AT_VALUES = 10, 18, 29, 32, 34
AT_YA, AT_MIX, AT_YB = 62, 78, 85
SLOTS_PER_X = SLOTS // CHUNKS
AT_COLS, AT_P0, AT_SPATIAL = 7, 12, 14
AT_P1, AT_GLR, AT_AV, AT_YO = 5, 59, 99, 104
G_F, G_Q, G_DIAG, G_SUMS, G_LEVEL = 1, 4, 7, (5, 5, 7), (10, 10, 12)


def group_start(n):
    return SLOTS * (O_F[n] + 1) + 1


def av_place(i):
    return AT_AV + SLOTS * (i // 2) + 2 * (i % 2)


def av_heads(i):
    c = i // 2
    return (4, P, 4 * c) if c < 2 else (2, 2 * P, 8 + 2 * (c - 2))


def trunk(nc, x, p, norm_mix, w_in_even, sinks_a, vnorm_b, w_spatial_b, b_spatial_b, w_out_even,
          w_in_odd, lower_bounds_c, onorm_c, w_gate_up_d, b_gate_d, onorm_d, w_out_odd,
          w_ple_proj, ple_norm, ple_gate_norm, w_ple_gate, final_norm, out):
    with ExitStack() as ctx:
        def sb(name, shape, dt=F32):
            return ctx.enter_context(nc.sbuf_tensor(name, shape, dt))

        def sem(name):
            return ctx.enter_context(nc.semaphore(name))

        raw = sb("raw", [P, RING, K_PER_SLOT * COLS])
        whi = sb("whi", [P, RING, K_PER_SLOT * COLS], F32R)
        wlo = sb("wlo", [P, RING, K_PER_SLOT * COLS], F32R)
        h = sb("h", [P, TILES, D_MODEL])
        bhi = [sb(f"bhi{i}", [P, KT, SEQ], F32R) for i in range(2)]
        blo = [sb(f"blo{i}", [P, KT, SEQ], F32R) for i in range(2)]
        phi = sb("phi", [P, PLE // P, SEQ], F32R)
        plo = sb("plo", [P, PLE // P, SEQ], F32R)
        e = sb("e", [P, TILES, D_MODEL])
        ident = sb("ident", [P, P])
        ones = sb("ones", [P, P])
        cols = sb("cols", [P, N_ROWS])
        band = sb("band", [P, 2, P])
        lmask = sb("lmask", [P, len(LEVELS) - 1, P // 2])
        nsink = sb("nsink", [P, HEADS_A])
        small = sb("small", [P, 512])
        glrT = sb("glrT", [GLR, SEQ])
        glr = sb("glr_z", [P, TILES, GLR])
        junk = sb("junk", [P, COLS])
        upw = sb("upw", [GLR, 4 * P])
        WORK = 15872
        work = sb("work", [P, WORK])

        def flat(a):
            return a.rearrange("p a b -> p (a b)")

        def part(first, a, b):
            return work[:, first:first + a * b].rearrange("p (a b) -> p a b", b=b)

        qo = part(0, TILES, 1024)
        qT = part(2048, 8, SEQ)
        kv = part(4096, TILES, 256)
        kT = work[:, 4608:5632].rearrange("p (g z n) -> p g z n", g=KV_A, z=2)
        Pm = part(5632, 2, COLS)
        PT = part(6656, 2, COLS)
        ga = part(7680, TILES, 1024)
        u_b = part(9728, TILES, 1024)
        v_b = part(11776, TILES, 1024)
        vgain = work[:, 13824:14848]
        wT = part(14848, GROUPS_B, P)
        kpad = work[:, 6656:7680].rearrange("p (t g z d) -> p t g z d", t=TILES, g=KV_A, z=2)
        rows = work[0:N_ROWS, 7680:7680 + P]
        level_buf = [flat(e)[:, 1024 * i:1024 * (i + 1)] for i in range(4)]
        wsp = part(11776, GROUPS_B, P)
        pin0 = part(5632, TILES, PLE)
        sg0 = part(2048, TILES, COLS)
        zq = part(0, TILES, COLS)
        zf = part(1024, TILES, COLS)
        gq = part(2048, 4, SEQ)
        gk = part(3072, 4, SEQ)
        gg = part(4096, 4, SEQ)
        lv = part(5120, 2, 1024)
        ATd = part(7168, 24, P)
        ATx = part(10240, 12, P)
        O = part(11776, TILES, D_MODEL)
        pin1 = part(0, TILES, PLE)
        sgate = [part(5120 + 1024 * i, TILES, COLS) for i in range(2)]
        gbc = work[:, 13824:15872]

        ms = small[:, 0:64].rearrange("p (r t c) -> p r t c", r=8, t=2)
        mean = small[:, 64:80].rearrange("p (r t) -> p r t", r=8)
        var = small[:, 80:96].rearrange("p (r t) -> p r t", r=8)
        rstd = small[:, 96:112].rearrange("p (r t) -> p r t", r=8)

        def heads_of(first, n):
            return small[:, first:first + 2 * n].rearrange("p (t h) -> p t h", t=2)

        mhalf = small[:, 112:136]
        nmax, dsink, esink, psumr, rinv = (heads_of(136 + 32 * i, HEADS_A) for i in range(5))
        oms, ovar, orstd = (heads_of(296 + 24 * i, 12) for i in range(3))
        lb_max, lb_a, lb_b, lb_sum, lb, omlb = (small[:, 368 + 8 * i:376 + 8 * i] for i in range(6))

        acc = [[ctx.enter_context(nc.psum_tensor(f"acc{a}{t}", [P, COLS], F32)) for t in range(2)] for a in range(2)]
        T = [ctx.enter_context(nc.psum_tensor(f"T{i}", [P, COLS], F32)) for i in range(2)]
        M0 = ctx.enter_context(nc.psum_tensor("M0", [P, COLS], F32))
        M1 = ctx.enter_context(nc.psum_tensor("M1", [P, COLS], F32))

        landed = [sem(f"landed{i}") for i in range(RING)]
        hi_made, lo_made, slot_used = sem("hi_made"), sem("lo_made"), sem("slot_used")
        acc_read = [sem("acc_read0"), sem("acc_read1")]
        t_full, t_read, t_hi, x_turned, x_split = (sem(n) for n in ("t_full", "t_read", "t_hi", "x_turned", "x_split"))
        m0_full, m0_read, m1_full, m1_read = sem("m0_full"), sem("m0_read"), sem("m1_full"), sem("m1_read")
        x_in = [sem(f"x_in{i}") for i in range(CHUNKS)]
        first_rows_in, rows_in, wsp_in, p_in, sink_in, vgain_in, up_in, gain_in, stored = (
            sem(n) for n in ("first_rows_in", "rows_in", "wsp_in", "p_in", "sink_in", "vgain_in", "up_in", "gain_in", "stored"))
        small_zero, ident_made, masks_made, kpad_zero, scores_zero = (
            sem(n) for n in ("small_zero", "ident_made", "masks_made", "kpad_zero", "scores_zero"))
        cols_full, cols_made, spatial_masked, lb_shifted, lb_exps = (
            sem(n) for n in ("cols_full", "cols_made", "spatial_masked", "lb_shifted", "lb_exps"))
        squares, mean_made, rstd_made = sem("squares"), sem("mean_made"), sem("rstd_made")
        kpad_made, scores_shifted, probs_made, ga_made, y_gated, v_normed = (
            sem(n) for n in ("kpad_made", "scores_shifted", "probs_made", "ga_made", "y_gated", "v_normed"))
        f_made, ln_made, abs_made, lv_sub, lv_exp, lv_mul, o_squares, o_rstd = (
            sem(n) for n in ("f_made", "ln_made", "abs_made", "lv_sub", "lv_exp", "lv_mul",
                             "o_squares", "o_rstd"))
        e_scaled, h_gated, h_gained, tile_full, tile_gates, tile_gated = (
            sem(n) for n in ("e_scaled", "h_gated", "h_gained", "tile_full", "tile_gates", "tile_gated"))
        normed = [sem("normed0"), sem("normed1")]
        dve_step, act_step, pool_step = sem("dve_step"), sem("act_step"), sem("pool_step")

        def matrix(c):
            phase, i = c
            if phase[:-1] == "in":
                layer = int(phase[-1])
                return (w_in_even, w_in_odd)[layer][0], (EVEN_IN, ODD_IN)[layer][i][0]
            return {"e0": w_ple_proj[0], "e1": w_ple_proj[1], "out0": w_out_even[0], "out1": w_out_odd[0],
                    "gate0": w_ple_gate[0], "gate1": w_ple_gate[1]}[phase], i * COLS

        def width(c):
            return EVEN_IN[c[1]][1] if c[0] == "in0" else ODD_IN[c[1]][1] if c[0] == "in1" else COLS

        def source(c, s):
            (w, c0), n = matrix(c), width(c)
            r0 = s * K_PER_SLOT * P
            return w[r0:r0 + K_PER_SLOT * P, c0:c0 + n].rearrange("(k p) n -> p k n", p=P)

        def slot_view(ring, c, s):
            n = width(c)
            r = (FIRST_SLOT[c] + s) % RING
            return ring[:, r, 0:K_PER_SLOT * n].rearrange("p (k n) -> p k n", n=n)

        def wait_chunk(eng, c):
            eng.wait_ge(slot_used, FIRST_SLOT[c] + slots_of(c))

        def wait_read(eng, c):
            eng.wait_ge(acc_read[NUMBER[c] % 2], NUMBER[c] // 2 + 1)

        def wait_use(eng, s, table, name):
            eng.wait_ge(s, table[name] + 1)

        def wait_rstd(eng, name):
            eng.wait_ge(rstd_made, STAT_NO[name] + 1)

        banks = {"x1": (M0, M1), "x2": acc[1]}

        def av_bank(i):
            return (M1, m1_full, m1_read, M1_NO) if i % 2 == 0 else (M0, m0_full, m0_read, M0_NO)

        def score_bank(a):
            return (M1, m1_full, m1_read, M1_NO) if SCORES.index(a) % 2 else (M0, m0_full, m0_read, M0_NO)

        def level_views(a, m):
            return a.rearrange("p (b z m) -> p b z m", z=2, m=m)

        block = ctx.enter_context(nc.Block())

        @block.sync
        def _(sp):
            def row_load(row, v, signal):
                n = v.shape[0] // P
                sp.dma_start(rows[row:row + n, :], v.rearrange("(r c) -> r c", c=P)).then_inc(signal, 16)
                return row + n

            def weights(c, first=0, end=SLOTS):
                for s in range(first, min(end, slots_of(c))):
                    n = FIRST_SLOT[c] + s
                    if n >= RING:
                        sp.wait_ge(lo_made, n - RING + 1)
                    sp.dma_start(slot_view(raw, c, s), source(c, s)).then_inc(landed[n % RING], 16)

            def weight_chunks(first, count):
                w, c0, n0 = *matrix(first), FIRST_SLOT[first]
                with sp.Fori(0, count) as i:
                    for s in range(SLOTS):
                        r, r0 = (n0 + s) % RING, s * K_PER_SLOT * P
                        sp.wait_ge(lo_made, i * SLOTS + (n0 + s - RING + 1))
                        sp.dma_start(raw[:, r, :].rearrange("p (k n) -> p k n", n=COLS),
                                     w[r0:r0 + K_PER_SLOT * P, bass.ds(i * COLS + c0, COLS)].rearrange("(k p) n -> p k n", p=P)
                                     ).then_inc(landed[r], 16)

            row = row_load(0, norm_mix.rearrange("a b -> (a b)"), first_rows_in)
            for c in range(CHUNKS):
                sp.dma_start(h[:, :, c * COLS:(c + 1) * COLS],
                             x[0, :, c * COLS:(c + 1) * COLS].rearrange("(t p) d -> p t d", p=P)).then_inc(x_in[c], 16)
                if K_PER_SLOT * c < RING:
                    weights(PLAN[0], K_PER_SLOT * c, K_PER_SLOT * (c + 1))
            for v in (ple_gate_norm.rearrange("a b -> (a b)"), onorm_c[0], onorm_d[0],
                      b_spatial_b[0].rearrange("a b -> (a b)"), lower_bounds_c.rearrange("a b -> (a b)"), b_gate_d[0]):
                row = row_load(row, v, rows_in)
            sp.dma_start(pin0, p[0, 0].rearrange("(t p) d -> p t d", p=P)).then_inc(p_in, 16)
            sp.dma_start(wsp, w_spatial_b[0].rearrange("g t s -> t g s")).then_inc(wsp_in, 16)
            sp.dma_start(nsink[:], sinks_a[0].partition_broadcast(P)).then_inc(sink_in, 16)
            sp.dma_start(vgain, vnorm_b[0].partition_broadcast(P)).then_inc(vgain_in, 16)
            weights(PLAN[0], RING)
            for i in range(1, E_WIDE):
                weights(("in0", i))
            weight_chunks(("in0", E_WIDE), len(EVEN_IN) - E_WIDE)
            for i in range(CHUNKS):
                weights(("e0", i))
            weights(("out0", 0))
            wait_use(sp, m1_read, M1_NO, "mix3")
            sp.dma_start(gbc, ple_norm[0].partition_broadcast(P)).then_inc(gain_in, 16)
            sp.dma_start(upw[:], w_gate_up_d[0]).then_inc(up_in, 16)
            wait_use(sp, t_full, T_NO, "ya1")
            sp.dma_start(pin1, p[1, 0].rearrange("(t p) d -> p t d", p=P)).then_inc(p_in, 16)
            weight_chunks(("out0", 1), CHUNKS - 1)
            weight_chunks(("gate0", 0), CHUNKS)
            for i in range(len(ODD_IN)):
                weights(("in1", i))
            for i in range(CHUNKS):
                weights(("e1", i))
            weights(("out1", 0))
            wait_use(sp, t_full, T_NO, "yo3")
            sp.dma_start(gbc, ple_norm[1].partition_broadcast(P)).then_inc(gain_in, 16)
            weight_chunks(("out1", 1), CHUNKS - 1)
            weights(("gate1", 0))
            sp.wait_ge(e_scaled, 2 * CHUNKS)
            sp.dma_start(gbc, final_norm.partition_broadcast(P)).then_inc(gain_in, 16)
            weight_chunks(("gate1", 1), CHUNKS - 1)
            for t in range(TILES):
                for c in range(CHUNKS):
                    sp.wait_ge(normed[c % 2], CHUNKS // 2 * t + c // 2 + 1)
                    cs = slice(c * COLS, (c + 1) * COLS)
                    sp.dma_start(out[0, t * P:(t + 1) * P, cs], e[:, t, cs]).then_inc(stored, 16)
            sp.wait_ge(stored, 16 * CHUNKS * TILES)

        @block.tensor
        def _(pe):
            def take_T(name):
                if T_NO[name]:
                    pe.wait_ge(t_read, T_NO[name])

            def turn(name, src):
                B = banks.get(name, T)
                if B is T:
                    take_T(name)
                for k in range(4):
                    for t in range(TILES):
                        last = nc.tensor.transpose(B[k // 2][:, (k % 2) * SEQ + t * P:(k % 2) * SEQ + (t + 1) * P],
                                                   src[:, t, k * P:(k + 1) * P], ident[:])
                last.then_inc(t_full if B is T else x_turned, 1)

            def turn_x(c):
                pe.wait_ge(x_in[c], 16)
                turn(f"x{c}", h[:, :, c * COLS:(c + 1) * COLS])

            def turn_p(name, src, loads):
                pe.wait_ge(p_in, 16 * loads)
                take_T(name)
                for k in range(PLE // P):
                    for t in range(TILES):
                        last = nc.tensor.transpose(T[0][:, k * SEQ + t * P:k * SEQ + (t + 1) * P],
                                                   src[:, t, k * P:(k + 1) * P], ident[:])
                last.then_inc(t_full, 1)

            def slot(c, s, hi, lo):
                n = FIRST_SLOT[c] + s
                wh, wl = slot_view(whi, c, s), slot_view(wlo, c, s)
                k_n, w = wh.shape[1:]
                pe.wait_ge(lo_made, n + 1)
                for k in range(k_n):
                    first, final = s == 0 and k == 0, s == slots_of(c) - 1 and k == k_n - 1
                    for t in range(TILES):
                        o = acc[NUMBER[c] % 2][t][:, 0:w]
                        xh, xl = (b[:, K_PER_SLOT * s + k, t * P:(t + 1) * P] for b in (hi, lo))
                        nc.tensor.matmul(o, xh, wl[:, k, :], start=first, stop=False)
                        nc.tensor.matmul(o, xl, wh[:, k, :], start=False, stop=False)
                        last = nc.tensor.matmul(o, xh, wh[:, k, :], start=False, stop=final)
                last.then_inc(slot_used, 1)

            def last_slots(c, hi, lo):
                for t in range(TILES):
                    for s in range(SLOTS - RING, SLOTS):
                        wh, wl = slot_view(whi, c, s), slot_view(wlo, c, s)
                        if t == 0:
                            pe.wait_ge(lo_made, FIRST_SLOT[c] + s + 1)
                        for k in range(K_PER_SLOT):
                            final = s == SLOTS - 1 and k == K_PER_SLOT - 1
                            o = acc[NUMBER[c] % 2][t][:]
                            xh, xl = (b[:, K_PER_SLOT * s + k, t * P:(t + 1) * P] for b in (hi, lo))
                            nc.tensor.matmul(o, xh, wl[:, k, :], start=False, stop=False)
                            nc.tensor.matmul(o, xl, wh[:, k, :], start=False, stop=False)
                            last = nc.tensor.matmul(o, xh, wh[:, k, :], start=False, stop=final)
                    last.then_inc(tile_full, 1)

            def chunk(c, buf, late=None, between=lambda s: None):
                if NUMBER[c] >= 2:
                    wait_read(pe, PLAN[NUMBER[c] - 2])
                for s in range(SLOTS - RING if c == PLAN[-1] else SLOTS):
                    if s == SLOTS - 2 and late:
                        wait_use(pe, t_read, T_NO, late)
                    if c == PLAN[0] and s % SLOTS_PER_X == 0:
                        k = s // SLOTS_PER_X
                        if f"x{k}" in T_NO:
                            wait_use(pe, t_read, T_NO, f"x{k}")
                        else:
                            pe.wait_ge(x_split, k)
                    slot(c, s, bhi[buf], blo[buf])
                    between(s)
                if c == PLAN[-1]:
                    last_slots(c, bhi[buf], blo[buf])

            def embed(layer):
                wait_use(pe, t_read, T_NO, f"p{layer}")
                for i in range(CHUNKS):
                    wait_read(pe, PLAN[NUMBER[(f"e{layer}", i)] - 2])
                    slot((f"e{layer}", i), 0, phi, plo)

            def scores(u):
                b, heads = UNITS[u]
                if u == 0:
                    wait_use(pe, t_read, T_NO, "q1")
                else:
                    wait_use(pe, m0_read, M0_NO, f"S{u - 1}")
                nk = P * (b + 1)
                for i, hd in enumerate(heads):
                    last = nc.tensor.matmul(M0[:, i * nk:(i + 1) * nk], qT[:, hd // 2, b * P:(b + 1) * P],
                                            kT[:, hd // 8, hd % 2, 0:nk], start=True, stop=True)
                last.then_inc(m0_full, 1)

            def turn_probs(u):
                pe.wait_ge(probs_made, u + 1)
                take_T(f"P{u}")
                for i in range(4):
                    last = nc.tensor.transpose(T[0][:, i * P:(i + 1) * P], Pm[:, u % 2, i * P:(i + 1) * P], ident[:])
                last.then_inc(t_full, 1)

            def values(u):
                b, heads = UNITS[u]
                wait_use(pe, t_read, T_NO, f"P{u}")
                if u:
                    wait_use(pe, m1_read, M1_NO, f"O{u - 1}")
                for i, hd in enumerate(heads):
                    v0 = P + (hd // 8) * HD_A
                    for j in range(b + 1):
                        q = (i * (b + 1) + j) * P
                        last = nc.tensor.matmul(M1[:, i * HD_A:(i + 1) * HD_A], PT[:, u % 2, q:q + P],
                                                kv[:, j, v0:v0 + HD_A], start=(j == 0), stop=(j == b))
                last.then_inc(m1_full, 1)

            def mix(i):
                t, half = i // 2, i % 2
                pe.wait_ge(m1_read, M1_NO[f"mix{i}"])
                for g in range(4 * half, 4 * half + 4):
                    last = nc.tensor.matmul(M1[:, (g % 4) * P:(g % 4 + 1) * P], wT[:, g, :],
                                            v_b[:, t, g * P:(g + 1) * P], start=True, stop=True)
                last.then_inc(m1_full, 1)

            def even(i, s):
                at = SLOTS * i + s
                if at == 1:
                    turn_x(3)
                if at == AT_COLS:
                    pe.wait_ge(rows_in, 16 * 6)
                    take_T("cols")
                    nc.tensor.transpose(T[0][:, 0:N_ROWS], rows, ident[0:N_ROWS, 0:N_ROWS]).then_inc(t_full, 1)
                if at == AT_P0:
                    turn_p("p0", pin0, 1)
                if at == AT_SPATIAL:
                    pe.wait_ge(wsp_in, 16)
                    take_T("wsp")
                    for g in range(GROUPS_B):
                        last = nc.tensor.transpose(T[g // 4][:, (g % 4) * P:(g % 4 + 1) * P], wsp[:, g, :], ident[:])
                    last.then_inc(t_full, 1)
                if at == AT_K:
                    pe.wait_ge(kpad_made, 1)
                    take_T("k")
                    for g in range(KV_A):
                        for z in range(2):
                            for t in range(TILES):
                                last = nc.tensor.transpose(T[g][:, z * SEQ + t * P:z * SEQ + (t + 1) * P],
                                                           kpad[:, t, g, z, :], ident[:])
                    last.then_inc(t_full, 1)
                for c in range(2):
                    if at == AT_Q + SLOTS * c:
                        wait_read(pe, ("in0", E_Q + c))
                        turn(f"q{c}", qo[:, :, c * COLS:(c + 1) * COLS])
                for u in range(len(UNITS)):
                    if at == AT_SCORES + 2 * u:
                        scores(u)
                    if at == AT_TURN + 2 * u:
                        turn_probs(u)
                    if at == AT_VALUES + 2 * u:
                        values(u)
                for c in range(2):
                    if at == AT_YA + 3 * c:
                        pe.wait_ge(y_gated, c + 1)
                        turn(f"ya{c}", qo[:, :, c * COLS:(c + 1) * COLS])
                for m in range(4):
                    if at == AT_MIX + m:
                        if m == 0:
                            pe.wait_ge(v_normed, TILES)
                            pe.wait_ge(spatial_masked, 1)
                        mix(m)
                if at == AT_YB:
                    pe.wait_ge(y_gated, 3)
                    turn("yb0", u_b[:, :, 0:COLS])

            def level(n, i):
                m, X = LEVELS[i], level_buf[i % 4]
                pe.wait_ge(lv_mul, n * len(LEVELS) + i + 1)
                bank, full, read, number = score_bank(i)
                pe.wait_ge(read, number[f"A{n}{i}"])
                if m == P:
                    for hd in range(4):
                        last = nc.tensor.matmul(bank[:, hd * P:(hd + 1) * P], X[:, hd * SEQ:hd * SEQ + P],
                                                X[:, hd * SEQ + P:(hd + 1) * SEQ], start=True, stop=True)
                else:
                    for j in range(8):
                        Xj = X[:, j * P:(j + 1) * P]
                        last = nc.tensor.matmul(bank[:, j * 64:(j + 1) * 64].rearrange("p (b m) -> p b m", m=m), Xj,
                                                level_views(Xj, m)[:, :, 1, :], start=True, stop=True)
                last.then_inc(full, 1)

            def diagonal(n, half):
                bank, full, read, number = score_bank(f"d{half}")
                pe.wait_ge(read, number[f"A{n}d{half}"])
                for j in range(4):
                    o = (4 * half + j) * P
                    last = nc.tensor.matmul(bank[:, j * P:(j + 1) * P], flat(gk)[:, o:o + P], flat(gq)[:, o:o + P],
                                            start=True, stop=True)
                last.then_inc(full, 1)

            def apply_scores(i):
                c, t = i // 2, i % 2
                bank, full, read, number = av_bank(i)
                n_heads, dv, first = av_heads(i)
                wait_read(pe, ("in1", O_V + c))
                wait_use(pe, m1_read, M1_NO, f"A{first // 4}7")
                pe.wait_ge(read, number[f"AV{i}"])
                v = (zq, zf)[c % 2]
                for j in range(n_heads):
                    o = bank[:, j * dv:(j + 1) * dv]
                    if t:
                        nc.tensor.matmul(o, ATx[:, first + j, :], v[:, 0, j * dv:(j + 1) * dv], start=True, stop=False)
                    last = nc.tensor.matmul(o, ATd[:, 2 * (first + j) + t, :], v[:, t, j * dv:(j + 1) * dv],
                                            start=(t == 0), stop=True)
                last.then_inc(full, 1)

            def turn_o(c):
                wait_use(pe, m0_read, M0_NO, f"AV{2 * c + 1}")
                turn(f"yo{c}", O[:, :, c * COLS:(c + 1) * COLS])

            def odd(i, s):
                at = SLOTS * i + s
                if at == 2:
                    pe.wait_ge(h_gated, CHUNKS)
                    turn("gate03", h[:, :, 3 * COLS:4 * COLS])
                if at == AT_P1:
                    turn_p("p1", pin1, 2)
                for n in range(GROUPS_LA):
                    b = group_start(n)
                    if at == b + G_F:
                        wait_read(pe, ("in1", O_F[n]))
                        turn(f"f{n}", zf)
                    for half in range(2):
                        if at == b + G_F + half and n == 2:
                            if half == 0:
                                pe.wait_ge(up_in, 16)
                            pe.wait_ge(m1_read, M1_NO[f"up{half}"])
                            for j in range(2):
                                hd = 2 * half + j
                                last = nc.tensor.matmul(M1[:, j * SEQ:(j + 1) * SEQ], upw[:, hd * P:(hd + 1) * P],
                                                        glrT[:], start=True, stop=True)
                            last.then_inc(m1_full, 1)
                    if at == b + G_Q:
                        turn(f"g{n}", zq)
                    for j in range(len(LEVELS)):
                        if at == b + G_LEVEL[n] + 2 * j:
                            level(n, j)
                    for half in range(2):
                        if at == b + G_DIAG + half:
                            diagonal(n, half)
                if at == AT_GLR:
                    wait_read(pe, ("in1", O_GLR))
                    take_T("glr")
                    for t in range(TILES):
                        last = nc.tensor.transpose(T[0][0:GLR, t * P:(t + 1) * P], glr[:, t, :], ident[:])
                    last.then_inc(t_full, 1)
                for j in range(6):
                    if at == av_place(j):
                        apply_scores(j)
                for c in range(2):
                    if at == AT_YO + SLOTS * c:
                        turn_o(c)

            def turn_out(layer, c):
                wait_read(pe, (f"out{layer}", c))
                turn(f"out{layer}{c}", h[:, :, c * COLS:(c + 1) * COLS])

            def turn_gate(c):
                pe.wait_ge(h_gated, c + 1)
                turn(f"gate0{c}", h[:, :, c * COLS:(c + 1) * COLS])

            pe.wait_ge(ident_made, 1)
            pe.wait_ge(first_rows_in, 16)
            nc.tensor.transpose(M1[:, 0:C_GATE], rows[0:C_GATE, :], ident[0:C_GATE, 0:C_GATE]).then_inc(cols_full, 1)
            turn_x(0)
            pe.wait_ge(cols_made, 1)
            turn_x(1)
            turn_x(2)
            for i in range(len(EVEN_IN)):
                chunk(("in0", i), 0, between=lambda s: even(i, s))
            embed(0)
            pe.wait_ge(y_gated, 4)
            turn("yb1", u_b[:, :, COLS:2 * COLS])
            for c in range(CHUNKS):
                chunk(("out0", c), 1, late=None if c else "yb1",
                      between=lambda s: turn_out(0, c - 1) if c and s == 2 else None)
            for c in range(CHUNKS):
                chunk(("gate0", c), 0, late=None if c else "out03",
                      between=lambda s: None if s != 2 else turn_gate(c - 1) if c else turn_out(0, 3))
            for i in range(len(ODD_IN)):
                chunk(("in1", i), 1, late=None if i else "gate03", between=lambda s: odd(i, s))
            embed(1)
            turn_o(2)
            apply_scores(6)
            apply_scores(7)
            for c in range(CHUNKS):
                chunk(("out1", c), 0, late=None if c else "yo3",
                      between=lambda s: turn_out(1, c - 1) if c and s == 2 else turn_o(3) if c == 0 and s == 3 else None)
            for c in range(CHUNKS):
                chunk(("gate1", c), 1, late=None if c else "out13",
                      between=lambda s: turn_out(1, 3) if c == 0 and s == 2 else None)

        @block.scalar
        def _(act):
            steps = [0]
            sq_n, o_sq_n = [0], [0]

            def link(ins):
                steps[0] += 1
                ins.then_inc(act_step, 1)
                act.wait_ge(act_step, steps[0])

            def split_w(c, s):
                n = FIRST_SLOT[c] + s
                act.wait_ge(landed[n % RING], 16 * (n // RING + 1))
                if n >= RING:
                    act.wait_ge(slot_used, n - RING + 1)
                nc.scalar.activation(slot_view(whi, c, s), slot_view(raw, c, s), ACT.Copy).then_inc(hi_made, 1)

            def split_T(name):
                buf, k0, gain = SPLITS[name]
                B = banks.get(name, T)
                if B is T:
                    wait_use(act, t_full, T_NO, name)
                else:
                    act.wait_ge(x_turned, ["x1", "x2"].index(name) + 1)
                if gain is None:
                    hi = phi if buf == "p" else bhi[buf]
                    for i in range(1 if buf == "p" else 2):
                        last = nc.scalar.activation(hi[:, k0 + 2 * i:k0 + 2 * i + 2, :].rearrange("p a b -> p (a b)"),
                                                    T[i][:], ACT.Copy)
                else:
                    if gain == C_MIX:
                        act.wait_ge(cols_made, 1)
                    for k in range(4):
                        last = nc.scalar.activation(bhi[buf][:, k0 + k, :], B[k // 2][:, (k % 2) * SEQ:(k % 2 + 1) * SEQ],
                                                    ACT.Copy, scale=cols[:, gain + k:gain + k + 1])
                last.then_inc(t_hi, 1)

            def square(src, dst):
                if sq_n[0]:
                    act.wait_ge(squares, sq_n[0])
                if o_sq_n[0]:
                    act.wait_ge(o_squares, o_sq_n[0])
                sq_n[0] += 1
                nc.scalar.activation(junk[:, 0:src.shape[-1]], src, ACT.Square, accum_out=dst).then_inc(squares, 1)

            def square_chunk(src, stat, c):
                for t in range(TILES):
                    square(src[:, t, c * COLS:(c + 1) * COLS], ms[:, STAT_NO[stat], t, c:c + 1])

            def read_out(c, dst, func, stat):
                wait_chunk(act, c)
                wait_rstd(act, stat)
                for t in range(TILES):
                    last = nc.scalar.activation(dst(t), acc[NUMBER[c] % 2][t][:, 0:dst(t).shape[-1]], func,
                                                scale=rstd[:, STAT_NO[stat], t:t + 1])
                last.then_inc(acc_read[NUMBER[c] % 2], 1)

            def softmax(u):
                b, heads = UNITS[u]
                act.wait_ge(scores_shifted, u + 1)
                nk = P * (b + 1)
                for i, hd in enumerate(heads):
                    s = Pm[:, u % 2, i * nk:(i + 1) * nk]
                    nc.scalar.activation(s, s, ACT.Exp, bias=nmax[:, b, hd:hd + 1], accum_out=psumr[:, b, hd:hd + 1])
                hs = slice(heads[0], heads[-1] + 1)
                nc.scalar.activation(esink[:, b, hs], dsink[:, b, hs], ACT.Exp).then_inc(probs_made, 1)

            def even(i, s):
                at = SLOTS * i + s
                if at in (SLOTS - 1, SLOTS):
                    if at == SLOTS - 1:
                        act.wait_ge(small_zero, 1)
                    t = at - SLOTS + 1
                    nc.scalar.activation(e[:, t, :], h[:, t, :], ACT.Square,
                                         accum_out=ms[:, STAT_NO["X"], t, 0:1]).then_inc(squares, 1)
                    sq_n[0] += 1
                if at == AT_P0 + 2:
                    split_T("p0")
                if at == AT_SPATIAL + 2:
                    act.wait_ge(lb_shifted, 1)
                    nc.scalar.activation(small[:, 376:392], small[:, 376:392], ACT.Exp).then_inc(lb_exps, 1)
                if s == 1 and i:
                    c = i - 1
                    if c == E_KV:
                        read_out(("in0", c), lambda t: kv[:, t, :], ACT.Copy, "X")
                    for first, dst, func in ((E_Q, qo, ACT.Copy), (E_GA, ga, ACT.Copy), (E_U, u_b, ACT.Gelu),
                                             (E_VB, v_b, ACT.Gelu)):
                        if first <= c < first + 2:
                            o = (c - first) * COLS
                            read_out(("in0", c), lambda t: dst[:, t, o:o + COLS], func, "X")
                    if c == E_GB:
                        read_out(("in0", c), lambda t: sg0[:, t, :], ACT.Silu, "X")
                if at == AT_K + 2:
                    wait_use(act, t_full, T_NO, "k")
                    for g in range(KV_A):
                        last = nc.scalar.activation(kT[:, g].rearrange("p z n -> p (z n)"), T[g][:], ACT.Copy)
                    last.then_inc(t_read, 1)
                for c in range(2):
                    if at == AT_Q + SLOTS * c + 2:
                        wait_use(act, t_full, T_NO, f"q{c}")
                        for j in range(2):
                            last = nc.scalar.activation(flat(qT[:, 4 * c + 2 * j:4 * c + 2 * j + 2, :]), T[j][:], ACT.Copy,
                                                        scale=HD_A ** -0.5)
                        last.then_inc(t_read, 1)
                for u in range(len(UNITS)):
                    if at == AT_SCORES + 2 * u + 2:
                        softmax(u)
                    if at == AT_TURN + 2 * u + 2:
                        wait_use(act, t_full, T_NO, f"P{u}")
                        if u >= 2:
                            wait_use(act, m1_full, M1_NO, f"O{u - 2}")
                        nc.scalar.activation(PT[:, u % 2, :], T[0][:], ACT.Copy).then_inc(t_read, 1)
                for c in range(2):
                    if at == AT_YA - 2 + c:
                        g = ga[:, :, c * COLS:(c + 1) * COLS]
                        wait_read(act, ("in0", E_GA + c))
                        nc.scalar.activation(g, g, ACT.Silu).then_inc(ga_made, 1)
                    if at == AT_YA + 3 * c + 2:
                        split_T(f"ya{c}")
                if at == SLOTS * (E_VB + 2) + 2:
                    wait_read(act, ("in0", E_VB + 1))
                    for c in range(2):
                        square_chunk(v_b, "V", c)
                if at == AT_YB + 2:
                    split_T("yb0")

            def read_embed(layer, i):
                wait_read(act, (f"e{layer}", i))
                square_chunk(e, f"E{layer}", i)

            def read_outproj(layer, c):
                wait_read(act, (f"out{layer}", c))
                square_chunk(h, f"H{2 * layer}", c)

            def read_gate(layer, c):
                n = CHUNKS * layer + c
                if n >= 2:
                    act.wait_ge(h_gated, n - 1)
                read_out((f"gate{layer}", c), lambda t: sgate[n % 2][:, t, :], ACT.Sigmoid, f"H{2 * layer}")

            def square_gate(layer, c):
                act.wait_ge(h_gated, CHUNKS * layer + c + 1)
                square_chunk(h, f"H{2 * layer + 1}", c)

            def odd(i, s):
                at = SLOTS * i + s
                if at == 1:
                    read_gate(0, 3)
                if at == 3:
                    square_gate(0, 3)
                if at == 4:
                    split_T("gate03")
                if at == AT_P1 + 2:
                    split_T("p1")
                if s == 2 and i:
                    read_odd(i - 1)
                if at == AT_GLR + 2:
                    wait_use(act, t_full, T_NO, "glr")
                    nc.scalar.activation(glrT[:], T[0][0:GLR, 0:SEQ], ACT.Copy).then_inc(t_read, 1)
                for n in range(GROUPS_LA):
                    b = group_start(n)
                    if at == b + G_F + 3 and n < 2:
                        wait_use(act, t_full, T_NO, f"f{n}")
                        for j in range(2):
                            last = nc.scalar.activation(lv[:, 0, j * COLS:(j + 1) * COLS], T[j][:], ACT.Sigmoid)
                        last.then_inc(t_read, 1)
                    if at == b + G_F + 4 and n < 2:
                        act.wait_ge(f_made, n + 1)
                        nc.scalar.activation(lv[:, 0, :], lv[:, 1, :], ACT.Ln).then_inc(ln_made, 1)
                    if at == b + G_F + 3 and n == 2:
                        wait_use(act, t_full, T_NO, "f2")
                        wait_use(act, m1_full, M1_NO, "A17")
                        for j in range(2):
                            last = nc.scalar.activation(flat(gk)[:, j * COLS:(j + 1) * COLS], T[j][:], ACT.Copy)
                        last.then_inc(t_read, 1)
                    for half in range(2):
                        if at == b + G_F + half + 3 and n == 2:
                            wait_use(act, m1_full, M1_NO, f"up{half}")
                            for j in range(2):
                                hd = 2 * half + j
                                last = nc.scalar.activation(lv[:, 0, hd * SEQ:(hd + 1) * SEQ], M1[:, j * SEQ:(j + 1) * SEQ],
                                                            ACT.Abs, bias=cols[:, C_BG + hd:C_BG + hd + 1])
                            last.then_inc(abs_made, 1)
                    if at == b + G_F + 4 and n == 2:
                        act.wait_ge(abs_made, 2)
                        link(nc.scalar.activation(lv[:, 0, :], lv[:, 0, :], ACT.Exp, scale=-1.0))
                        nc.scalar.activation(lv[:, 0, :], lv[:, 0, :], ACT.Ln, bias=1.0).then_inc(ln_made, 1)
                    if at == b + G_Q + 2:
                        wait_use(act, t_full, T_NO, f"g{n}")
                        if n:
                            wait_use(act, m1_full, M1_NO, f"A{n - 1}7")
                        for j in range(2):
                            last = nc.scalar.activation(flat(gq)[:, j * COLS:(j + 1) * COLS], T[j][:], ACT.Copy,
                                                        scale=SCALE_LA)
                        last.then_inc(t_read, 1)
                    for j in range(len(LEVELS)):
                        if at == b + G_LEVEL[n] + 2 * j - 3:
                            act.wait_ge(lv_sub, n * len(LEVELS) + j + 1)
                            X = level_buf[j % 4]
                            if j == 0:
                                for hd in range(4):
                                    nc.scalar.activation(X[:, hd * SEQ:hd * SEQ + P], gg[:, hd, 0:P], ACT.Exp,
                                                         bias=gg[:, hd, P - 1:P], scale=-1.0)
                                nc.scalar.activation(level_views(X, P)[:, :, 1, :], gg[:, :, P:SEQ], ACT.Exp).then_inc(lv_exp, 1)
                            else:
                                nc.scalar.activation(X, X, ACT.Exp).then_inc(lv_exp, 1)
                    if at == b + G_LEVEL[n] + 2:
                        wait_use(act, m0_full, M0_NO, f"A{n}0")
                        nc.scalar.activation(flat(ATx[:, 4 * n:4 * n + 4, :]), M0[:], ACT.Copy).then_inc(m0_read, 1)
                for j in range(6):
                    if at == av_place(j) + 2:
                        square_o(j)
                for c in range(2):
                    if at == AT_YO + SLOTS * c + 2:
                        split_T(f"yo{c}")

            def square_o(j):
                bank, full, _, number = av_bank(j)
                n_heads, dv, first = av_heads(j)
                wait_use(act, full, number, f"AV{j}")
                act.wait_ge(squares, sq_n[0])
                for k in range(n_heads):
                    if o_sq_n[0]:
                        act.wait_ge(o_squares, o_sq_n[0])
                    o_sq_n[0] += 1
                    nc.scalar.activation(junk[:, 0:dv], bank[:, k * dv:(k + 1) * dv], ACT.Square,
                                         accum_out=oms[:, j % 2, first + k:first + k + 1]).then_inc(o_squares, 1)

            def read_odd(c):
                cc = ("in1", c)
                if c in O_GATES:
                    col, skip = O_GATES[c], GLR if c == O_GLR else 0
                    n = ODD_IN[c][1] - skip
                    wait_chunk(act, cc)
                    wait_rstd(act, "H1")
                    if c == O_GLR:
                        for t in range(TILES):
                            nc.scalar.activation(glr[:, t, :], acc[NUMBER[cc] % 2][t][:, 0:GLR], ACT.Copy,
                                                 scale=rstd[:, STAT_NO["H1"], t:t + 1])
                    for t in range(TILES):
                        last = nc.scalar.activation(O[:, t, col:col + n], acc[NUMBER[cc] % 2][t][:, skip:skip + n], ACT.Silu,
                                                    scale=rstd[:, STAT_NO["H1"], t:t + 1])
                    last.then_inc(acc_read[NUMBER[cc] % 2], 1)
                    return
                if c in (O_Q[0], O_F[0]):
                    wait_use(act, t_full, T_NO, "p1")
                elif c in O_Q or c in O_F:
                    wait_use(act, t_full, T_NO, f"g{O_Q.index(c) - 1}" if c in O_Q else f"f{O_F.index(c) - 1}")
                elif c < O_V + 2:
                    wait_use(act, t_full, T_NO, ("g2", "f2")[c - O_V])
                else:
                    wait_use(act, m0_full, M0_NO, f"AV{2 * (c - O_V) - 3}")
                dst = zq if c in O_Q or c in (O_V, O_V + 2) else zf
                read_out(cc, lambda t: dst[:, t, :], ACT.Copy, "H1")

            def embed_and_out(layer, last_of_in):
                for i in range(CHUNKS):
                    split_w((f"e{layer}", i), 0)
                    if i == 1:
                        last_of_in()
                for c in range(CHUNKS):
                    for s in range(SLOTS):
                        split_w((f"out{layer}", c), s)
                        if c:
                            if s == 2:
                                read_outproj(layer, c - 1)
                            if s == 4:
                                split_T(f"out{layer}{c - 1}")
                        elif layer:
                            if s == 0:
                                split_T("yo2")
                            if s in (1, 2):
                                square_o(5 + s)
                            if s == 5:
                                split_T("yo3")
                            if s in (3, 4, 6, 7):
                                read_embed(layer, (3, 4, 6, 7).index(s))
                        else:
                            if s == 2:
                                split_T("yb1")
                            if s >= 4:
                                read_embed(layer, s - 4)

            def gate_phase(layer):
                for c in range(CHUNKS):
                    for s in range(SLOTS):
                        split_w((f"gate{layer}", c), s)
                        if s == 1 and c == 0:
                            read_outproj(layer, 3)
                        if s == 4 and c == 0:
                            split_T(f"out{layer}3")
                        if s == 1 + layer and c:
                            read_gate(layer, c - 1)
                        if s == 3 + layer and c:
                            square_gate(layer, c - 1)
                        if s == 4 and c and layer == 0:
                            split_T(f"gate0{c - 1}")

            for i in range(len(EVEN_IN)):
                for s in range(SLOTS):
                    if i == 0 and s % SLOTS_PER_X == 0:
                        split_T(f"x{s // SLOTS_PER_X}")
                    split_w(("in0", i), s)
                    even(i, s)

            def last_gate_b():
                act.wait_ge(y_gated, 3)
                read_out(("in0", E_GB + 1), lambda t: sg0[:, t, :], ACT.Silu, "X")

            embed_and_out(0, last_gate_b)
            gate_phase(0)
            for i in range(len(ODD_IN)):
                for s in range(SLOTS):
                    split_w(("in1", i), s)
                    odd(i, s)
            embed_and_out(1, lambda: read_odd(len(ODD_IN) - 1))
            gate_phase(1)
            g, cs = sgate[(2 * CHUNKS - 1) % 2], slice((CHUNKS - 1) * COLS, D_MODEL)
            act.wait_ge(h_gated, 2 * CHUNKS - 2)
            for t in range(TILES):
                act.wait_ge(tile_full, t + 1)
                nc.scalar.activation(g[:, t, :], acc[NUMBER[PLAN[-1]] % 2][t][:], ACT.Sigmoid,
                                     scale=rstd[:, STAT_NO["H2"], t:t + 1]).then_inc(tile_gates, 1)
                act.wait_ge(tile_gated, t + 1)
                square(h[:, t, cs], ms[:, STAT_NO["H3"], t, CHUNKS - 1:CHUNKS])
                act.wait_ge(rstd_made, STAT_NO["H3"] + t + 1)
                act.wait_ge(h_gained, TILES * (CHUNKS - 1) + t + 1)
                for c in range(0, CHUNKS, 2):
                    o = e[:, t, c * COLS:(c + 1) * COLS]
                    nc.scalar.activation(o, o, ACT.Copy, scale=rstd[:, STAT_NO["H3"], t:t + 1]).then_inc(normed[0], 1)

        @block.vector
        def _(dve):
            steps = [0]

            def link(ins):
                steps[0] += 1
                ins.then_inc(dve_step, 1)
                dve.wait_ge(dve_step, steps[0])

            def split_w(c, s):
                n = FIRST_SLOT[c] + s
                dve.wait_ge(hi_made, n + 1)
                if n >= RING:
                    dve.wait_ge(slot_used, n - RING + 1)
                nc.vector.tensor_tensor(slot_view(wlo, c, s), slot_view(raw, c, s), slot_view(whi, c, s).bitcast(F32),
                                        ALU.subtract).then_inc(lo_made, 1)

            def split_T(name):
                buf, k0, gain = SPLITS[name]
                dve.wait_ge(t_hi, SPLIT_NO[name] + 1)
                B = banks.get(name, T)
                hi, lo = (phi, plo) if buf == "p" else (bhi[buf], blo[buf])
                if gain is None:
                    for i in range(1 if buf == "p" else 2):
                        ks = slice(k0 + 2 * i, k0 + 2 * i + 2)
                        last = nc.vector.tensor_tensor(flat(lo[:, ks, :]), T[i][:], flat(hi[:, ks, :]).bitcast(F32),
                                                       ALU.subtract)
                else:
                    for k in range(4):
                        last = nc.vector.scalar_tensor_tensor(
                            out=lo[:, k0 + k, :], in0=B[k // 2][:, (k % 2) * SEQ:(k % 2 + 1) * SEQ],
                            scalar=cols[:, gain + k:gain + k + 1], in1=hi[:, k0 + k, :].bitcast(F32),
                            op0=ALU.mult, op1=ALU.subtract)
                last.then_inc(t_read if B is T else x_split, 1)

            def row_mean(name):
                i = STAT_NO[name]
                dve.wait_ge(squares, sum(n for _, n, _ in STATS[:i + 1]))
                nc.vector.tensor_reduce(mean[:, i, :], ms[:, i], AX.X, ALU.add).then_inc(mean_made, 1)

            def shift_scores(u):
                b, heads = UNITS[u]
                n, nk = len(heads), P * (b + 1)
                hs = slice(heads[0], heads[-1] + 1)
                wait_use(dve, m0_full, M0_NO, f"S{u}")
                if u >= 2:
                    wait_use(dve, t_full, T_NO, f"P{u - 2}")
                mask = band[:] if b else band[:, 1:2, :]
                mask = flat(mask).unsqueeze(1).to_broadcast([P, n, nk])
                S = Pm[:, u % 2, :].rearrange("p (n k) -> p n k", k=nk)
                nc.vector.tensor_tensor(S, M0[:].rearrange("p (n k) -> p n k", k=nk), mask, ALU.add).then_inc(m0_read, 1)
                wait_use(dve, m0_read, M0_NO, f"S{u}")
                link(nc.vector.tensor_reduce(nmax[:, b, hs], S, AX.X, ALU.max, negate=True))
                link(nc.vector.tensor_tensor(nmax[:, b, hs], nmax[:, b, hs], nsink[:, hs], ALU.min))
                nc.vector.tensor_tensor(dsink[:, b, hs], nmax[:, b, hs], nsink[:, hs], ALU.subtract).then_inc(scores_shifted, 1)

            def attention_out(u):
                b, heads = UNITS[u]
                n = len(heads)
                hs = slice(heads[0], heads[-1] + 1)
                dve.wait_ge(probs_made, u + 1)
                link(nc.vector.tensor_tensor(rinv[:, b, hs], psumr[:, b, hs], esink[:, b, hs], ALU.add))
                link(nc.vector.reciprocal(rinv[:, b, hs], rinv[:, b, hs]))
                wait_use(dve, m1_full, M1_NO, f"O{u}")
                o = qo[:, b, heads[0] * HD_A:(heads[-1] + 1) * HD_A].rearrange("p (n d) -> p n d", d=HD_A)
                nc.vector.tensor_tensor(o, M1[:, 0:n * HD_A].rearrange("p (n d) -> p n d", d=HD_A),
                                        rinv[:, b, hs].unsqueeze(2).to_broadcast([P, n, HD_A]), ALU.mult).then_inc(m1_read, 1)

            def gate_b(c):
                wait_read(dve, ("in0", E_GB + c))
                wait_use(dve, m1_read, M1_NO, "mix3")
                ub = u_b[:, :, c * COLS:(c + 1) * COLS]
                nc.vector.tensor_tensor(ub, ub, sg0, ALU.mult).then_inc(y_gated, 1)

            def even(i, s):
                at = SLOTS * i + s
                if at == AT_COLS + 1:
                    row_mean("X")
                if at == AT_COLS + 2:
                    wait_use(dve, t_full, T_NO, "cols")
                    nc.vector.tensor_copy(cols[:, C_GATE:N_ROWS], T[0][:, C_GATE:N_ROWS]).then_inc(t_read, 1)
                    wait_use(dve, t_read, T_NO, "cols")
                    link(nc.vector.tensor_tensor(lb_max, cols[:, C_LB:C_LB + 8], cols[:, C_LB + 8:C_LB + 16], ALU.max))
                    nc.vector.tensor_tensor(lb_a, cols[:, C_LB:C_LB + 8], lb_max, ALU.subtract)
                    nc.vector.tensor_tensor(lb_b, cols[:, C_LB + 8:C_LB + 16], lb_max, ALU.subtract).then_inc(lb_shifted, 1)
                if at == AT_P0 + 2:
                    split_T("p0")
                if at == AT_SPATIAL + 2:
                    wait_use(dve, t_full, T_NO, "wsp")
                    for j in range(2):
                        last = nc.vector.tensor_copy(flat(wT[:, 4 * j:4 * j + 4, :]), T[j][:])
                    last.then_inc(t_read, 1)
                    dve.wait_ge(lb_exps, 1)
                    link(nc.vector.tensor_tensor(lb_sum, lb_a, lb_b, ALU.add))
                    link(nc.vector.reciprocal(lb_sum, lb_sum))
                    link(nc.vector.tensor_tensor(lb, lb_b, lb_sum, ALU.mult))
                    link(nc.vector.tensor_scalar(omlb, lb, -1.0, 1.0, ALU.mult, ALU.add))
                    dve.wait_ge(sink_in, 16)
                    link(nc.vector.tensor_scalar(nsink[:], nsink[:], -1.0, None, ALU.mult))
                    dve.wait_ge(masks_made, 1)
                if at == AT_K - 1:
                    wait_read(dve, ("in0", E_KV))
                    dve.wait_ge(kpad_zero, 1)
                    for g in range(KV_A):
                        for z in range(2):
                            last = nc.vector.tensor_copy(kpad[:, :, g, z, z * HD_A:(z + 1) * HD_A],
                                                         kv[:, :, g * HD_A:(g + 1) * HD_A])
                    last.then_inc(kpad_made, 1)
                for u in range(len(UNITS)):
                    if at == AT_SCORES + 2 * u + 2:
                        shift_scores(u)
                    if at == AT_VALUES + 2 * u + 2:
                        attention_out(u)
                for c in range(2):
                    if at == AT_YA - 1 + c:
                        dve.wait_ge(ga_made, c + 1)
                        wait_use(dve, m1_read, M1_NO, f"O{len(UNITS) - 1}")
                        q = qo[:, :, c * COLS:(c + 1) * COLS]
                        nc.vector.tensor_tensor(q, q, ga[:, :, c * COLS:(c + 1) * COLS], ALU.mult).then_inc(y_gated, 1)
                    if at == AT_YA + 3 * c + 2:
                        split_T(f"ya{c}")
                if at == AT_MIX - 3:
                    row_mean("V")
                if at == AT_MIX - 1:
                    wait_rstd(dve, "V")
                    dve.wait_ge(vgain_in, 16)
                    for t in range(TILES):
                        nc.vector.scalar_tensor_tensor(out=v_b[:, t, :], in0=v_b[:, t, :], scalar=rstd[:, STAT_NO["V"], t:t + 1],
                                                       in1=vgain, op0=ALU.mult, op1=ALU.mult).then_inc(v_normed, 1)
                for m in range(4):
                    if at == AT_MIX + m + 2:
                        wait_use(dve, m1_full, M1_NO, f"mix{m}")
                        t, half = m // 2, m % 2
                        for g in range(4 * half, 4 * half + 4):
                            ub = u_b[:, t, g * P:(g + 1) * P]
                            last = nc.vector.scalar_tensor_tensor(
                                out=ub, in0=M1[:, (g % 4) * P:(g % 4 + 1) * P], scalar=cols[:, C_BSP + g:C_BSP + g + 1],
                                in1=ub, op0=ALU.add, op1=ALU.mult)
                        last.then_inc(m1_read, 1)
                if at == AT_YB - 1:
                    gate_b(0)
                if at == AT_YB + 2:
                    split_T("yb0")

            def read_embed(layer, i):
                c = (f"e{layer}", i)
                wait_chunk(dve, c)
                for t in range(TILES):
                    last = nc.vector.tensor_copy(e[:, t, i * COLS:(i + 1) * COLS], acc[NUMBER[c] % 2][t][:])
                last.then_inc(acc_read[NUMBER[c] % 2], 1)

            def read_outproj(layer, i):
                c = (f"out{layer}", i)
                wait_chunk(dve, c)
                for t in range(TILES):
                    ht = h[:, t, i * COLS:(i + 1) * COLS]
                    last = nc.vector.tensor_tensor(ht, acc[NUMBER[c] % 2][t][:], ht, ALU.add)
                last.then_inc(acc_read[NUMBER[c] % 2], 1)

            def scale_embed(layer, i):
                if i == 0:
                    row_mean(f"E{layer}")
                    wait_rstd(dve, f"E{layer}")
                    dve.wait_ge(gain_in, 16 * (layer + 1))
                for t in range(TILES):
                    et = e[:, t, i * COLS:(i + 1) * COLS]
                    last = nc.vector.scalar_tensor_tensor(out=et, in0=et, scalar=rstd[:, STAT_NO[f"E{layer}"], t:t + 1],
                                                          in1=gbc[:, i * COLS:(i + 1) * COLS], op0=ALU.mult, op1=ALU.mult)
                last.then_inc(e_scaled, 1)

            def apply_gate(layer, i):
                c = (f"gate{layer}", i)
                n = CHUNKS * layer + i
                wait_read(dve, c)
                dve.wait_ge(e_scaled, n + 1)
                g, cs = sgate[n % 2], slice(i * COLS, (i + 1) * COLS)
                link(nc.vector.tensor_tensor(g, g, e[:, :, cs], ALU.mult))
                nc.vector.tensor_tensor(h[:, :, cs], h[:, :, cs], g, ALU.add).then_inc(h_gated, 1)
                if layer:
                    gain_h(i)

            def gain_h(i):
                if i == 0:
                    dve.wait_ge(gain_in, 48)
                dve.wait_ge(h_gated, CHUNKS + i + 1)
                for t in range(TILES):
                    cs = slice(i * COLS, (i + 1) * COLS)
                    nc.vector.tensor_tensor(e[:, t, cs], h[:, t, cs], gbc[:, cs], ALU.mult).then_inc(h_gained, 1)

            def select(n, i):
                m = LEVELS[i]
                bank, full, read, number = score_bank(i)
                wait_use(dve, full, number, f"A{n}{i}")
                for a in ("d0", "d1") if i == 1 else (i - 1,):
                    _, _, before, number = score_bank(a)
                    wait_use(dve, before, number, f"A{n}{a}")
                nb = P // (2 * m)
                dst = ATd[:, 8 * n:8 * n + 8, :].rearrange("p j (b z m) -> p j b z m", z=2, m=m)[:, :, :, 1, :]
                mask = lmask[:, i - 1, :].bitcast(I32).rearrange("p (b m) -> p b m", m=m).unsqueeze(1).to_broadcast([P, 8, nb, m])
                nc.vector.copy_predicated(dst, mask, bank[:].rearrange("p (j b m) -> p j b m", j=8, m=m)).then_inc(read, 1)

            def select_diagonal(n, half):
                bank, full, read, number = score_bank(f"d{half}")
                wait_use(dve, full, number, f"A{n}d{half}")
                dve.wait_ge(scores_zero, 1)
                mask = ident[:].bitcast(I32).unsqueeze(1).to_broadcast([P, 4, P])
                nc.vector.copy_predicated(ATd[:, 8 * n + 4 * half:8 * n + 4 * half + 4, :], mask,
                                          bank[:].rearrange("p (j b) -> p j b", j=4)).then_inc(read, 1)

            def sum_decays(n):
                for j in range(8):
                    last = nc.vector.tensor_tensor_scan(flat(gg)[:, j * P:(j + 1) * P], ones[:], lv[:, 0, j * P:(j + 1) * P],
                                                        0.0, ALU.mult, ALU.add)
                last.then_inc(lv_sub, 1)
                dve.wait_ge(lv_sub, n * len(LEVELS) + 1)

            def exponents(n, i):
                m = LEVELS[i]
                g, X = level_views(flat(gg), m), level_views(level_buf[i % 4], m)
                ref = g[:, :, 0, m - 1:m].to_broadcast([P, g.shape[1], m])
                nc.vector.tensor_tensor(X[:, :, 0, :], ref, g[:, :, 0, :], ALU.subtract)
                nc.vector.tensor_tensor(X[:, :, 1, :], g[:, :, 1, :], ref, ALU.subtract).then_inc(lv_sub, 1)

            def gate_o(i):
                t, col = i % 2, (i // 2) * COLS
                bank, full, read, number = av_bank(i)
                n_heads, dv, first = av_heads(i)
                wait_use(dve, full, number, f"AV{i}")
                dve.wait_ge(o_rstd, i + 1)
                for j in range(n_heads):
                    o = O[:, t, col + j * dv:col + (j + 1) * dv]
                    last = nc.vector.scalar_tensor_tensor(out=o, in0=bank[:, j * dv:(j + 1) * dv],
                                                          scalar=orstd[:, t, first + j:first + j + 1], in1=o,
                                                          op0=ALU.mult, op1=ALU.mult)
                last.then_inc(read, 1)

            def odd(i, s):
                at = SLOTS * i + s
                if at == 2:
                    apply_gate(0, 3)
                if at == 4:
                    split_T("gate03")
                    row_mean("H1")
                if at == AT_P1 + 2:
                    split_T("p1")
                for n in range(GROUPS_LA):
                    b = group_start(n)
                    if at == b + G_F + 3 and n < 2:
                        wait_use(dve, t_read, T_NO, f"f{n}")
                        f = lv[:, 1, :]
                        for hd in range(4):
                            hc = 4 * n + hd
                            last = nc.vector.tensor_scalar(f[:, hd * SEQ:(hd + 1) * SEQ], lv[:, 0, hd * SEQ:(hd + 1) * SEQ],
                                                           omlb[:, hc:hc + 1], lb[:, hc:hc + 1], ALU.mult, ALU.add)
                        link(last)
                        link(nc.vector.tensor_scalar(flat(gk), f, -1.0, 1.0, ALU.mult, ALU.add))
                        nc.vector.tensor_scalar(f, f, LN_LEAST, None, ALU.max).then_inc(f_made, 1)
                    for half in range(2):
                        if at == b + G_F + half + 3 and n == 2:
                            f = lv[:, 1, :]
                            dve.wait_ge(abs_made, half + 1)
                            for j in range(2):
                                hd = 2 * half + j
                                last = nc.vector.tensor_scalar(f[:, hd * SEQ:(hd + 1) * SEQ], M1[:, j * SEQ:(j + 1) * SEQ],
                                                               cols[:, C_BG + hd:C_BG + hd + 1], 0.0, ALU.add, ALU.min)
                            last.then_inc(m1_read, 1)
                    if at == b + G_F + 5 and n == 2:
                        f = lv[:, 1, :]
                        wait_use(dve, m1_read, M1_NO, "up1")
                        dve.wait_ge(ln_made, 3)
                        link(nc.vector.tensor_tensor(lv[:, 0, :], f, lv[:, 0, :], ALU.subtract))
                        link(nc.vector.tensor_scalar(lv[:, 0, :], lv[:, 0, :], 1.0 / 16.0, None, ALU.mult))
                    if at == b + G_SUMS[n]:
                        dve.wait_ge(ln_made, n + 1)
                        sum_decays(n)
                    for half in range(2):
                        if at == b + G_DIAG + half + 2:
                            select_diagonal(n, half)
                    for j in range(1, len(LEVELS)):
                        if at == b + G_LEVEL[n] + 2 * j - 3:
                            exponents(n, j)
                        if at == b + G_LEVEL[n] + 2 * j + 2:
                            select(n, j)
                for j in range(5):
                    if at == av_place(j) + 3:
                        gate_o(j)
                for c in range(2):
                    if at == AT_YO + SLOTS * c + 2:
                        split_T(f"yo{c}")

            def embed_and_out(layer, last_of_in):
                for i in range(CHUNKS):
                    split_w((f"e{layer}", i), 0)
                    if i == 1:
                        last_of_in()
                read_embed(layer, 0)
                read_embed(layer, 1)
                for c in range(CHUNKS):
                    for s in range(SLOTS):
                        split_w((f"out{layer}", c), s)
                        if c:
                            if s == 2:
                                read_outproj(layer, c - 1)
                            if s == 4:
                                split_T(f"out{layer}{c - 1}")
                            if s == 6:
                                scale_embed(layer, c - 1)
                        else:
                            if s == 0:
                                read_embed(layer, 2)
                                read_embed(layer, 3)
                            if layer and s == 0:
                                split_T("yo2")
                            if layer and s in (1, 2):
                                gate_o(5 + s)
                            if s == (5 if layer else 2):
                                split_T("yo3" if layer else "yb1")
                scale_embed(layer, 3)

            def gate_phase(layer):
                for c in range(CHUNKS):
                    for s in range(SLOTS):
                        split_w((f"gate{layer}", c), s)
                        if s == 1 and c == 0:
                            read_outproj(layer, 3)
                        if s == 4 and c == 0:
                            split_T(f"out{layer}3")
                            row_mean(f"H{2 * layer}")
                        if s == 2 + layer and c:
                            apply_gate(layer, c - 1)
                        if s == 4 and c and layer == 0:
                            split_T(f"gate0{c - 1}")

            nc.vector.memset(small[:], 0.0).then_inc(small_zero, 1)
            dve.wait_ge(small_zero, 1)
            link(nc.vector.memset(mhalf, -0.5))
            dve.wait_ge(cols_full, 1)
            nc.vector.tensor_copy(cols[:, 0:C_GATE], M1[:, 0:C_GATE]).then_inc(cols_made, 1)
            dve.wait_ge(cols_made, 1)
            for i in range(len(EVEN_IN)):
                for s in range(SLOTS):
                    if i == 0 and s % SLOTS_PER_X == 0:
                        split_T(f"x{s // SLOTS_PER_X}")
                    split_w(("in0", i), s)
                    even(i, s)
            embed_and_out(0, lambda: gate_b(1))
            gate_phase(0)
            for i in range(len(ODD_IN)):
                for s in range(SLOTS):
                    split_w(("in1", i), s)
                    odd(i, s)
            embed_and_out(1, lambda: gate_o(5))
            gate_phase(1)
            g, cs = sgate[(2 * CHUNKS - 1) % 2], slice((CHUNKS - 1) * COLS, D_MODEL)
            i = STAT_NO["H3"]
            for t in range(TILES):
                dve.wait_ge(tile_gates, t + 1)
                link(nc.vector.tensor_tensor(g[:, t, :], g[:, t, :], e[:, t, cs], ALU.mult))
                nc.vector.tensor_tensor(h[:, t, cs], h[:, t, cs], g[:, t, :], ALU.add).then_inc(tile_gated, 1)
                dve.wait_ge(tile_gated, t + 1)
                nc.vector.tensor_tensor(e[:, t, cs], h[:, t, cs], gbc[:, cs], ALU.mult).then_inc(h_gained, 1)
                dve.wait_ge(squares, sum(n for _, n, _ in STATS) - TILES + t + 1)
                nc.vector.tensor_reduce(mean[:, i, t:t + 1], ms[:, i, t, :], AX.X, ALU.add).then_inc(mean_made, 1)
                dve.wait_ge(rstd_made, i + t + 1)
                dve.wait_ge(h_gained, TILES * (CHUNKS - 1) + t + 1)
                for c in range(1, CHUNKS, 2):
                    o = e[:, t, c * COLS:(c + 1) * COLS]
                    nc.vector.tensor_scalar(o, o, rstd[:, i, t:t + 1], None, ALU.mult).then_inc(normed[1], 1)

        @block.gpsimd
        def _(pool):
            steps = [0]

            def link(ins):
                steps[0] += 1
                ins.then_inc(pool_step, 1)
                pool.wait_ge(pool_step, steps[0])

            def keep(a, pattern, base, per_partition, fill, op=ALU.is_ge):
                return nc.gpsimd.affine_select(out=a, in_=a, pattern=pattern, compare_op=op, fill=fill, base=base,
                                               channel_multiplier=per_partition)

            def root(name):
                i = STAT_NO[name]
                pool.wait_ge(mean_made, i + 1)
                link(nc.gpsimd.tensor_scalar(var[:, i, :], mean[:, i, :], 1.0 / STATS[i][2], EPS, ALU.mult, ALU.add))
                nc.gpsimd.tensor_tensor(rstd[:, i, :], var[:, i, :], mhalf[:, 0:TILES], ALU.pow).then_inc(rstd_made, 1)

            link(nc.gpsimd.memset(ident[:], 0.0))
            keep(ident[:], [[-1, P]], 0, 1, 1.0, ALU.not_equal).then_inc(ident_made, 1)
            nc.gpsimd.memset(kpad, 0.0).then_inc(kpad_zero, 1)
            link(nc.gpsimd.memset(band[:], 0.0))
            link(keep(band[:, 0, :], [[1, P]], -1, -1, NEG_INF))
            link(keep(band[:, 1, :], [[-1, P]], 0, 1, NEG_INF))
            link(nc.gpsimd.memset(lmask[:], 1.0))
            for i, m in enumerate(LEVELS[1:]):
                v, nb = lmask[:, i, :], P // (2 * m)
                link(keep(v, [[-2 * m, nb], [0, m]], 0, 1, 0.0))
                link(keep(v, [[2 * m, nb], [0, m]], m - 1, -1, 0.0))
            nc.gpsimd.memset(ones[:], 1.0).then_inc(masks_made, 1)
            root("X")
            wait_use(pool, t_read, T_NO, "wsp")
            nc.gpsimd.affine_select(out=wT, in_=wT, pattern=[[0, GROUPS_B], [1, P]], compare_op=ALU.is_ge, fill=0.0, base=0,
                                    channel_multiplier=-1).then_inc(spatial_masked, 1)
            for name in ("V", "E0", "H0"):
                root(name)
            wait_use(pool, t_full, T_NO, "yb1")
            nc.gpsimd.memset(ATd, 0.0).then_inc(scores_zero, 1)
            root("H1")
            with pool.Fori(0, GROUPS_LA) as n:
                for i, m in enumerate(LEVELS):
                    pool.wait_ge(lv_exp, n * len(LEVELS) + (i + 1))
                    X, k, q = (level_views(a, m) for a in (level_buf[i % 4], flat(gk), flat(gq)))
                    nc.gpsimd.tensor_tensor(X[:, :, 0, :], X[:, :, 0, :], k[:, :, 0, :], ALU.mult)
                    nc.gpsimd.tensor_tensor(X[:, :, 1, :], X[:, :, 1, :], q[:, :, 1, :], ALU.mult).then_inc(lv_mul, 1)
            for i in range(8):
                n_heads, dv, first = av_heads(i)
                pool.wait_ge(o_squares, sum(av_heads(j)[0] for j in range(i + 1)))
                hs = slice(first, first + n_heads)
                link(nc.gpsimd.tensor_scalar(ovar[:, i % 2, hs], oms[:, i % 2, hs], 1.0 / dv, EPS, ALU.mult, ALU.add))
                nc.gpsimd.tensor_tensor(orstd[:, i % 2, hs], ovar[:, i % 2, hs], mhalf[:, 0:n_heads], ALU.pow).then_inc(o_rstd, 1)
            for name in ("E1", "H2"):
                root(name)
            i = STAT_NO["H3"]
            for t in range(TILES):
                pool.wait_ge(mean_made, i + t + 1)
                link(nc.gpsimd.tensor_scalar(var[:, i, t:t + 1], mean[:, i, t:t + 1], 1.0 / D_MODEL, EPS, ALU.mult, ALU.add))
                nc.gpsimd.tensor_tensor(rstd[:, i, t:t + 1], var[:, i, t:t + 1], mhalf[:, 0:1], ALU.pow).then_inc(rstd_made, 1)


_INS = ["x", "p", "norm_mix", "w_in_even", "sinks_a", "vnorm_b", "w_spatial_b", "b_spatial_b", "w_out_even",
        "w_in_odd", "lower_bounds_c", "onorm_c", "w_gate_up_d", "b_gate_d", "onorm_d", "w_out_odd",
        "w_ple_proj", "ple_norm", "ple_gate_norm", "w_ple_gate", "final_norm"]


def kernel(**inputs):
    import numpy as np
    import concourse.bacc as bacc
    from concourse.bass_utils import run_bass_kernel_spmd

    nc = bacc.Bacc("TRN2", target_bir_lowering=False, num_devices=1, dynamic_dma_scratch_size=1024)
    arrays, args = {}, []
    for name in _INS:
        a = np.ascontiguousarray(inputs[name])
        arrays[f"in_{name}"] = a
        args.append(nc.dram_tensor(f"in_{name}", a.shape, mybir.dt.from_np(a.dtype), kind="ExternalInput").ap())
    out = nc.dram_tensor("out", (1, SEQ, D_MODEL), F32, kind="ExternalOutput").ap()
    trunk(nc, *args, out)
    return run_bass_kernel_spmd(nc, [arrays], core_ids=[0]).results[0]["out"]
```
